# Optimizing a Trainium2 kernel written in Bass

```python
import math
import jax, jax.numpy as jnp
from jax import lax
import numpy as np

D_MODEL = 1024
BATCH = 1
SEQ = 128
DEPTH = 2
DEC_BATCH = 1
DEC_SEQ = 256
PAST_LEN = 128

GRID_W = 64
N_MIXERS = 2
N_A_LAYERS = (DEPTH + 1) // 2
N_B_LAYERS = DEPTH // 2
A_HEAD_DIM = 64
A_HEADS = D_MODEL // A_HEAD_DIM
A_KV_HEADS = 4
B_HEAD_DIM = 64
B_HEADS = D_MODEL // (2 * B_HEAD_DIM)
N_EXPERTS = 16
N_GROUPS = 4
EXPERTS_PER_GROUP = N_EXPERTS // N_GROUPS
TOP_K = 2
D_EXPERT = 512
N_MOD = 6
ROPE_THETA = 10000.0
Q_BLOCK = 128
EPS = 1e-6

kernel_name = 'hybrid_diffusion_gqa_diffattn_grouped_moe_step'

def rms_norm(x, g):
    xf = x.astype(jnp.float32)
    y = xf * lax.rsqrt(jnp.mean(xf * xf, axis=-1, keepdims=True) + EPS)
    return (y * g.astype(jnp.float32)).astype(x.dtype)

def modulation(cvec, w, b):
    m = jax.nn.silu(cvec) @ w + b
    return jnp.split(m[:, None, :], N_MOD, axis=-1)

def modulate(h, shift, scale):
    return h * (1 + scale) + shift

def grid_angles(n, head_dim):
    rows = n // GRID_W
    row = jnp.repeat(jnp.arange(rows, dtype=jnp.float32), GRID_W)
    col = jnp.tile(jnp.arange(GRID_W, dtype=jnp.float32), rows)
    d_axis = head_dim // 2
    inv = ROPE_THETA ** (-jnp.arange(0, d_axis, 2, dtype=jnp.float32) / d_axis)
    return row[:, None] * inv, col[:, None] * inv

def _rotate(x, ang):
    x1, x2 = jnp.split(x, 2, axis=-1)
    c, s = jnp.cos(ang), jnp.sin(ang)
    return jnp.concatenate([x1 * c - x2 * s, x2 * c + x1 * s], axis=-1)

def axial_rope(x, angles):
    ang_row, ang_col = angles
    shape = (ang_row.shape[0],) + (1,) * (x.ndim - 3) + (ang_row.shape[1],)
    xf = x.astype(jnp.float32)
    xr, xc = jnp.split(xf, 2, axis=-1)
    out = jnp.concatenate([_rotate(xr, ang_row.reshape(shape)), _rotate(xc, ang_col.reshape(shape))], axis=-1)
    return out.astype(x.dtype)

def query_blocks(q):
    b, s = q.shape[:2]
    return jnp.moveaxis(q.reshape((b, s // Q_BLOCK, Q_BLOCK) + q.shape[2:]), 1, 0)

def unblock(o):
    o = jnp.moveaxis(o, 0, 1)
    return o.reshape((o.shape[0], o.shape[1] * o.shape[2]) + o.shape[3:])

def gqa_attention(q, k, v):
    b, s, h, d = q.shape
    g = k.shape[2]
    qg = q.reshape(b, s, g, h // g, d)
    scale = d ** -0.5

    def block(qb):
        sc = jnp.einsum('bqgrd,bkgd->bgrqk', qb, k, preferred_element_type=jnp.float32) * scale
        p = jax.nn.softmax(sc, axis=-1).astype(v.dtype)
        return jnp.einsum('bgrqk,bkgd->bqgrd', p, v)

    return unblock(lax.map(block, query_blocks(qg))).reshape(b, s, h * d)

def diff_attention(q, k, v, lam):
    scale = q.shape[-1] ** -0.5

    def block(qb):
        sc = jnp.einsum('bqhmd,bkhmd->bhmqk', qb, k, preferred_element_type=jnp.float32) * scale
        p = jax.nn.softmax(sc, axis=-1)
        a = (p[:, :, 0] - lam * p[:, :, 1]).astype(v.dtype)
        return jnp.einsum('bhqk,bkhe->bqhe', a, v)

    return unblock(lax.map(block, query_blocks(q)))

def a_project(h, w_qkv, g_q, g_k):
    b, n, _ = h.shape
    q, k, v = jnp.split(h @ w_qkv, [A_HEADS * A_HEAD_DIM, (A_HEADS + A_KV_HEADS) * A_HEAD_DIM], axis=-1)
    q = rms_norm(q.reshape(b, n, A_HEADS, A_HEAD_DIM), g_q)
    k = rms_norm(k.reshape(b, n, A_KV_HEADS, A_HEAD_DIM), g_k)
    return q, k, v.reshape(b, n, A_KV_HEADS, A_HEAD_DIM)

def b_project(h, w_qkv):
    b, n, _ = h.shape
    q, k, v = jnp.split(h @ w_qkv, 3, axis=-1)
    return (q.reshape(b, n, B_HEADS, 2, B_HEAD_DIM), k.reshape(b, n, B_HEADS, 2, B_HEAD_DIM),
            v.reshape(b, n, B_HEADS, 2 * B_HEAD_DIM))

def b_finish(o, g_sub, lam_init, w_o):
    b, s = o.shape[:2]
    o = rms_norm(o, g_sub) * (1.0 - lam_init)
    return o.reshape(b, s, D_MODEL) @ w_o

def grouped_moe(h, w_router, b_router, w_gate, w_up, w_down):
    b, n, d = h.shape
    t = h.reshape(b * n, d)
    s = jax.nn.sigmoid((t @ w_router + b_router).astype(jnp.float32))
    sg = s.reshape(-1, N_GROUPS, EXPERTS_PER_GROUP)
    group_score = jnp.sum(lax.top_k(sg, TOP_K)[0], axis=-1)
    best = jnp.argmax(group_score, axis=-1)
    in_group = jnp.arange(N_GROUPS)[None, :] == best[:, None]
    masked = jnp.where(in_group[:, :, None], sg, -jnp.inf).reshape(-1, N_EXPERTS)
    top_v, top_i = lax.top_k(masked, TOP_K)
    gates = top_v / jnp.sum(top_v, axis=-1, keepdims=True)
    combine = jnp.sum(jax.nn.one_hot(top_i, N_EXPERTS, dtype=jnp.float32) * gates[..., None], axis=1)
    out = jnp.zeros(t.shape, jnp.float32)
    for e in range(N_EXPERTS):
        he = jax.nn.silu(t @ w_gate[e]) * (t @ w_up[e])
        out = out + combine[:, e:e + 1] * (he @ w_down[e]).astype(jnp.float32)
    return out.astype(h.dtype).reshape(b, n, d)

def setup_inputs(seed: int = 0) -> dict:
    key = jax.random.key(seed)
    ks = jax.random.split(key, 32)
    f32 = jnp.float32
    nrm = lambda k, shape, s: jax.random.normal(k, shape, f32) * s
    D = D_MODEL
    return {
        'x_prompt': nrm(ks[0], (BATCH, SEQ, D), 1.0),
        'x_sample': nrm(ks[1], (DEC_BATCH, DEC_SEQ, D), 1.0),
        'cache_k_a': nrm(ks[2], (DEC_BATCH, N_A_LAYERS, PAST_LEN, A_KV_HEADS, A_HEAD_DIM), 1.0),
        'cache_v_a': nrm(ks[3], (DEC_BATCH, N_A_LAYERS, PAST_LEN, A_KV_HEADS, A_HEAD_DIM), 1.0),
        'cache_k_b': nrm(ks[4], (DEC_BATCH, N_B_LAYERS, PAST_LEN, B_HEADS, 2, B_HEAD_DIM), 1.0),
        'cache_v_b': nrm(ks[5], (DEC_BATCH, N_B_LAYERS, PAST_LEN, B_HEADS, 2 * B_HEAD_DIM), 1.0),
        'c': nrm(ks[6], (DEC_BATCH, D), 1.0),
        'c_ctx': nrm(ks[7], (D,), 1.0),
        'w_mod': nrm(ks[8], (DEPTH, D, N_MOD * D), 0.5 * D ** -0.5),
        'b_mod': nrm(ks[9], (DEPTH, N_MOD * D), 0.02),
        'g_attn': 1.0 + nrm(ks[10], (DEPTH, D), 0.02),
        'g_ffn': 1.0 + nrm(ks[11], (DEPTH, D), 0.02),
        'w_qkv_a': nrm(ks[12], (N_A_LAYERS, D, (A_HEADS + 2 * A_KV_HEADS) * A_HEAD_DIM), D ** -0.5),
        'w_o_a': nrm(ks[13], (N_A_LAYERS, A_HEADS * A_HEAD_DIM, D), (A_HEADS * A_HEAD_DIM) ** -0.5),
        'g_q_a': 1.0 + nrm(ks[14], (N_A_LAYERS, A_HEAD_DIM), 0.02),
        'g_k_a': 1.0 + nrm(ks[15], (N_A_LAYERS, A_HEAD_DIM), 0.02),
        'w_qkv_b': nrm(ks[16], (N_B_LAYERS, D, 3 * D), D ** -0.5),
        'w_o_b': nrm(ks[17], (N_B_LAYERS, D, D), D ** -0.5),
        'lam_q1': nrm(ks[18], (N_B_LAYERS, B_HEAD_DIM), 0.1),
        'lam_k1': nrm(ks[19], (N_B_LAYERS, B_HEAD_DIM), 0.1),
        'lam_q2': nrm(ks[20], (N_B_LAYERS, B_HEAD_DIM), 0.1),
        'lam_k2': nrm(ks[21], (N_B_LAYERS, B_HEAD_DIM), 0.1),
        'g_sub_b': 1.0 + nrm(ks[22], (N_B_LAYERS, 2 * B_HEAD_DIM), 0.02),
        'w_router': nrm(ks[23], (D, N_EXPERTS), D ** -0.5),
        'b_router': nrm(ks[24], (N_EXPERTS,), 0.01),
        'w_gate': nrm(ks[25], (DEPTH, N_EXPERTS, D, D_EXPERT), D ** -0.5),
        'w_up': nrm(ks[26], (DEPTH, N_EXPERTS, D, D_EXPERT), D ** -0.5),
        'w_down': nrm(ks[27], (DEPTH, N_EXPERTS, D_EXPERT, D), D_EXPERT ** -0.5),
        'g_final': 1.0 + nrm(ks[28], (D,), 0.02),
    }

def reference(x_prompt, x_sample, cache_k_a, cache_v_a, cache_k_b, cache_v_b, c, c_ctx,
              w_mod, b_mod, g_attn, g_ffn, w_qkv_a, w_o_a, g_q_a, g_k_a,
              w_qkv_b, w_o_b, lam_q1, lam_k1, lam_q2, lam_k2, g_sub_b,
              w_router, b_router, w_gate, w_up, w_down, g_final):
    rope_a = grid_angles(x_sample.shape[1], A_HEAD_DIM)
    rope_b = grid_angles(x_sample.shape[1], B_HEAD_DIM)
    xp, xs = x_prompt, x_sample
    new_k_a, new_v_a, new_k_b, new_v_b = [], [], [], []
    for l in range(DEPTH):
        mp = modulation(c_ctx[None, :], w_mod[l], b_mod[l])
        ms = modulation(c, w_mod[l], b_mod[l])
        hp = modulate(rms_norm(xp, g_attn[l]), mp[0], mp[1])
        hs = modulate(rms_norm(xs, g_attn[l]), ms[0], ms[1])
        j = l // N_MIXERS
        if l % N_MIXERS == 0:
            qp, kp, vp = a_project(hp, w_qkv_a[j], g_q_a[j], g_k_a[j])
            out_p = gqa_attention(qp, kp, vp) @ w_o_a[j]
            qs, ks_, vs = a_project(hs, w_qkv_a[j], g_q_a[j], g_k_a[j])
            qs, ks_ = axial_rope(qs, rope_a), axial_rope(ks_, rope_a)
            k_all = jnp.concatenate([ks_, cache_k_a[:, j]], axis=1)
            v_all = jnp.concatenate([vs, cache_v_a[:, j]], axis=1)
            out_s = gqa_attention(qs, k_all, v_all) @ w_o_a[j]
            new_k_a.append(kp)
            new_v_a.append(vp)
        else:
            lam_init = 0.8 - 0.6 * math.exp(-0.3 * l)
            lam = (jnp.exp(jnp.sum((lam_q1[j] * lam_k1[j]).astype(jnp.float32)))
                   - jnp.exp(jnp.sum((lam_q2[j] * lam_k2[j]).astype(jnp.float32))) + lam_init)
            qp, kp, vp = b_project(hp, w_qkv_b[j])
            out_p = b_finish(diff_attention(qp, kp, vp, lam), g_sub_b[j], lam_init, w_o_b[j])
            qs, ks_, vs = b_project(hs, w_qkv_b[j])
            qs, ks_ = axial_rope(qs, rope_b), axial_rope(ks_, rope_b)
            k_all = jnp.concatenate([ks_, cache_k_b[:, j]], axis=1)
            v_all = jnp.concatenate([vs, cache_v_b[:, j]], axis=1)
            out_s = b_finish(diff_attention(qs, k_all, v_all, lam), g_sub_b[j], lam_init, w_o_b[j])
            new_k_b.append(kp)
            new_v_b.append(vp)
        xp = xp + mp[2] * out_p
        xs = xs + ms[2] * out_s
        hp = modulate(rms_norm(xp, g_ffn[l]), mp[3], mp[4])
        hs = modulate(rms_norm(xs, g_ffn[l]), ms[3], ms[4])
        xp = xp + mp[5] * grouped_moe(hp, w_router, b_router, w_gate[l], w_up[l], w_down[l])
        xs = xs + ms[5] * grouped_moe(hs, w_router, b_router, w_gate[l], w_up[l], w_down[l])
    y_prompt = rms_norm(xp, g_final)
    y_sample = rms_norm(xs, g_final)
    state_k_a = jnp.stack(new_k_a, axis=1)
    state_v_a = jnp.stack(new_v_a, axis=1)
    state_k_b = jnp.stack(new_k_b, axis=1)
    state_v_b = jnp.stack(new_v_b, axis=1)
    return (y_prompt, y_sample, state_k_a, state_v_a, state_k_b, state_v_b)


_drawn_inputs = setup_inputs


def setup_inputs(seed=0):
    import zlib

    import numpy as np

    out = dict(_drawn_inputs(seed))
    spreads = {}
    factors = {'g_attn': 2.943,
     'g_q_a': 8.0,
     'g_k_a': 3.014,
     'lam_q2': 2.893,
     'lam_k2': 2.685,
     'g_sub_b': 25.651,
     'g_final': 7.495,
     'cache_k_a': 8.0,
     'cache_v_a': 8.0,
     'cache_k_b': 8.0,
     'cache_v_b': 8.0}
    for name, (base, spread) in spreads.items():
        noise = np.random.default_rng([zlib.crc32(name.encode()), seed]).standard_normal(out[name].shape)
        drawn = base * np.exp(spread * noise) if base else spread * noise
        out[name] = __import__('jax').numpy.asarray(drawn.astype(out[name].dtype))
    for name, factor in factors.items():
        out[name] = (out[name] * factor).astype(out[name].dtype)
    return out
```

```python
from contextlib import ExitStack

import numpy as np

import concourse.bass as bass
from concourse import mybir

F32 = mybir.dt.float32
I32 = mybir.dt.int32
ALU = mybir.AluOpType
ACT = mybir.ActivationFunctionType
X = mybir.AxisListType.X

P = 128
D = 1024
NT = 3
KC = D // P
E = 16
DE = 512
NG = 4
GRID_W = 64
CAP = 64
XT = (2 * NT * P - 1) // CAP
TILES = E + XT
EPS = 1e-6
SKIP = 4096
SLOT = 4096
NSLOT = 6
N_MOD = 6

C_ID, C_UP, C_ONE = 0, 128, 256
C_COS, C_SIN = 384, 512
C_HALF, C_REVE, C_REVG, C_THR = 640, 641, 657, 661
C_N = 666


def shape_constants():
    c = np.zeros((P, C_N), np.float32)
    c[:, C_ID:C_ID + P] = np.eye(P)
    c[:, C_UP:C_UP + P] = np.triu(np.ones((P, P)), 1)
    c[:, C_ONE:C_ONE + P] = 1.0
    inv = np.power(np.float32(10000.0), -np.arange(0, 32, 2, dtype=np.float32) / np.float32(32))
    for t in range(2):
        tok = np.arange(P) + P * t
        row = (tok // GRID_W).astype(np.float32)[:, None] * inv
        col = (tok % GRID_W).astype(np.float32)[:, None] * inv
        c[:, C_COS + 64 * t:C_COS + 64 * (t + 1)] = np.concatenate([np.cos(row)] * 2 + [np.cos(col)] * 2, 1)
        c[:, C_SIN + 64 * t:C_SIN + 64 * (t + 1)] = np.concatenate(
            [-np.sin(row), np.sin(row), -np.sin(col), np.sin(col)], 1)
    c[:, C_HALF] = np.arange(P) // CAP
    c[:, C_REVE:C_REVE + E] = E - np.arange(E)
    c[:, C_REVG:C_REVG + NG] = NG - np.arange(NG)
    c[:, C_THR:C_THR + 5] = CAP * np.arange(1, 6)
    i = np.zeros((P, 12 + 2 * TILES), np.int32)
    for k in range(2):
        for t in range(NT):
            i[:, 2 * (NT * k + t)] = P * t + np.arange(P)
            i[:, 2 * (NT * k + t) + 1] = NT * P * k + P * t + np.arange(P)
    i[:, 12:] = SKIP
    return c, i


def hybrid_step_kernel(nc, t_):
    with ExitStack() as ctx:
        def sb(name, shape, dt=F32):
            return ctx.enter_context(nc.sbuf_tensor(name, shape, dt))

        sems = {}

        def S(name):
            if name not in sems:
                sems[name] = ctx.enter_context(nc.semaphore(name))
            return sems[name]

        FIRST = dict(bias=32, mod_ps=12, mod_sb=12, mod_stored=64, ld_cols=32, ld_gate_attn=32, ld_cache=32, xn_ready=3,
                     xn_turned=6, hT_dve=3, hT_act=3, qkv_done=9, qkv_copied=9, qk_ready=3, qk_turned=10, qkT_dve=5,
                     qkT_act=5, state_out=32, s_done=24, nm_ready=24, p_ready=24, p_turned=24, pT_act=24, pT_dve=24,
                     o_done=24, o_copied=24, o_ready=3, o_turned=6, oT_dve=3, oT_act=3, wo_done=6, wo_copied=6, x_attn=6,
                     sq_attn=3, sq_ffn=3, ld_rows=80, ld_gate_ffn=32, h_ready=3, h_stored=48, hr_turned=6, hr_dve=3,
                     hr_act=3, logits=3, lg_ready=1, sig_ready=1, oh_ready=1, ranks=1, nx_ready=1, rows_ready=1,
                     listed=96, ld_list=32, idx_ready=1, tiles_done=1, scattered=16 * TILES, x_moe=3, xg_main=E,
                     xg_more=XT, y_main=E + 1, ld_y0=32, ld_y1=32, ld_y2=32)
        FIRST |= {f"{x}_main": E for x in ("xc", "x_turned", "xT", "gu", "silu", "h", "h_turned", "hT", "down")}
        FIRST |= {f"gather{r}": 16 * len(range(r, TILES, 4)) for r in range(4)}

        def tile_sem(name, l):
            return S(f"{name}{l}") if name.endswith("_more") and name != "xg_more" else S(name)

        def at(name, l, n):
            if name.endswith("_more") and name != "xg_more":
                return tile_sem(name, l), n
            return S(name), n + (FIRST[name] if l == 1 else 0)

        mod_d = nc.dram_tensor("mod_scratch", [2, 2, N_MOD * D], F32, kind="Internal").ap()
        h_d = nc.dram_tensor("h_scratch", [2, 2 * NT * P, 512], F32, kind="Internal").ap()
        y_ds = [nc.dram_tensor(f"y_scratch{l}", [4 * NT * P, 512], F32, kind="Internal").ap() for l in range(2)]
        h_ds = [nc.dram_tensor(f"h_scratch{l}", [2 * NT * P, 512], F32, kind="Internal").ap() for l in range(2)]
        list_ds = [nc.dram_tensor(f"list_scratch{l}", [CAP * TILES, 2], I32, kind="Internal").ap() for l in range(2)]

        ring = sb("ring", [P, NSLOT, SLOT])
        x = sb("x", [P, NT, D])
        gate_bc = sb("gate_bc", [P, 2, D])
        cf = sb("cf", [P, C_N])
        ci = sb("ci", [P, 12 + 2 * TILES], I32)
        modsb = sb("modsb", [P, 12, P])
        cs = sb("cs", [P, KC, 32])
        cvec = sb("cvec", [P, 2, KC])
        gcol = sb("gcol", [P, 2, KC])
        colp = sb("colp", [P, 2, 2, KC])
        a1 = sb("a1", [P, 2, KC])
        wr = sb("wr", [P, KC, E])
        br = sb("br", [P, E])
        gqk = sb("gqk", [P, 2, 64])
        gsub = sb("gsub", [P, P])
        lamv = sb("lamv", [P, 4, 64])
        small = sb("small", [P, 16])
        ss = sb("ss", [P, 24])
        rs = sb("rs", [P, 24])
        mx = sb("mx", [P, 2, 2])
        nm = sb("nm", [P, 2, 2])
        sm = sb("sm", [P, 2, 2])
        rsm = sb("rsm", [P, 2, 2])
        work = sb("work", [P, 19712])
        rti = sb("rti", [P, 6], I32)
        nxi = sb("nxi", [P, E], I32)
        tick = sb("tick", [1, TILES])
        lst = sb("lst", [P, 2 * TILES], I32)
        gi = sb("gi", [P, 2 * TILES], I32)
        PS = ctx.enter_context(nc.psum_tensor("PS", [P, 8, 512], F32))

        ident = cf[:, C_ID:C_ID + P]
        upper = cf[:, C_UP:C_UP + P]
        ones = cf[:, C_ONE:C_ONE + P]

        W_R1, W_R2, W_R3, W_V, W_KT, W_P, W_PT = 0, 3072, 6144, 9216, 13312, 17408, 18944
        r1 = work[:, W_R1:W_R1 + 3072]
        r2 = work[:, W_R2:W_R2 + 3072]
        r3 = work[:, W_R3:W_R3 + 3072]
        hT = r1.rearrange("p (k n) -> p k n", k=KC)
        qT = r1.rearrange("p (k n) -> p k n", k=KC)
        xn = r2.rearrange("p (t n) -> p t n", t=NT)
        q = xn
        k_ = r3.rearrange("p (t n) -> p t n", t=NT)
        oT = r3.rearrange("p (k n) -> p k n", k=KC)
        v = work[:, W_V:W_V + 4096].rearrange("p (t n) -> p t n", t=4)
        kc = gate_bc[:, 0, :]
        kT = work[:, W_KT:W_KT + 4096].rearrange("p (k n) -> p k n", k=KC)
        pr_ = work[:, W_P:W_P + 1536].rearrange("p (i m n) -> p i m n", i=2, m=2)
        ptt = work[:, W_PT:W_PT + 768].rearrange("p (m n) -> p m n", m=2)
        tmp1 = work[:, W_P:W_P + 1024]
        tmp2 = work[:, W_P + 1024:W_P + 2048]
        hperm = r1.rearrange("p (t n) -> p t n", t=NT)
        gbc = work[:, W_R2:W_R2 + 1024]
        junk = [work[:, a:a + 1024] for a in (W_R2 + 1024, W_R2 + 2048, W_R3 + 1024)]
        hTr = work[:, W_R3:W_R3 + 1024].rearrange("p (b n) -> p b n", b=2)
        sbc = work[:, W_KT:W_KT + 4096].rearrange("p (v m n) -> p v m n", v=2, m=2)
        xg = work[:, 0:TILES * 512]
        W_X = TILES * 512
        xc = work[:, W_X:W_X + 1024].rearrange("p (b n) -> p b n", b=2)
        xT = work[:, W_X + 1024:W_X + 2048].rearrange("p (b c n) -> p b c n", b=2, c=4)
        sg = work[:, W_X + 2048:W_X + 2560].rearrange("p (b n) -> p b n", b=2)
        hE = work[:, W_X + 2560:W_X + 3072].rearrange("p (b n) -> p b n", b=2)
        hTt = work[:, W_X + 3072:W_X + 3584].rearrange("p (b c n) -> p b c n", b=2, c=2)
        yk = work[:, 0:6144].rearrange("p (j n) -> p j n", j=6)
        ubuf = work[:, 6144:7168]
        assert W_X + 3584 <= 19712

        rt = modsb[:].rearrange("p a b -> p (a b)")

        def R(a, n):
            return rt[:, a:a + n]

        def plan():
            jobs, n = [], 0

            def add(kind, l, j):
                nonlocal n
                jobs.append((kind, l, j, n % NSLOT, n // NSLOT))
                n += 1
            for j in range(4):
                add("mod", 0, j)
            for j in range(3):
                add("qkv", 0, j)
            for j in range(4, 12):
                add("mod", 0, j)
            for j in range(12):
                add("mod", 1, j)
            for j in range(2):
                add("wo", 0, j)
            return jobs, n
        jobs, _ = plan()
        uses = [0] * NSLOT
        place = {}
        for kind, l, j, s, _u in jobs:
            place[(kind, l, j)] = (s, uses[s])
            uses[s] += 1
        moe_base = [list(uses)]
        for s in range(NSLOT):
            uses[s] += 8
        jobs_b = [("qkv", 1, j) for j in range(6)] + [("wo", 1, j) for j in range(2)]
        for n, (kind, l, j) in enumerate(jobs_b):
            place[(kind, l, j)] = (n % NSLOT, uses[n % NSLOT])
            uses[n % NSLOT] += 1
        moe_base.append(list(uses))

        w_ready = [S(f"w_ready{s}") for s in range(NSLOT)]

        def last_use(kind, l, j):
            return at("mod_ps", l, j + 1) if kind == "mod" else at(f"{kind}_done", l, NT * (j + 1))

        wqkv = [t_["w_qkv_a"][0], t_["w_qkv_b"][0]]
        wo = [t_["w_o_a"][0], t_["w_o_b"][0]]

        def chunk_src(w, j):
            return w.rearrange("(p k) n -> p k n", k=KC)[:, :, 512 * j:512 * (j + 1)]

        block = ctx.enter_context(nc.Block())

        @block.sync
        def _(sp):
            freed = [None] * NSLOT

            def load(kind, l, j):
                s, _ = place[(kind, l, j)]
                if freed[s]:
                    sp.wait_ge(*freed[s])
                freed[s] = last_use(kind, l, j)
                src = {"mod": t_["w_mod"][l], "qkv": wqkv[l], "wo": wo[l]}[kind]
                sp.dma_start(ring[:, s, :].rearrange("p (k n) -> p k n", k=KC), chunk_src(src, j)).then_inc(w_ready[s], 16)

            def expert(l, e, par):
                for m, w in enumerate((t_["w_gate"], t_["w_up"], t_["w_down"])):
                    s = 3 * par + m
                    src = w[l, bass.ds(e, 1)]
                    if m < 2:
                        pat = dict(dst=ring[:, s, :], src=src.rearrange("a (p k) n -> (a p) (k n)", k=KC))
                    else:
                        pat = dict(dst=ring[:, s, :].rearrange("p (q n) -> p q n", q=4), src=src.rearrange("a (q p) n -> p (a q) n", p=P))
                    yield m, s, pat

            def experts(l):
                for par in range(2):
                    for m, s, a in expert(l, par, par):
                        sp.wait_ge(*freed[s])
                        sp.dma_start(a["dst"], a["src"]).then_inc(w_ready[s], 16)
                with sp.Fori(1, E // 2) as i:
                    for par in range(2):
                        for m, s, a in expert(l, 2 * i + par, par):
                            sp.wait_ge(*at("gu_main" if m < 2 else "down_main", l, 2 * i + (par - 1)))
                            sp.dma_start(a["dst"], a["src"]).then_inc(w_ready[s], 16)
                for s in range(NSLOT):
                    freed[s] = at("gu_main" if s % 3 < 2 else "down_main", l, E - 1 + s // 3)

            for kind, l, j, _s, _u in jobs:
                load(kind, l, j)
            experts(0)
            for kind, l, j in jobs_b:
                load(kind, l, j)
            experts(1)

        @block.gpsimd
        def _(pool):
            def bc(ap1d):
                return ap1d.partition_broadcast(P)

            pool.dma_start(cf[:], t_["consts"]).then_inc(S("ld_const"), 16)
            pool.dma_start(ci[:], t_["iconsts"]).then_inc(S("ld_const"), 16)
            pool.dma_start(cvec[:, 0, :], t_["c_ctx"].rearrange("(p k) -> p k", k=KC)).then_inc(S("ld_c"), 16)
            pool.dma_start(cvec[:, 1, :], t_["c"][0].rearrange("(p k) -> p k", k=KC)).then_inc(S("ld_c"), 16)
            pool.dma_start(x[:, 0, :], t_["x_prompt"][0]).then_inc(S("ld_x"), 16)
            pool.dma_start(x[:, 1:3, :], t_["x_sample"][0].rearrange("(t p) n -> p t n", p=P)).then_inc(S("ld_x"), 16)
            pool.memset(modsb[:], 0.0).then_inc(S("mod_zero"), 1)
            pool.memset(work[:, W_R3:W_X], 0.0).then_inc(S("work_zero"), 1)
            pool.memset(cs[:], 0.0).then_inc(S("cs_zero"), 1)

            def load_bias(l):
                for vec in range(2):
                    pool.dma_start(modsb[vec:P:32, :, :],
                                   t_["b_mod"][l].rearrange("(n g c) -> g n c", g=4, c=P)).then_inc(S("bias"), 16)

            pool.wait_ge(S("mod_zero"), 1)
            load_bias(0)
            for l in range(2):
                pool.dma_start(gcol[:, l, :], t_["g_attn"][l].rearrange("(p k) -> p k", k=KC)).then_inc(S("ld_par"), 16)
            pool.dma_start(gqk[:, 0, :], bc(t_["g_q_a"][0])).then_inc(S("ld_par"), 16)
            pool.dma_start(gqk[:, 1, :], bc(t_["g_k_a"][0])).then_inc(S("ld_par"), 16)
            pool.dma_start(gsub[:], bc(t_["g_sub_b"][0])).then_inc(S("ld_par"), 16)
            for i, n in enumerate(("lam_q1", "lam_k1", "lam_q2", "lam_k2")):
                pool.dma_start(lamv[:, i, :], bc(t_[n][0])).then_inc(S("ld_par"), 16)
            pool.dma_start(wr[:], t_["w_router"].rearrange("(p k) e -> p k e", k=KC)).then_inc(S("ld_par"), 16)
            pool.dma_start(br[:], bc(t_["b_router"])).then_inc(S("ld_par"), 16)
            pool.wait_ge(S("ld_const"), 32)
            for l in range(2):
                pool.dma_start(list_ds[l].rearrange("(p c) w -> p (c w)", p=CAP), ci[0:CAP, 12:]).then_inc(S("list_init"), 16)

            def mod_store(l, part):
                lo, hi = (0, 4) if part == 0 else (4, 12)
                pool.wait_ge(*at("mod_sb", l, hi))
                for vec in range(2):
                    pool.dma_start(mod_d[l, vec].rearrange("(n g c) -> g n c", g=4, c=P)[:, lo:hi, :],
                                   modsb[vec:P:32, lo:hi, :]).then_inc(S("mod_stored"), 16)

            def mod_cols(l):
                pool.wait_ge(*at("mod_stored", l, 32 if l == 0 else 64))
                for vec in range(2):
                    pool.dma_start(colp[:, vec, :, :],
                                   mod_d[l, vec, 0:2 * D].rearrange("(m p k) -> p m k", m=2, k=KC)).then_inc(S("ld_cols"), 16)

            def row_bc(dst, l, vec, m, sem):
                pool.dma_start(dst, bc(mod_d[l, vec, m * D:(m + 1) * D])).then_inc(S(sem), 16)

            def cache(l):
                pool.wait_ge(S("work_zero"), 1)
                kk, vv = (t_["cache_k_a"], t_["cache_v_a"]) if l == 0 else (t_["cache_k_b"], t_["cache_v_b"])
                n = 256 if l == 0 else 1024
                fk = "p a b -> p (a b)" if l == 0 else "p a b c -> p (a b c)"
                pool.dma_start(kc[:, 0:n], kk[0, 0].rearrange(fk)).then_inc(S("ld_cache"), 16)
                pool.dma_start(v[:, 3, 0:n], vv[0, 0].rearrange("p a b -> p (a b)")).then_inc(S("ld_cache"), 16)

            def states(l):
                n = 256 if l == 0 else 1024
                pool.wait_ge(*at("qkv_copied", l, 9 if l == 0 else 18))
                pool.dma_start(t_[f"state_v{l}"], v[:, 0, 0:n]).then_inc(S("state_out"), 16)
                if l == 0:
                    pool.wait_ge(*at("qk_ready", 0, 1))
                pool.dma_start(t_[f"state_k{l}"], k_[:, 0, 0:n]).then_inc(S("state_out"), 16)

            def moe_dmas(l):
                pool.wait_ge(*at("x_attn", l, 6))
                pool.wait_ge(*at("state_out", l, 32))
                pool.wait_ge(*at("mod_stored", 1, 64))
                pool.dma_start(gbc, bc(t_["g_ffn"][l])).then_inc(S("ld_rows"), 16)
                for vec in range(2):
                    row_bc(sbc[:, vec, 0, :], l, vec, 3, "ld_rows")
                    row_bc(sbc[:, vec, 1, :], l, vec, 4, "ld_rows")
                for vec in range(2):
                    row_bc(gate_bc[:, vec, :], l, vec, 5, "ld_gate_ffn")
                for t in range(NT):
                    pool.wait_ge(*at("h_ready", l, t + 1))
                    pool.dma_start(h_ds[l].rearrange("(t p h) n -> t p (h n)", t=NT, h=2)[t], hperm[:, t, :]).then_inc(S("h_stored"), 16)
                pool.wait_ge(*at("rows_ready", l, 1))
                pool.wait_ge(S("list_init"), 32)
                for k in range(2 * NT):
                    pool.indirect_dma_start(list_ds[l], bass.IndirectOffsetOnAxis(ap=rti[:, k:k + 1], axis=0),
                                            ci[:, 2 * k:2 * k + 2], None).then_inc(S("listed"), 16)
                pool.wait_ge(*at("listed", l, 96))
                for half in range(2):
                    pool.dma_start(lst[CAP * half:CAP * (half + 1), :],
                                   list_ds[l].rearrange("(p c) w -> p (c w)", p=CAP)).then_inc(S("ld_list"), 16)
                pool.wait_ge(*at("h_stored", l, 16 * NT))
                pool.wait_ge(*at("idx_ready", l, 1))
                order = []
                xs = 0
                for e in range(E):
                    order.append(e)
                    for _ in range(2):
                        if xs < XT:
                            order.append(E + xs)
                            xs += 1
                GR = 4

                def gathered(n):
                    pool.wait_ge(*at(f"gather{n % GR}", l, 16 * (n // GR + 1)))
                    pool.memset(tick[0:1, n:n + 1], 0.0).then_inc(S("xg_main" if order[n] < E else "xg_more"), 1)

                for n, c in enumerate(order):
                    pool.indirect_dma_start(xg[:, 512 * c:512 * (c + 1)], None, h_ds[l],
                                            bass.IndirectOffsetOnAxis(ap=gi[:, 2 * c:2 * c + 1], axis=0),
                                            bounds_check=2 * NT * P - 1, oob_is_err=False).then_inc(S(f"gather{n % GR}"), 16)
                    if n >= GR - 1:
                        gathered(n - GR + 1)
                for n in range(TILES - GR + 1, TILES):
                    gathered(n)
                for c in range(TILES):
                    if c < E:
                        pool.wait_ge(*at("y_main", l, c + 2))
                    elif c == E:
                        pool.wait_ge(*at("tiles_done", l, 1))
                    pool.indirect_dma_start(y_ds[l], bass.IndirectOffsetOnAxis(ap=gi[:, 2 * c + 1:2 * c + 2], axis=0),
                                            xg[:, 512 * c:512 * (c + 1)], None,
                                            bounds_check=4 * NT * P - 1, oob_is_err=False).then_inc(S("scattered"), 16)
                pool.wait_ge(*at("scattered", l, 16 * TILES))
                for j in range(2 * NT):
                    pool.dma_start(yk[:, j, :], y_ds[l].rearrange("(j p h) n -> j p (h n)", p=P, h=2)[j]).then_inc(S(f"ld_y{j % NT}"), 16)

            mod_store(0, 0)
            mod_cols(0)
            cache(0)
            mod_store(0, 1)
            pool.wait_ge(*at("mod_stored", 0, 64))
            pool.wait_ge(*at("qk_turned", 0, 1))
            for vec in range(2):
                row_bc(gate_bc[:, vec, :], 0, vec, 2, "ld_gate_attn")
            load_bias(1)
            states(0)
            mod_store(1, 0)
            mod_store(1, 1)
            pool.wait_ge(S("a1_ready"), 1)
            mod_cols(1)
            moe_dmas(0)
            pool.wait_ge(*at("x_moe", 0, 3))
            cache(1)
            pool.wait_ge(*at("qk_turned", 1, 2))
            for vec in range(2):
                row_bc(gate_bc[:, vec, :], 1, vec, 2, "ld_gate_attn")
            states(1)
            moe_dmas(1)
            pool.wait_ge(*at("x_moe", 1, 3))
            pool.dma_start(ubuf, bc(t_["g_final"])).then_inc(S("ld_gf"), 16)
            for t in range(NT):
                pool.wait_ge(S("y_ready"), t + 1)
                dst = t_["y_prompt"] if t == 0 else t_["y_sample"][P * (t - 1):P * t, :]
                pool.dma_start(dst, yk[:, t, :]).then_inc(S("y_out"), 16)
            pool.wait_ge(S("y_out"), 16 * NT)

        steps = [(t, pr) for t in range(NT) for pr in range(8)]

        def blocks_of(t):
            return [0] if t == 0 else [1, 2, 3]

        def kcols(t):
            return slice(0, P) if t == 0 else slice(P, 4 * P)

        def qk_groups(l):
            npair = 2 if l == 0 else 8
            out = []
            for b in (3, 0, 1, 2):
                for a in range(0, npair, 4):
                    out.append(("k", b, a, min(4, npair - a)))
                if b < 3:
                    for a in (0, 4):
                        out.append(("q", b, a, 4))
            return out

        @block.tensor
        def _(pe):
            def slot_ready(kind, l, j):
                s, u = place[(kind, l, j)]
                pe.wait_ge(w_ready[s], 16 * (u + 1))
                return s

            nmod = [0]

            def mod_slot(l, j):
                s = slot_ready("mod", l, j)
                if l == 0 and j == 0:
                    pe.wait_ge(S("cs_ready"), 1)
                if j >= 1:
                    pe.wait_ge(*at("mod_sb", l, j))
                for k in range(KC):
                    for g in range(4):
                        mm = pe.matmul(PS[32 * g:32 * g + 32, 7, 0:P], cs[:, k, :],
                                       ring[:, s, 512 * k + P * g:512 * k + P * (g + 1)], start=(k == 0), stop=(k == KC - 1))
                mm.then_inc(S("mod_ps"), 1)

            def norm_transposes(l):
                for g in range(6):
                    t, half = g // 2, g % 2
                    pe.wait_ge(*at("xn_ready", l, t + 1))
                    if g >= 2:
                        pe.wait_ge(*at("hT_dve" if g % 2 == 0 else "hT_act", l, g // 2))
                    for c in range(4):
                        tr = pe.transpose(PS[:, g % 2, P * c:P * (c + 1)], xn[:, t, 4 * half + c::KC], ident)
                    tr.then_inc(S("xn_turned"), 1)

            def project(l, kind, nslots, lhs, ready):
                for j in range(nslots):
                    s = slot_ready(kind, l, j)
                    for t in range(NT):
                        n = NT * j + t
                        if j == 0:
                            ready(t)
                        else:
                            pe.wait_ge(*at(f"{kind}_copied", l, n - NT + 1))
                        for k in range(KC):
                            mm = pe.matmul(PS[:, 2 + t, :], lhs[:, k, P * t:P * (t + 1)], ring[:, s, 512 * k:512 * (k + 1)],
                                           start=(k == 0), stop=(k == KC - 1))
                        mm.then_inc(S(f"{kind}_done"), 1)

            def hT_ready(l):
                def f(t):
                    pe.wait_ge(*at("hT_dve", l, t + 1))
                    pe.wait_ge(*at("hT_act", l, t + 1))
                return f

            def qk_transposes(l):
                pe.wait_ge(*at("ld_cache", l, 32))
                for n, (what, b, a, cnt) in enumerate(qk_groups(l)):
                    if b == 0 and l == 1:
                        pe.wait_ge(*at("qkv_copied", 1, 12))
                    elif b < 3:
                        pe.wait_ge(*at("qk_ready", l, b + 1 - l))
                    if n >= 2:
                        pe.wait_ge(*at("qkT_dve" if n % 2 == 0 else "qkT_act", l, n // 2))
                    for c in range(cnt):
                        i = a + c
                        if what == "k":
                            src = kc[:, P * i:P * (i + 1)] if b == 3 else k_[:, b, P * i:P * (i + 1)]
                        else:
                            src = q[:, b, P * i:P * (i + 1)]
                        tr = pe.transpose(PS[:, n % 2, P * c:P * (c + 1)], src, ident)
                    tr.then_inc(S("qk_turned"), 1)

            def scores(l, i):
                t, pr = steps[i]
                nk = P * len(blocks_of(t))
                if i == 0:
                    g = len(qk_groups(l))
                    pe.wait_ge(*at("qkT_dve", l, (g + 1) // 2))
                    pe.wait_ge(*at("qkT_act", l, g // 2))
                    pe.wait_ge(*at("qkv_copied", l, 9 if l == 0 else 18))
                if i >= 2:
                    pe.wait_ge(*at("p_ready", l, i - 1))
                for m in range(2):
                    mm = pe.matmul(PS[:, 2 * (i % 2) + m, 0:nk], qT[64 * m:64 * m + 64, pr, P * t:P * (t + 1)],
                                   kT[64 * m:64 * m + 64, pr // 4 if l == 0 else pr, kcols(t)], start=True, stop=True)
                mm.then_inc(S("s_done"), 1)

            def weighted(l, i):
                t, pr = steps[i]
                bl = blocks_of(t)
                pe.wait_ge(*(at("p_ready", 0, i + 1) if l == 0 else (S("a_ready"), i + 1)))
                for m in range(2 if l == 0 else 1):
                    for c in range(len(bl)):
                        tr = pe.transpose(PS[:, 4 + m, P * c:P * (c + 1)], pr_[:, i % 2, m, P * c:P * (c + 1)], ident)
                tr.then_inc(S("p_turned"), 1)
                pe.wait_ge(*at("pT_act", l, i + 1))
                if l == 0:
                    pe.wait_ge(*at("pT_dve", l, i + 1))
                if i >= 1:
                    pe.wait_ge(*at("o_copied", l, i))
                for m in range(2 if l == 0 else 1):
                    for c, b in enumerate(bl):
                        if l == 0:
                            g = 2 * (pr // 4) + m
                            out, vals = PS[:, 6, 64 * m:64 * m + 64], v[:, b, 64 * g:64 * g + 64]
                        else:
                            out, vals = PS[:, 6, 0:P], v[:, b, P * pr:P * (pr + 1)]
                        mm = pe.matmul(out, ptt[:, m, P * c:P * (c + 1)], vals, start=(c == 0), stop=(c == len(bl) - 1))
                mm.then_inc(S("o_done"), 1)

            def o_transposes(l):
                for g in range(6):
                    t, half = g // 2, g % 2
                    pe.wait_ge(*(at("o_copied", 0, 8 * (t + 1)) if l == 0 else (S("o_ready"), t + 1)))
                    if g >= 2:
                        pe.wait_ge(*at("oT_dve" if g % 2 == 0 else "oT_act", l, g // 2))
                    for c in range(4):
                        tr = pe.transpose(PS[:, g % 2, P * c:P * (c + 1)], q[:, t, 4 * half + c::KC], ident)
                    tr.then_inc(S("o_turned"), 1)

            def oT_ready(l):
                def f(t):
                    pe.wait_ge(*at("oT_dve", l, t + 1))
                    pe.wait_ge(*at("oT_act", l, t + 1))
                return f

            def router(l):
                for t in range(NT):
                    pe.wait_ge(*at("h_ready", l, t + 1))
                    for half in range(2):
                        g = 2 * t + half
                        if g >= 2:
                            pe.wait_ge(*at("hr_dve" if half == 0 else "hr_act", l, t))
                        for c in range(4):
                            tr = pe.transpose(PS[:, half, P * c:P * (c + 1)],
                                              hperm[:, t, P * (4 * half + c):P * (4 * half + c + 1)], ident)
                        tr.then_inc(S("hr_turned"), 1)
                    pe.wait_ge(*at("hr_dve", l, t + 1))
                    pe.wait_ge(*at("hr_act", l, t + 1))
                    for k in range(KC):
                        mm = pe.matmul(PS[:, 2, E * t:E * (t + 1)], hTr[:, k // 4, P * (k % 4):P * (k % 4 + 1)], wr[:, k, :],
                                       start=(k == 0), stop=(k == KC - 1))
                    mm.then_inc(S("logits"), 1)
                pe.wait_ge(*at("oh_ready", l, 1))
                for t in range(NT):
                    for u in range(t + 1):
                        mm = pe.matmul(PS[:, 3, E * t:E * (t + 1)], upper if u == t else ones, R(0, 48)[:, E * u:E * (u + 1)],
                                       start=(u == 0), stop=(u == t))
                for u in range(NT):
                    mm = pe.matmul(PS[:, 3, 64:64 + E], ones, R(0, 48)[:, E * u:E * (u + 1)], start=(u == 0), stop=(u == NT - 1))
                mm.then_inc(S("ranks"), 1)

            def experts(l):
                base = moe_base[l]

                def tile(b, par, nth):
                    B, tag = 4 * b, "main" if b == 0 else "more"
                    pe.wait_ge(*at(f"xc_{tag}", l, nth))
                    for c in range(4):
                        tr = pe.transpose(PS[:, B, P * c:P * (c + 1)], xc[:, b, P * c:P * (c + 1)], ident)
                    tr.then_inc(tile_sem(f"x_turned_{tag}", l), 1)
                    pe.wait_ge(*at(f"xT_{tag}", l, nth))
                    s = 3 * par
                    for k in range(KC):
                        for g in range(2):
                            mm = pe.matmul(PS[64 * g:64 * g + 64, B + 1, :], xT[:, b, k % 4, 64 * (k // 4):64 * (k // 4) + 64],
                                           ring[:, s:s + 2, 512 * k + 256 * g:512 * k + 256 * (g + 1)],
                                           start=(k == 0), stop=(k == KC - 1))
                    mm.then_inc(tile_sem(f"gu_{tag}", l), 1)
                    pe.wait_ge(*at(f"h_{tag}", l, nth))
                    for c in range(2):
                        tr = pe.transpose(PS[:, B + 2, P * c:P * (c + 1)], hE[:, b, P * c:P * (c + 1)], ident)
                    tr.then_inc(tile_sem(f"h_turned_{tag}", l), 1)
                    pe.wait_ge(*at(f"hT_{tag}", l, nth))
                    pe.wait_ge(*at(f"y_{tag}", l, nth))
                    pe_down(b, B, s + 2, tag, nth)

                def pe_down(b, B, s, tag, nth):
                    for f in range(4):
                        for g in range(2):
                            mm = pe.matmul(PS[64 * g:64 * g + 64, B + 3, :], hTt[:, b, f % 2, 64 * (f // 2):64 * (f // 2) + 64],
                                           ring[:, s, 1024 * f + 512 * g:1024 * f + 512 * (g + 1)], start=(f == 0), stop=(f == 3))
                    mm.then_inc(tile_sem(f"down_{tag}", l), 1)

                pe.wait_ge(*at("nx_ready", l, 1))
                more = pe.alloc_register(f"pe_more{l}")
                pe.reg_mov(more, 0)
                with pe.Fori(0, E // 2) as i:
                    for par in range(2):
                        e = 2 * i + par
                        for m in range(3):
                            pe.wait_ge(w_ready[3 * par + m], 16 * (base[3 * par + m] + i + 1))
                        nx = pe.value_load(nxi[0:1, bass.ds(e, 1)], min_val=0, max_val=5)
                        with pe.If(nx > 0):
                            with pe.Fori(0, nx):
                                pe.reg_add(more, more, 1)
                                tile(1, par, pe.snap(more))
                            pe.nop()
                        with pe.Else():
                            pe.nop()
                        tile(0, par, e + 1)

            pe.wait_ge(S("ld_const"), 32)
            for j in range(4):
                mod_slot(0, j)
            norm_transposes(0)
            project(0, "qkv", 3, hT, hT_ready(0))
            for j in range(4, 12):
                mod_slot(0, j)
            qk_transposes(0)
            for i in range(len(steps) + 1):
                if i < len(steps):
                    scores(0, i)
                if i % 2 == 0 and i < 24:
                    mod_slot(1, i // 2)
                if i:
                    weighted(0, i - 1)
            o_transposes(0)
            project(0, "wo", 2, oT, oT_ready(0))
            router(0)
            experts(0)
            norm_transposes(1)
            project(1, "qkv", 6, hT, hT_ready(1))
            qk_transposes(1)
            for i in range(len(steps) + 1):
                if i < len(steps):
                    scores(1, i)
                if i:
                    weighted(1, i - 1)
            o_transposes(1)
            project(1, "wo", 2, oT, oT_ready(1))
            router(1)
            experts(1)

        @block.vector
        def _(dve):
            chain = [0]

            def link(ins):
                chain[0] += 1
                ins.then_inc(S("dve_chain"), 1)
                dve.wait_ge(S("dve_chain"), chain[0])

            def done(ins, name, n):
                ins.then_inc(S(name), 1)
                dve.wait_ge(S(name), n)

            def add_bias(l, j):
                dve.wait_ge(*at("mod_ps", l, j + 1))
                if j == 0:
                    dve.wait_ge(*at("bias", l, 32))
                dve.tensor_tensor(modsb[:, j, :], PS[:, 7, 0:P], modsb[:, j, :], ALU.add).then_inc(S("mod_sb"), 1)

            roots = [0]

            def rstd(n, inv_n):
                roots[0] += 1
                dve.tensor_scalar(rs[:, 0:n], ss[:, 0:n], inv_n, EPS, ALU.mult, ALU.add).then_inc(S("var_ready"), 1)
                dve.wait_ge(S("std_ready"), roots[0])
                link(dve.reciprocal(rs[:, 0:n], rs[:, 0:n]))

            def norm_attn(l):
                dve.wait_ge(*at("sq_attn", l, NT))
                rstd(NT, 1.0 / D)
                for t in range(NT):
                    dve.tensor_scalar(xn[:, t, :], x[:, t, :], rs[:, t:t + 1], None, ALU.mult).then_inc(S("xn_ready"), 1)

            def cols(l):
                dve.wait_ge(*at("ld_cols", l, 32))
                dve.wait_ge(S("ld_par"), 16 * 11)
                for vec in range(2):
                    ins = dve.scalar_tensor_tensor(a1[:, vec, :], colp[:, vec, 1, :], 1.0, gcol[:, l, :], ALU.add, ALU.mult)
                ins.then_inc(S("a1_ready" if l == 0 else "a1_ready_b"), 1)
                dve.wait_ge(S("a1_ready" if l == 0 else "a1_ready_b"), 1)

            def hT_even(l):
                for g in range(0, 6, 2):
                    t = g // 2
                    vec = min(t, 1)
                    dve.wait_ge(*at("xn_turned", l, g + 1))
                    for c in range(4):
                        ins = dve.tensor_scalar(hT[:, c, P * t:P * (t + 1)], PS[:, 0, P * c:P * (c + 1)],
                                                a1[:, vec, c:c + 1], colp[:, vec, 0, c:c + 1], ALU.mult, ALU.add)
                    ins.then_inc(S("hT_dve"), 1)

            def head_sq(src, nh, w, dst):
                link(dve.tensor_tensor(tmp1[:, 0:nh * w], src, src, ALU.mult))
                link(dve.tensor_reduce(dst, tmp1[:, 0:nh * w].rearrange("p (h d) -> p h d", h=nh), X, ALU.add))

            def scale_heads(dst, nh, w, r, g, end=link):
                v3 = dst.rearrange("p (h d) -> p h d", h=nh)
                link(dve.tensor_tensor(v3, v3, r.unsqueeze(2).to_broadcast([P, nh, w]), ALU.mult))
                end(dve.tensor_tensor(v3, v3, g.unsqueeze(1).to_broadcast([P, nh, w]), ALU.mult))

            def rope(dst, nh, t, end=link):
                cos = cf[:, C_COS + 64 * (t - 1):C_COS + 64 * t]
                sin = cf[:, C_SIN + 64 * (t - 1):C_SIN + 64 * t]
                n = nh * 64
                dve.tensor_tensor(tmp1[:, 0:n].rearrange("p (h d) -> p h d", h=nh), dst.rearrange("p (h d) -> p h d", h=nh),
                                  cos.unsqueeze(1).to_broadcast([P, nh, 64]), ALU.mult)
                s5 = dst.rearrange("p (h f d) -> p h f d", h=2 * nh, f=2)
                t5 = tmp2[:, 0:n].rearrange("p (h f d) -> p h f d", h=2 * nh, f=2)
                for rc in range(2):
                    for f in range(2):
                        sn = sin[:, 32 * rc + 16 * f:32 * rc + 16 * f + 16]
                        ins = dve.tensor_tensor(t5[:, rc::2, f, :], s5[:, rc::2, 1 - f, :],
                                                sn.unsqueeze(1).to_broadcast([P, nh, 16]), ALU.mult)
                link(ins)
                end(dve.tensor_tensor(dst, tmp1[:, 0:n], tmp2[:, 0:n], ALU.add))

            def qk_norm_rope(l):
                nk = 256 if l == 0 else 1024
                dve.wait_ge(*at("qkv_copied", l, 9 if l == 0 else 12))
                for t in range(NT):
                    end = lambda ins, t=t: done(ins, "qk_ready", t + 1 + 2 * l)
                    if l == 0:
                        head_sq(q[:, t, :], 16, 64, ss[:, 0:16])
                        head_sq(k_[:, t, 0:256], 4, 64, ss[:, 16:20])
                        rstd(20, 1.0 / 64)
                        scale_heads(q[:, t, :], 16, 64, rs[:, 0:16], gqk[:, 0, :])
                        scale_heads(k_[:, t, 0:256], 4, 64, rs[:, 16:20], gqk[:, 1, :], link if t else end)
                    if t:
                        rope(q[:, t, :], 16, t)
                        rope(k_[:, t, 0:nk], nk // 64, t, end)

            def evac_group(l, n, what, b, a, cnt, copy):
                src = PS[:, n % 2, 0:P * cnt].rearrange("p (c n) -> p c n", c=cnt)
                dst = (kT if what == "k" else qT)[:, a:a + cnt, P * b:P * (b + 1)]
                return copy(dst, src)

            def qk_even(l):
                for n, (what, b, a, cnt) in enumerate(qk_groups(l)):
                    if n % 2 == 0:
                        dve.wait_ge(*at("qk_turned", l, n + 1))
                        evac_group(l, n, what, b, a, cnt, dve.tensor_copy).then_inc(S("qkT_dve"), 1)

            def row_max(l, i):
                t, pr = steps[i]
                nk = P * len(blocks_of(t))
                dve.wait_ge(*at("s_done", l, i + 1))
                link(dve.tensor_reduce(mx[:, i % 2, :], PS[:, 2 * (i % 2):2 * (i % 2) + 2, 0:nk], X, ALU.max))
                dve.tensor_scalar(nm[:, i % 2, :], mx[:, i % 2, :], -0.125, None, ALU.mult).then_inc(S("nm_ready"), 1)

            def after_exp(l, i):
                t, pr = steps[i]
                nk = P * len(blocks_of(t))
                dve.wait_ge(*at("p_ready", l, i + 1))
                link(dve.reciprocal(rsm[:, i % 2, :], sm[:, i % 2, :]))
                if l == 0:
                    dve.wait_ge(*at("p_turned", l, i + 1))
                    dve.tensor_copy(ptt[:, 0, 0:nk], PS[:, 4, 0:nk]).then_inc(S("pT_dve"), 1)
                else:
                    dve.tensor_tensor(rsm[:, i % 2, 1:2], rsm[:, i % 2, 1:2], small[:, 4:5], ALU.mult)
                    link(dve.tensor_scalar(pr_[:, i % 2, 0, 0:nk], pr_[:, i % 2, 0, 0:nk], rsm[:, i % 2, 0:1], None, ALU.mult))
                    dve.scalar_tensor_tensor(pr_[:, i % 2, 0, 0:nk], pr_[:, i % 2, 1, 0:nk], rsm[:, i % 2, 1:2],
                                             pr_[:, i % 2, 0, 0:nk], ALU.mult, ALU.add).then_inc(S("a_ready"), 1)

            def take_o(l, i):
                t, pr = steps[i]
                dve.wait_ge(*at("o_done", l, i + 1))
                if l == 0:
                    dst = q[:, t, :].rearrange("p (m f d) -> p m f d", m=2, f=2)[:, pr // 4, :, 64 * (pr % 4):64 * (pr % 4) + 64]
                    src = PS[:, 6, 0:P].rearrange("p (f d) -> p f d", f=2)
                    dve.tensor_tensor(dst, src, rsm[:, i % 2, :].unsqueeze(2).to_broadcast([P, 2, 64]),
                                      ALU.mult).then_inc(S("o_copied"), 1)
                else:
                    dve.tensor_copy(q[:, t, P * pr:P * (pr + 1)], PS[:, 6, 0:P]).then_inc(S("o_copied"), 1)

            def attention(l):
                for i in range(len(steps) + 1):
                    if i < len(steps):
                        row_max(l, i)
                    if l == 0 and i % 2 == 0 and i < 24:
                        add_bias(1, i // 2)
                    if i:
                        after_exp(l, i - 1)
                        take_o(l, i - 1)
                for t in range(NT):
                    if l == 1:
                        if t == 0:
                            dve.wait_ge(*at("o_copied", 1, len(steps)))
                        head_sq(q[:, t, :], 8, P, ss[:, 0:8])
                        rstd(8, 1.0 / P)
                        scale_heads(q[:, t, :], 8, P, rs[:, 0:8], gsub[:], lambda ins, t=t: done(ins, "o_ready", t + 1))

            def oT_even(l):
                dve.wait_ge(*at("state_out", l, 32))
                for g in range(0, 6, 2):
                    dve.wait_ge(*at("o_turned", l, g + 1))
                    dve.tensor_copy(oT[:, 0:4, P * (g // 2):P * (g // 2 + 1)],
                                    PS[:, 0, :].rearrange("p (c n) -> p c n", c=4)).then_inc(S("oT_dve"), 1)

            def add_attn(l):
                dve.wait_ge(*at("ld_gate_attn", l, 32))
                for j in range(2):
                    for t in range(NT):
                        n = NT * j + t
                        dve.wait_ge(*at("wo_done", l, n + 1))
                        dve.tensor_tensor(tmp1[:, 0:512], PS[:, 2 + t, :], gate_bc[:, min(t, 1), 512 * j:512 * (j + 1)],
                                          ALU.mult).then_inc(S("wo_copied"), 1)
                        dve.wait_ge(*at("wo_copied", l, n + 1))
                        dve.tensor_tensor(x[:, t, 512 * j:512 * (j + 1)], x[:, t, 512 * j:512 * (j + 1)], tmp1[:, 0:512],
                                          ALU.add).then_inc(S("x_attn"), 1)
                        dve.wait_ge(*at("x_attn", l, n + 1))

            def norm_ffn(l):
                dve.wait_ge(*at("sq_ffn", l, NT))
                rstd(NT, 1.0 / D)
                dve.wait_ge(*at("ld_rows", l, 80))
                for vec in range(2):
                    link(dve.scalar_tensor_tensor(sbc[:, vec, 1, :], sbc[:, vec, 1, :], 1.0, gbc, ALU.add, ALU.mult))
                for t in range(NT):
                    vec = min(t, 1)
                    out = hperm[:, t, :].rearrange("p (k a) -> p a k", k=KC)
                    tmp = tmp1.rearrange("p (a k) -> p a k", k=KC)
                    link(dve.scalar_tensor_tensor(tmp1[:], x[:, t, :], rs[:, t:t + 1], sbc[:, vec, 1, :], ALU.mult, ALU.mult))
                    ins = dve.tensor_tensor(out, tmp, sbc[:, vec, 0, :].rearrange("p (a k) -> p a k", k=KC), ALU.add)
                    ins.then_inc(S("h_ready"), 1)
                    dve.wait_ge(*at("h_ready", l, t + 1))

            def route(l):
                for t in range(NT):
                    dve.wait_ge(*at("hr_turned", l, 2 * t + 1))
                    if t:
                        dve.wait_ge(*at("logits", l, t))
                    dve.tensor_copy(hTr[:, 0, :], PS[:, 0, :]).then_inc(S("hr_dve"), 1)
                dve.wait_ge(*at("logits", l, NT))
                oh = R(0, 48)
                sg_, m_ = R(48, 48), R(96, 48)
                p6 = R(144, 72).rearrange("p (g c) -> p g c", g=12)
                t3 = lambda ap, n: ap.rearrange("p (t e) -> p t e", t=n)
                oh1, oh2 = R(216, 48), R(264, 48)
                cand = R(312, 48)
                gs, gm, ing, t0 = R(360, 12), R(372, 3), R(375, 12), R(387, 12)
                vv = R(400, 6)
                cc = R(406, 6)
                sm3, rk = R(412, 3), R(416, 48)
                rr, bs, jj, tl = R(464, 6), R(470, 6), R(476, 6), R(482, 6)
                pref = R(490, 64)
                cmp_ = R(556, 80)
                dve.tensor_tensor(t3(sg_, 3), t3(PS[:, 2, 0:48], 3), br[:].unsqueeze(1).to_broadcast([P, 3, E]),
                                  ALU.add).then_inc(S("lg_ready"), 1)
                dve.wait_ge(*at("sig_ready", l, 1))
                s4 = sg_.rearrange("p (g c) -> p g c", g=12)
                dve.tensor_tensor(p6[:, :, 0:3], s4[:, :, 0:3], s4[:, :, 1:4], ALU.add)
                dve.tensor_tensor(p6[:, :, 3:5], s4[:, :, 0:2], s4[:, :, 2:4], ALU.add)
                link(dve.tensor_tensor(p6[:, :, 5:6], s4[:, :, 0:1], s4[:, :, 3:4], ALU.add))
                link(dve.tensor_reduce(gs, p6, X, ALU.max))
                link(dve.tensor_reduce(gm, t3(gs, 3), X, ALU.max))
                link(dve.tensor_tensor(t3(t0, 3), t3(gs, 3), gm.unsqueeze(2).to_broadcast([P, 3, NG]), ALU.is_equal))
                link(dve.tensor_tensor(t3(t0, 3), t3(t0, 3),
                                       cf[:, C_REVG:C_REVG + NG].unsqueeze(1).to_broadcast([P, 3, NG]), ALU.mult))
                link(dve.tensor_reduce(gm, t3(t0, 3), X, ALU.max))
                link(dve.tensor_tensor(t3(ing, 3), t3(t0, 3), gm.unsqueeze(2).to_broadcast([P, 3, NG]), ALU.is_equal))
                dve.tensor_scalar(t0, ing, 4.0, -4.0, ALU.mult, ALU.add)
                link(dve.tensor_tensor(t3(m_, 12), s4, ing.unsqueeze(2).to_broadcast([P, 12, 4]), ALU.mult))
                link(dve.tensor_tensor(t3(m_, 12), t3(m_, 12), t0.unsqueeze(2).to_broadcast([P, 12, 4]), ALU.add))
                for k, o in enumerate((oh1, oh2)):
                    vk, ck = vv[:, 3 * k:3 * k + 3], cc[:, 3 * k:3 * k + 3]
                    link(dve.tensor_reduce(vk, t3(m_, 3), X, ALU.max))
                    link(dve.tensor_tensor(t3(cand, 3), t3(m_, 3), vk.unsqueeze(2).to_broadcast([P, 3, E]), ALU.is_equal))
                    link(dve.tensor_tensor(t3(cand, 3), t3(cand, 3),
                                           cf[:, C_REVE:C_REVE + E].unsqueeze(1).to_broadcast([P, 3, E]), ALU.mult))
                    link(dve.tensor_reduce(ck, t3(cand, 3), X, ALU.max))
                    link(dve.tensor_tensor(t3(o, 3), t3(cand, 3), ck.unsqueeze(2).to_broadcast([P, 3, E]), ALU.is_equal))
                    if k == 0:
                        link(dve.scalar_tensor_tensor(m_, o, -8.0, m_, ALU.mult, ALU.add))
                dve.tensor_tensor(oh, oh1, oh2, ALU.add).then_inc(S("oh_ready"), 1)
                link(dve.tensor_tensor(sm3, vv[:, 0:3], vv[:, 3:6], ALU.add))
                link(dve.reciprocal(sm3, sm3))
                for k in range(2):
                    dve.tensor_tensor(small[:, 8 + 3 * k:11 + 3 * k], vv[:, 3 * k:3 * k + 3], sm3, ALU.mult)
                dve.memset(pref, 0.0)
                link(dve.tensor_scalar(cc, cc, -1.0, float(E), ALU.mult, ALU.add))
                dve.wait_ge(*at("ranks", l, 1))
                link(dve.tensor_copy(rk, PS[:, 3, 0:48]))
                thr = cf[:, C_THR:C_THR + 5]
                c16 = cmp_.rearrange("p (e c) -> p e c", e=E)
                link(dve.tensor_tensor(c16, PS[:, 3, 64:80].unsqueeze(2).to_broadcast([P, E, 5]),
                                       thr.unsqueeze(1).to_broadcast([P, E, 5]), ALU.is_gt))
                link(dve.tensor_reduce(pref[:, 16:32], c16, X, ALU.add))
                dve.tensor_copy(nxi[:], pref[:, 16:32]).then_inc(S("nx_ready"), 1)
                for n, step in enumerate((1, 2, 4, 8)):
                    a, b = 32 * (n % 2), 32 * ((n + 1) % 2)
                    link(dve.tensor_tensor(pref[:, b + 16:b + 32], pref[:, a + 16:a + 32], pref[:, a + 16 - step:a + 32 - step], ALU.add))
                dve.wait_ge(*at("nx_ready", l, 1))
                link(dve.tensor_copy(t0[:, 0:12], nxi[:, 0:12]))
                link(dve.tensor_tensor(pref[:, 16:32], pref[:, 16:32], nxi[:], ALU.subtract))
                for k, o in enumerate((oh1, oh2)):
                    link(dve.tensor_tensor(cand, o, rk, ALU.mult))
                    link(dve.tensor_reduce(rr[:, 3 * k:3 * k + 3], t3(cand, 3), X, ALU.add))
                    link(dve.tensor_tensor(t3(cand, 3), t3(o, 3), pref[:, 16:32].unsqueeze(1).to_broadcast([P, 3, E]), ALU.mult))
                    link(dve.tensor_reduce(bs[:, 3 * k:3 * k + 3], t3(cand, 3), X, ALU.add))
                c6 = cmp_[:, 0:30].rearrange("p (e c) -> p e c", e=6)
                link(dve.tensor_tensor(c6, rr.unsqueeze(2).to_broadcast([P, 6, 5]), thr.unsqueeze(1).to_broadcast([P, 6, 5]), ALU.is_ge))
                link(dve.tensor_reduce(jj, c6, X, ALU.add))
                link(dve.scalar_tensor_tensor(tl, jj, float(E - 1), bs, ALU.add, ALU.add))
                dve.tensor_scalar(bs, jj, 0.0, None, ALU.is_equal)
                link(dve.tensor_tensor(cc, cc, tl, ALU.subtract))
                link(dve.tensor_tensor(cc, cc, bs, ALU.mult))
                link(dve.tensor_tensor(tl, tl, cc, ALU.add))
                link(dve.scalar_tensor_tensor(rr, jj, -float(CAP), rr, ALU.mult, ALU.add))
                link(dve.scalar_tensor_tensor(tl, rr, float(TILES), tl, ALU.mult, ALU.add))
                dve.tensor_copy(rti[:], tl).then_inc(S("rows_ready"), 1)
                dve.wait_ge(*at("ld_list", l, 32))
                dve.tensor_scalar(gi[:], lst[:], 2.0, cf[:, C_HALF:C_HALF + 1], ALU.mult, ALU.add).then_inc(S("idx_ready"), 1)

            def experts(l):
                more = dve.alloc_register(f"dve_more{l}")
                dve.reg_mov(more, 0)

                def tile(b, col, nth):
                    B, tag = 4 * b, "main" if b == 0 else "more"
                    dve.wait_ge(*at(f"xg_{tag}", l, nth))
                    dve.tensor_copy(xc[:, b, :], xg[:, bass.ds(col, 512)]).then_inc(tile_sem(f"xc_{tag}", l), 1)
                    dve.wait_ge(*at(f"x_turned_{tag}", l, nth))
                    dve.tensor_copy(xT[:, b], PS[:, B, :].rearrange("p (c n) -> p c n", c=4)).then_inc(tile_sem(f"xT_{tag}", l), 1)
                    dve.wait_ge(*at(f"silu_{tag}", l, nth))
                    dve.tensor_tensor(hE[:, b, :], sg[:, b, :], PS[:, B + 1, 256:512], ALU.mult).then_inc(tile_sem(f"h_{tag}", l), 1)
                    dve.wait_ge(*at(f"h_turned_{tag}", l, nth))
                    dve.tensor_copy(hTt[:, b], PS[:, B + 2, 0:256].rearrange("p (c n) -> p c n", c=2)).then_inc(tile_sem(f"hT_{tag}", l), 1)

                with dve.Fori(0, E) as e:
                    nx = dve.value_load(nxi[0:1, bass.ds(e, 1)], min_val=0, max_val=5)
                    with dve.If(nx > 0):
                        with dve.Fori(0, nx):
                            reg = dve.snap(more)
                            tile(1, (reg + E) * 512, reg + 1)
                            dve.reg_add(more, more, 1)
                        dve.nop()
                    with dve.Else():
                        dve.nop()
                    tile(0, e * 512, e + 1)

            def combine(l):
                dve.wait_ge(*at("ld_gate_ffn", l, 32))
                for t in range(NT):
                    dve.wait_ge(*at(f"ld_y{t}", l, 32))
                    link(dve.tensor_scalar(ubuf, yk[:, t, :], small[:, 8 + t:9 + t], None, ALU.mult))
                    link(dve.scalar_tensor_tensor(ubuf, yk[:, NT + t, :], small[:, 11 + t:12 + t], ubuf, ALU.mult, ALU.add))
                    link(dve.tensor_tensor(ubuf, ubuf, gate_bc[:, min(t, 1), :], ALU.mult))
                    dve.tensor_tensor(x[:, t, :], x[:, t, :], ubuf, ALU.add).then_inc(S("x_moe"), 1)
                    dve.wait_ge(*at("x_moe", l, t + 1))

            dve.memset(small[:], 0.0).then_inc(S("small_zero"), 1)
            dve.wait_ge(S("small_zero"), 1)
            dve.wait_ge(S("ld_x"), 32)
            norm_attn(0)
            for j in range(4):
                add_bias(0, j)
            cols(0)
            hT_even(0)
            lam0 = 0.8 - 0.6 * float(np.exp(-0.3))
            for i in range(2):
                link(dve.tensor_tensor(lamv[:, 2 * i, :], lamv[:, 2 * i, :], lamv[:, 2 * i + 1, :], ALU.mult))
                link(dve.tensor_reduce(small[:, i:i + 1], lamv[:, 2 * i, :], X, ALU.add))
            dve.tensor_scalar(gsub[:], gsub[:], 1.0 - lam0, None, ALU.mult).then_inc(S("lam_dots"), 1)
            dve.wait_ge(S("lam_exp"), 1)
            link(dve.tensor_tensor(small[:, 4:5], small[:, 3:4], small[:, 2:3], ALU.subtract))
            link(dve.tensor_scalar(small[:, 4:5], small[:, 4:5], -lam0, None, ALU.add))
            for j in range(4, 12):
                add_bias(0, j)
            qk_norm_rope(0)
            qk_even(0)
            attention(0)
            oT_even(0)
            add_attn(0)
            norm_ffn(0)
            route(0)
            experts(0)
            combine(0)
            norm_attn(1)
            cols(1)
            hT_even(1)
            qk_norm_rope(1)
            qk_even(1)
            attention(1)
            oT_even(1)
            add_attn(1)
            norm_ffn(1)
            route(1)
            experts(1)
            combine(1)
            dve.wait_ge(S("sq_final"), NT)
            rstd(NT, 1.0 / D)
            dve.wait_ge(S("ld_gf"), 16)
            for t in range(NT):
                dve.scalar_tensor_tensor(yk[:, t, :], x[:, t, :], rs[:, t:t + 1], ubuf, ALU.mult, ALU.mult).then_inc(S("y_ready"), 1)

        @block.scalar
        def _(act):
            def squares(tag, dst, before):
                for t in range(NT):
                    act.wait_ge(*before(t))
                    act.activation(dst(t), x[:, t, :], ACT.Square, accum_out=ss[:, t:t + 1]).then_inc(S(f"sq_{tag}"), 1)

            roots = [0]

            def root(n):
                roots[0] += 1
                act.wait_ge(S("var_ready"), roots[0])
                act.activation(rs[:, 0:n], rs[:, 0:n], ACT.Sqrt).then_inc(S("std_ready"), 1)

            def hT_odd(l):
                act.wait_ge(S("a1_ready" if l == 0 else "a1_ready_b"), 1)
                for g in range(1, 6, 2):
                    t = g // 2
                    vec = min(t, 1)
                    act.wait_ge(*at("xn_turned", l, g + 1))
                    for c in range(4):
                        ins = act.activation(hT[:, 4 + c, P * t:P * (t + 1)], PS[:, 1, P * c:P * (c + 1)], ACT.Identity,
                                             scale=a1[:, vec, 4 + c:5 + c], bias=colp[:, vec, 0, 4 + c:5 + c])
                    ins.then_inc(S("hT_act"), 1)

            def take_qkv(l):
                for j in range(3 if l == 0 else 6):
                    for t in range(NT):
                        act.wait_ge(*at("qkv_done", l, NT * j + t + 1))
                        if j < 2 and l == 0:
                            ins = act.copy(q[:, t, 512 * j:512 * (j + 1)].rearrange("p (r f d) -> p f r d", r=4, f=2),
                                           PS[:, 2 + t, :].rearrange("p (f r d) -> p f r d", f=2, r=4))
                        elif j < 2:
                            ins = act.copy(q[:, t, 512 * j:512 * (j + 1)], PS[:, 2 + t, :])
                        elif l == 0:
                            act.copy(k_[:, t, 0:256], PS[:, 2 + t, 0:256])
                            ins = act.copy(v[:, t, 0:256], PS[:, 2 + t, 256:512])
                        elif j < 4:
                            ins = act.copy(k_[:, t, 512 * (j - 2):512 * (j - 1)], PS[:, 2 + t, :])
                        else:
                            ins = act.copy(v[:, t, 512 * (j - 4):512 * (j - 3)], PS[:, 2 + t, :])
                        ins.then_inc(S("qkv_copied"), 1)

            def qk_odd(l):
                for n, (what, b, a, cnt) in enumerate(qk_groups(l)):
                    if n % 2 == 1:
                        act.wait_ge(*at("qk_turned", l, n + 1))
                        src = PS[:, 1, 0:P * cnt].rearrange("p (c n) -> p c n", c=cnt)
                        act.copy((kT if what == "k" else qT)[:, a:a + cnt, P * b:P * (b + 1)], src).then_inc(S("qkT_act"), 1)

            def exps(l, i):
                t, pr = steps[i]
                nk = P * len(blocks_of(t))
                act.wait_ge(*at("nm_ready", l, i + 1))
                if i >= 2:
                    act.wait_ge(*at("p_turned", l, i - 1))
                    act.wait_ge(*at("o_copied", l, i - 1))
                for m in range(2):
                    ins = act.activation(pr_[:, i % 2, m, 0:nk], PS[:, 2 * (i % 2) + m, 0:nk], ACT.Exp,
                                         bias=nm[:, i % 2, m:m + 1], scale=0.125, accum_out=sm[:, i % 2, m:m + 1])
                ins.then_inc(S("p_ready"), 1)

            def take_pT(l, i):
                t, pr = steps[i]
                nk = P * len(blocks_of(t))
                m = 1 if l == 0 else 0
                act.wait_ge(*at("p_turned", l, i + 1))
                act.copy(ptt[:, m, 0:nk], PS[:, 4 + m, 0:nk]).then_inc(S("pT_act"), 1)

            def attention(l):
                for i in range(len(steps) + 1):
                    if i < len(steps):
                        exps(l, i)
                    if i:
                        take_pT(l, i - 1)

            def oT_odd(l):
                act.wait_ge(*at("state_out", l, 32))
                for g in range(1, 6, 2):
                    act.wait_ge(*at("o_turned", l, g + 1))
                    act.copy(oT[:, 4:8, P * (g // 2):P * (g // 2 + 1)],
                             PS[:, 1, :].rearrange("p (c n) -> p c n", c=4)).then_inc(S("oT_act"), 1)

            def route(l):
                for t in range(NT):
                    act.wait_ge(*at("hr_turned", l, 2 * t + 2))
                    if t:
                        act.wait_ge(*at("logits", l, t))
                    act.copy(hTr[:, 1, :], PS[:, 1, :]).then_inc(S("hr_act"), 1)
                act.wait_ge(*at("lg_ready", l, 1))
                act.activation(R(48, 48), R(48, 48), ACT.Sigmoid).then_inc(S("sig_ready"), 1)

            def experts(l):
                act.wait_ge(*at("nx_ready", l, 1))
                more = act.alloc_register(f"act_more{l}")
                act.reg_mov(more, 0)
                act.copy(ss[0:1, 20:21], cf[0:1, 0:1]).then_inc(S("y_main"), 1)
                act.copy(ss[0:1, 21:22], cf[0:1, 0:1]).then_inc(tile_sem("y_more", l), 1)

                def tile(b, col, nth):
                    B, tag = 4 * b, "main" if b == 0 else "more"
                    act.wait_ge(*at(f"gu_{tag}", l, nth))
                    act.activation(sg[:, b, :], PS[:, B + 1, 0:256], ACT.Silu).then_inc(tile_sem(f"silu_{tag}", l), 1)
                    act.wait_ge(*at(f"down_{tag}", l, nth))
                    act.activation(xg[:, bass.ds(col, 512)], PS[:, B + 3, :], ACT.Copy).then_inc(tile_sem(f"y_{tag}", l), 1)

                with act.Fori(0, E) as e:
                    nx = act.value_load(nxi[0:1, bass.ds(e, 1)], min_val=0, max_val=5)
                    with act.If(nx > 0):
                        with act.Fori(0, nx):
                            reg = act.snap(more)
                            tile(1, (reg + E) * 512, reg + 1)
                            act.reg_add(more, more, 1)
                        act.nop()
                    with act.Else():
                        act.nop()
                    tile(0, e * 512, e + 1)
                act.copy(ss[0:1, 22:23], cf[0:1, 0:1]).then_inc(S("tiles_done"), 1)

            act.wait_ge(S("ld_c"), 32)
            act.wait_ge(S("cs_zero"), 1)
            act.activation(cs[:, :, 0:2], cvec[:].rearrange("p v k -> p k v"), ACT.Silu).then_inc(S("cs_ready"), 1)
            act.wait_ge(S("work_zero"), 1)
            squares("attn", lambda t: k_[:, t, :], lambda t: (S("ld_x"), 32))
            root(NT)
            hT_odd(0)
            act.wait_ge(S("lam_dots"), 1)
            act.activation(small[:, 2:4], small[:, 0:2], ACT.Exp).then_inc(S("lam_exp"), 1)
            for l in range(2):
                if l == 1:
                    squares("attn", lambda t: k_[:, t, :], lambda t: at("x_moe", 0, NT))
                    root(NT)
                    hT_odd(1)
                take_qkv(l)
                if l == 0:
                    for t in range(NT):
                        root(20)
                qk_odd(l)
                attention(l)
                if l == 1:
                    for t in range(NT):
                        root(8)
                oT_odd(l)
                squares("ffn", lambda t: junk[t], lambda t: at("x_attn", l, NT + t + 1))
                root(NT)
                route(l)
                experts(l)
            squares("final", lambda t: yk[:, 3 + t, :], lambda t: at("x_moe", 1, t + 1))
            root(NT)


_INS = ['x_prompt', 'x_sample', 'cache_k_a', 'cache_v_a', 'cache_k_b', 'cache_v_b', 'c', 'c_ctx', 'w_mod', 'b_mod',
        'g_attn', 'g_ffn', 'w_qkv_a', 'w_o_a', 'g_q_a', 'g_k_a', 'w_qkv_b', 'w_o_b', 'lam_q1', 'lam_k1', 'lam_q2',
        'lam_k2', 'g_sub_b', 'w_router', 'b_router', 'w_gate', 'w_up', 'w_down', 'g_final']
_OUTS = [("y_prompt", (128, 1024)), ("y_sample", (256, 1024)), ("state_k0", (128, 256)), ("state_v0", (128, 256)),
         ("state_k1", (128, 1024)), ("state_v1", (128, 1024))]


def kernel(**inputs):
    import concourse.bacc as _bacc
    from concourse.bass_utils import run_bass_kernel_spmd as _run

    nc = _bacc.Bacc("TRN2", target_bir_lowering=False, num_devices=1)
    arrays, tensors = {}, {}
    cf, ci = shape_constants()
    for name, a in [(n, np.ascontiguousarray(inputs[n])) for n in _INS] + [("consts", cf), ("iconsts", ci)]:
        arrays[f"in_{name}_dram"] = a
        tensors[name] = nc.dram_tensor(f"in_{name}_dram", a.shape, mybir.dt.from_np(a.dtype), kind="ExternalInput").ap()
    for name, shape in _OUTS:
        tensors[name] = nc.dram_tensor(f"out_{name}_dram", shape, F32, kind="ExternalOutput").ap()
    hybrid_step_kernel(nc, tensors)
    r = _run(nc, [arrays], core_ids=[0])
    y_p, y_s, k_a, v_a, k_b, v_b = (r.results[0][f"out_{n}_dram"] for n, _ in _OUTS)
    return (y_p.reshape(1, 128, 1024), y_s.reshape(1, 256, 1024), k_a.reshape(1, 1, 128, 4, 64),
            v_a.reshape(1, 1, 128, 4, 64), k_b.reshape(1, 1, 128, 8, 2, 64), v_b.reshape(1, 1, 128, 8, 128))
```

```python
from contextlib import ExitStack

import numpy as np

import concourse.bass as bass
from concourse import mybir

F32 = mybir.dt.float32
I32 = mybir.dt.int32
ALU = mybir.AluOpType
ACT = mybir.ActivationFunctionType
X = mybir.AxisListType.X

P = 128
D = 1024
NT = 3
KC = D // P
E = 16
DE = 512
NG = 4
GRID_W = 64
CAP = 64
XT = (2 * NT * P - 1) // CAP
TILES = E + XT
EPS = 1e-6
SKIP = 4096
SLOT = 4096
NSLOT = 6
N_MOD = 6

C_ID, C_UP, C_ONE = 0, 128, 256
C_COS, C_SIN = 384, 512
C_HALF, C_REVE, C_REVG, C_THR = 640, 641, 657, 661
C_N = 666


def shape_constants():
    c = np.zeros((P, C_N), np.float32)
    c[:, C_ID:C_ID + P] = np.eye(P)
    c[:, C_UP:C_UP + P] = np.triu(np.ones((P, P)), 1)
    c[:, C_ONE:C_ONE + P] = 1.0
    inv = np.power(np.float32(10000.0), -np.arange(0, 32, 2, dtype=np.float32) / np.float32(32))
    for t in range(2):
        tok = np.arange(P) + P * t
        row = (tok // GRID_W).astype(np.float32)[:, None] * inv
        col = (tok % GRID_W).astype(np.float32)[:, None] * inv
        c[:, C_COS + 64 * t:C_COS + 64 * (t + 1)] = np.concatenate([np.cos(row)] * 2 + [np.cos(col)] * 2, 1)
        c[:, C_SIN + 64 * t:C_SIN + 64 * (t + 1)] = np.concatenate(
            [-np.sin(row), np.sin(row), -np.sin(col), np.sin(col)], 1)
    c[:, C_HALF] = np.arange(P) // CAP
    c[:, C_REVE:C_REVE + E] = E - np.arange(E)
    c[:, C_REVG:C_REVG + NG] = NG - np.arange(NG)
    c[:, C_THR:C_THR + 5] = CAP * np.arange(1, 6)
    i = np.zeros((P, 12 + 2 * TILES), np.int32)
    for k in range(2):
        for t in range(NT):
            i[:, 2 * (NT * k + t)] = P * t + np.arange(P)
            i[:, 2 * (NT * k + t) + 1] = NT * P * k + P * t + np.arange(P)
    i[:, 12:] = SKIP
    return c, i


def hybrid_step_kernel(nc, t_):
    with ExitStack() as ctx:
        def sb(name, shape, dt=F32):
            return ctx.enter_context(nc.sbuf_tensor(name, shape, dt))

        sems = {}

        def S(name):
            if name not in sems:
                sems[name] = ctx.enter_context(nc.semaphore(name))
            return sems[name]

        FIRST = dict(mod_ps=12, mod_sb=12, mod_stored=64, ld_cols=32, ld_gate_attn=32, ld_cache=32, xn_ready=3,
                     xn_turned=6, mod_bias=32, hT_dve=3, hT_act=3, qkv_done=9, qkv_copied=9, qk_ready=3, qk_turned=10, qkT_dve=5,
                     qkT_act=5, state_out=32, s_done=24, nm_ready=24, p_ready=24, p_turned=24, pT_act=24, pT_dve=24,
                     o_done=24, o_copied=24, o_ready=3, o_turned=6, oT_dve=3, oT_act=3, wo_done=6, wo_copied=6, x_attn=6,
                     sq_attn=3, sq_ffn=3, ld_rows=80, ld_gate_ffn=32, h_ready=3, h_stored=48, hr_turned=6, hr_dve=3,
                     hr_act=3, logits=3, lg_ready=1, sig_ready=1, oh_ready=1, ranks=1, nx_ready=1, rows_ready=1,
                     listed=96, ld_list=32, idx_ready=1, tiles_done=1, scattered=16 * E, x_moe=3, xg_main=E, y_main=E + 1, ld_y0=16, ld_y1=16, ld_y2=16, y_scaled=3)
        FIRST |= {f"{x}_main": E for x in ("xc", "x_turned", "xT", "gu", "silu", "h", "h_turned", "hT", "down")}
        FIRST |= {f"gather{r}": 16 * E // 4 for r in range(4)}

        def tile_sem(name, l):
            return S(f"{name}{l}") if name.endswith("_more") else S(name)

        def at(name, l, n):
            if name.endswith("_more"):
                return tile_sem(name, l), n
            return S(name), n + (FIRST[name] if l == 1 else 0)

        mod_d = nc.dram_tensor("mod_scratch", [2, 2, N_MOD * D], F32, kind="Internal").ap()
        y_ds = [nc.dram_tensor(f"y_scratch{l}", [4 * NT * P, 512], F32, kind="Internal").ap() for l in range(2)]
        h_ds = [nc.dram_tensor(f"h_scratch{l}", [2 * NT * P, 512], F32, kind="Internal").ap() for l in range(2)]
        list_ds = [nc.dram_tensor(f"list_scratch{l}", [CAP * TILES, 2], I32, kind="Internal").ap() for l in range(2)]

        ring = sb("ring", [P, NSLOT, SLOT])
        x = sb("x", [P, NT, D])
        gate_bc = sb("gate_bc", [P, 2, D])
        cf = sb("cf", [P, C_N])
        ci = sb("ci", [P, 12 + 2 * TILES], I32)
        modsb = sb("modsb", [P, 12, P])
        cs = sb("cs", [P, KC, 32])
        cvec = sb("cvec", [P, 2, KC])
        gcol = sb("gcol", [P, 2, KC])
        colp = sb("colp", [P, 2, 2, KC])
        a1 = sb("a1", [P, 2, KC])
        wr = sb("wr", [P, KC, E])
        br = sb("br", [P, E])
        gqk = sb("gqk", [P, 2, 64])
        rope_qk = sb("rope_qk", [P, 2, 2, 2, 64])
        gsub = sb("gsub", [P, P])
        small = sb("small", [P, 16])
        ss = sb("ss", [P, 64])
        rs = sb("rs", [P, 64])
        nm = sb("nm", [P, 2, 2])
        sm = sb("sm", [P, 4, 2])
        rsm = sb("rsm", [P, 4, 2])
        work = sb("work", [P, 19456])
        rti = sb("rti", [P, 6], I32)
        nxi = sb("nxi", [P, E + 1], I32)
        tick = sb("tick", [1, TILES])
        lst = sb("lst", [P, 2 * TILES], I32)
        gi = sb("gi", [P, 2 * TILES], I32)
        PS = ctx.enter_context(nc.psum_tensor("PS", [P, 8, 512], F32))

        ident = cf[:, C_ID:C_ID + P]
        upper = cf[:, C_UP:C_UP + P]
        ones = cf[:, C_ONE:C_ONE + P]

        W_R1, W_R2, W_R3, W_V, W_KT, W_P, W_SQ = 0, 3072, 6144, 9216, 13312, 17408, 18944
        r1 = work[:, W_R1:W_R1 + 3072]
        r2 = work[:, W_R2:W_R2 + 3072]
        r3 = work[:, W_R3:W_R3 + 3072]
        hT = r1.rearrange("p (k n) -> p k n", k=KC)
        qT = r1.rearrange("p (k n) -> p k n", k=KC)
        xn = r2.rearrange("p (t n) -> p t n", t=NT)
        q = xn
        k_ = r3.rearrange("p (t n) -> p t n", t=NT)
        oT = r3.rearrange("p (k n) -> p k n", k=KC)
        v = work[:, W_V:W_V + 4096].rearrange("p (t n) -> p t n", t=4)
        kc = gate_bc[:, 0, :]
        kT = work[:, W_KT:W_KT + 4096].rearrange("p (k n) -> p k n", k=KC)
        pr_ = work[:, W_P:W_P + 1536].rearrange("p (i m n) -> p i m n", i=2, m=2)
        gate_flat = gate_bc[:].rearrange("p a b -> p (a b)")
        ptt = gate_flat[:, 0:1536].rearrange("p (i m n) -> p i m n", i=2, m=2)
        lamv = gate_bc[:, 1, 0:256].rearrange("p (a b) -> p a b", a=4)
        sqo = work[:, W_SQ:W_SQ + 2 * P].rearrange("p (a b) -> p a b", a=2)
        sqb = work[:, W_KT:W_KT + 4096]
        tmp1 = work[:, W_P:W_P + 1024]
        tmp2 = work[:, W_P + 1024:W_P + 2048]
        hperm = r1.rearrange("p (t n) -> p t n", t=NT)
        gbc = work[:, W_V:W_V + 1024]
        junk = [work[:, W_R2 + 1024 * t:W_R2 + 1024 * (t + 1)] for t in range(NT)]
        hTr = work[:, W_V + 1024:W_V + 3072].rearrange("p (i b n) -> p i b n", i=2, b=2)
        sbc = work[:, W_KT:W_KT + 4096].rearrange("p (v m n) -> p v m n", v=2, m=2)
        xg = work[:, 0:TILES * 512]
        W_X = TILES * 512
        xc = work[:, W_X:W_X + 1024].rearrange("p (b n) -> p b n", b=2)
        xT = work[:, W_X + 1024:W_X + 2048].rearrange("p (b c n) -> p b c n", b=2, c=4)
        sg = work[:, W_X + 2048:W_X + 2560].rearrange("p (b n) -> p b n", b=2)
        hE = work[:, W_X + 2560:W_X + 3072].rearrange("p (b n) -> p b n", b=2)
        hTt = work[:, W_X + 3072:W_X + 3584].rearrange("p (b c n) -> p b c n", b=2, c=2)
        yk = work[:, 0:6144].rearrange("p (j n) -> p j n", j=6)
        ubuf = work[:, 6144:7168]
        assert W_X + 3584 <= 19456

        rt = work[:, W_V + 3072:W_V + 4096]

        def R(a, n):
            return rt[:, a:a + n]

        def plan():
            jobs, n = [], 0

            def add(kind, l, j):
                nonlocal n
                jobs.append((kind, l, j, n % NSLOT, n // NSLOT))
                n += 1
            for j in range(4):
                add("mod", 0, j)
            for j in range(3):
                add("qkv", 0, j)
            for j in range(4, 12):
                add("mod", 0, j)
            for j in range(6):
                add("mod", 1, j)
            for j in range(2):
                add("wo", 0, j)
            for j in range(6, 12):
                add("mod", 1, j)
            return jobs, n
        jobs, _ = plan()
        uses = [0] * NSLOT
        place = {}
        for kind, l, j, s, _u in jobs:
            place[(kind, l, j)] = (s, uses[s])
            uses[s] += 1
        moe_base = [list(uses)]
        for s in range(NSLOT):
            uses[s] += 8
        jobs_b = [("qkv", 1, j) for j in range(6)] + [("wo", 1, j) for j in range(2)]
        for n, (kind, l, j) in enumerate(jobs_b):
            place[(kind, l, j)] = (n % NSLOT, uses[n % NSLOT])
            uses[n % NSLOT] += 1
        moe_base.append(list(uses))

        w_ready = [S(f"w_ready{s}") for s in range(NSLOT)]

        def last_use(kind, l, j):
            return at("mod_ps", l, j + 1) if kind == "mod" else at(f"{kind}_done", l, NT * (j + 1))

        wqkv = [t_["w_qkv_a"][0], t_["w_qkv_b"][0]]
        wo = [t_["w_o_a"][0], t_["w_o_b"][0]]

        def chunk_src(w, j):
            return w.rearrange("(p k) n -> p k n", k=KC)[:, :, 512 * j:512 * (j + 1)]

        block = ctx.enter_context(nc.Block())

        @block.sync
        def _(sp):
            freed = [None] * NSLOT

            def load(kind, l, j):
                s, _ = place[(kind, l, j)]
                if freed[s]:
                    sp.wait_ge(*freed[s])
                freed[s] = last_use(kind, l, j)
                src = {"mod": t_["w_mod"][l], "qkv": wqkv[l], "wo": wo[l]}[kind]
                sp.dma_start(ring[:, s, :].rearrange("p (k n) -> p k n", k=KC), chunk_src(src, j)).then_inc(w_ready[s], 16)

            def expert(l, e, par):
                for m, w in enumerate((t_["w_gate"], t_["w_up"], t_["w_down"])):
                    s = 3 * par + m
                    src = w[l, bass.ds(e, 1)]
                    if m < 2:
                        pat = dict(dst=ring[:, s, :], src=src.rearrange("a (p k) n -> (a p) (k n)", k=KC))
                    else:
                        pat = dict(dst=ring[:, s, :].rearrange("p (q n) -> p q n", q=4), src=src.rearrange("a (q p) n -> p (a q) n", p=P))
                    yield m, s, pat

            def experts(l):
                for par in range(2):
                    for m, s, a in expert(l, par, par):
                        sp.wait_ge(*freed[s])
                        sp.dma_start(a["dst"], a["src"]).then_inc(w_ready[s], 16)
                with sp.Fori(1, E // 2) as i:
                    for par in range(2):
                        for m, s, a in expert(l, 2 * i + par, par):
                            sp.wait_ge(*at("gu_main" if m < 2 else "down_main", l, 2 * i + (par - 1)))
                            sp.dma_start(a["dst"], a["src"]).then_inc(w_ready[s], 16)
                for s in range(NSLOT):
                    freed[s] = at("gu_main" if s % 3 < 2 else "down_main", l, E - 1 + s // 3)

            sp.dma_start(cvec[:, 0, :], t_["c_ctx"].rearrange("(p k) -> p k", k=KC)).then_inc(S("ld_c"), 16)
            sp.dma_start(cvec[:, 1, :], t_["c"][0].rearrange("(p k) -> p k", k=KC)).then_inc(S("ld_c"), 16)
            sp.dma_start(x[:, 0, :], t_["x_prompt"][0]).then_inc(S("ld_x"), 16)
            sp.dma_start(x[:, 1:3, :], t_["x_sample"][0].rearrange("(t p) n -> p t n", p=P)).then_inc(S("ld_x"), 16)
            sp.dma_start(cf[:], t_["consts"]).then_inc(S("ld_const"), 16)
            sp.dma_start(ci[:], t_["iconsts"]).then_inc(S("ld_const"), 16)
            for n, (kind, l, j, _s, _u) in enumerate(jobs):
                if n == NSLOT:
                    sp.wait_ge(S("ld_cols"), 32)
                load(kind, l, j)
            experts(0)
            for n, (kind, l, j) in enumerate(jobs_b):
                if n == 2:
                    sp.wait_ge(S("ld_y2"), 16)
                load(kind, l, j)
            experts(1)

        @block.gpsimd
        def _(pool):
            def bc(ap1d):
                return ap1d.partition_broadcast(P)

            pool.memset(cs[:], 0.0).then_inc(S("cs_zero"), 1)
            for l in range(2):
                pool.dma_start(mod_d[l], t_["b_mod"][l].partition_broadcast(2)).then_inc(S("mod_bias"), 32)
            pool.memset(work[:, W_R3:W_X], 0.0).then_inc(S("work_zero"), 1)
            for l in range(2):
                pool.dma_start(gcol[:, l, :], t_["g_attn"][l].rearrange("(p k) -> p k", k=KC)).then_inc(S("ld_par"), 16)
            pool.dma_start(gqk[:, 0, :], bc(t_["g_q_a"][0])).then_inc(S("ld_par"), 16)
            pool.dma_start(gqk[:, 1, :], bc(t_["g_k_a"][0])).then_inc(S("ld_par"), 16)
            pool.dma_start(gsub[:], bc(t_["g_sub_b"][0])).then_inc(S("ld_par"), 16)
            for i, n in enumerate(("lam_q1", "lam_k1", "lam_q2", "lam_k2")):
                pool.dma_start(lamv[:, i, :], bc(t_[n][0])).then_inc(S("ld_par"), 16)
            pool.dma_start(wr[:], t_["w_router"].rearrange("(p k) e -> p k e", k=KC)).then_inc(S("ld_par"), 16)
            pool.dma_start(br[:], bc(t_["b_router"])).then_inc(S("ld_par"), 16)
            pool.wait_ge(S("ld_const"), 32)
            for l in range(2):
                pool.dma_start(list_ds[l].rearrange("(p c) w -> p (c w)", p=CAP), ci[0:CAP, 12:]).then_inc(S("list_init"), 16)

            def mod_store(l, part):
                lo, hi = (0, 4) if part == 0 else (4, 12)
                pool.wait_ge(S("mod_bias"), 64)
                pool.wait_ge(*at("mod_sb", l, hi))
                for vec in range(2):
                    pool.dma_start(mod_d[l, vec].rearrange("(n g c) -> g n c", g=4, c=P)[:, lo:hi, :],
                                   modsb[vec:P:32, lo:hi, :], accum_op=ALU.add).then_inc(S("mod_stored"), 16)

            def mod_cols(l):
                pool.wait_ge(*at("mod_stored", l, 32 if l == 0 else 64))
                for vec in range(2):
                    pool.dma_start(colp[:, vec, :, :],
                                   mod_d[l, vec, 0:2 * D].rearrange("(m p k) -> p m k", m=2, k=KC)).then_inc(S("ld_cols"), 16)

            def row_bc(dst, l, vec, m, sem):
                pool.dma_start(dst, bc(mod_d[l, vec, m * D:(m + 1) * D])).then_inc(S(sem), 16)

            def cache(l):
                pool.wait_ge(S("work_zero"), 1)
                kk, vv = (t_["cache_k_a"], t_["cache_v_a"]) if l == 0 else (t_["cache_k_b"], t_["cache_v_b"])
                n = 256 if l == 0 else 1024
                fk = "p a b -> p (a b)" if l == 0 else "p a b c -> p (a b c)"
                pool.dma_start(kc[:, 0:n], kk[0, 0].rearrange(fk)).then_inc(S("ld_cache"), 16)
                pool.dma_start(v[:, 3, 0:n], vv[0, 0].rearrange("p a b -> p (a b)")).then_inc(S("ld_cache"), 16)

            def states(l):
                n = 256 if l == 0 else 1024
                pool.wait_ge(*at("qkv_copied", l, 9 if l == 0 else 18))
                pool.dma_start(t_[f"state_v{l}"], v[:, 0, 0:n]).then_inc(S("state_out"), 16)
                if l == 0:
                    pool.wait_ge(*at("qk_ready", 0, 1))
                pool.dma_start(t_[f"state_k{l}"], k_[:, 0, 0:n]).then_inc(S("state_out"), 16)

            def ffn_rows(l):
                pool.wait_ge(*at("o_done", l, 24))
                for vec in range(2):
                    row_bc(gate_bc[:, vec, :], l, vec, 2, "ld_gate_attn")
                pool.dma_start(gbc, bc(t_["g_ffn"][l])).then_inc(S("ld_rows"), 16)
                for vec in range(2):
                    row_bc(sbc[:, vec, 0, :], l, vec, 3, "ld_rows")
                    row_bc(sbc[:, vec, 1, :], l, vec, 4, "ld_rows")

            def moe_dmas(l):
                for t in range(NT):
                    pool.wait_ge(*at("h_ready", l, t + 1))
                    pool.dma_start(h_ds[l].rearrange("(t p h) n -> t p (h n)", t=NT, h=2)[t], hperm[:, t, :]).then_inc(S("h_stored"), 16)
                pool.wait_ge(*at("rows_ready", l, 1))
                pool.wait_ge(S("list_init"), 32)
                for k in range(2 * NT):
                    pool.indirect_dma_start(list_ds[l], bass.IndirectOffsetOnAxis(ap=rti[:, k:k + 1], axis=0),
                                            ci[:, 2 * k:2 * k + 2], None).then_inc(S("listed"), 16)
                pool.wait_ge(*at("listed", l, 96))
                for half in range(2):
                    pool.dma_start(lst[CAP * half:CAP * (half + 1), :],
                                   list_ds[l].rearrange("(p c) w -> p (c w)", p=CAP)).then_inc(S("ld_list"), 16)
                pool.wait_ge(*at("h_stored", l, 16 * NT))
                pool.wait_ge(*at("idx_ready", l, 1))
                GR = 4

                def gather(c, sem):
                    pool.indirect_dma_start(xg[:, 512 * c:512 * (c + 1)], None, h_ds[l],
                                            bass.IndirectOffsetOnAxis(ap=gi[:, 2 * c:2 * c + 1], axis=0),
                                            bounds_check=2 * NT * P - 1, oob_is_err=False).then_inc(sem, 16)

                def scatter(c, sem):
                    pool.indirect_dma_start(y_ds[l], bass.IndirectOffsetOnAxis(ap=gi[:, 2 * c + 1:2 * c + 2], axis=0),
                                            xg[:, 512 * c:512 * (c + 1)], None,
                                            bounds_check=4 * NT * P - 1, oob_is_err=False).then_inc(sem, 16)

                def gathered(e):
                    pool.wait_ge(*at(f"gather{e % GR}", l, 16 * (e // GR + 1)))
                    pool.memset(tick[0:1, e:e + 1], 0.0).then_inc(S("xg_main"), 1)

                more = pool.value_load(nxi[0:1, E:E + 1], min_val=0, max_val=XT)

                def for_each_more(move, sem):
                    for n in range(XT):
                        with pool.If(more > n):
                            move(E + n, sem)
                            pool.nop()
                        with pool.Else():
                            pool.nop()
                    with pool.If(more > 0):
                        pool.wait_ge(sem, more * 16)
                        pool.nop()
                    with pool.Else():
                        pool.nop()

                gather(0, S("gather0"))
                gather(1, S("gather1"))
                for_each_more(gather, tile_sem("gather_more", l))
                pool.memset(tick[0:1, E:E + 1], 0.0).then_inc(tile_sem("xg_more", l), 1)
                for e in range(2, E):
                    gather(e, S(f"gather{e % GR}"))
                    gathered(e - 2)
                gathered(E - 2)
                gathered(E - 1)
                for vec in range(2):
                    row_bc(gate_bc[:, vec, :], l, vec, 5, "ld_gate_ffn")
                if l == 0:
                    mod_store(1, 1)
                    pool.wait_ge(*at("hT_act", 0, 3))
                    pool.wait_ge(*at("hT_dve", 0, 3))
                    mod_cols(1)
                for e in range(E):
                    pool.wait_ge(*at("y_main", l, e + 2))
                    scatter(e, S("scattered"))
                pool.wait_ge(*at("tiles_done", l, 1))
                for_each_more(scatter, tile_sem("scattered_more", l))
                pool.wait_ge(*at("scattered", l, 16 * E))
                for t in range(NT):
                    pool.dma_start(yk[:, t::NT, :].rearrange("p k (h n) -> p k h n", h=2),
                                   y_ds[l].rearrange("(k t p h) n -> t p k h n", k=2, p=P, h=2)[t]).then_inc(S(f"ld_y{t}"), 16)

            mod_store(0, 0)
            mod_cols(0)
            cache(0)
            mod_store(0, 1)
            states(0)
            mod_store(1, 0)
            pool.wait_ge(*at("mod_stored", 0, 64))
            ffn_rows(0)
            moe_dmas(0)
            pool.wait_ge(*at("x_moe", 0, 3))
            cache(1)
            states(1)
            ffn_rows(1)
            moe_dmas(1)
            pool.dma_start(ubuf, bc(t_["g_final"])).then_inc(S("ld_gf"), 16)
            for t in range(NT):
                pool.wait_ge(S("y_ready"), t + 1)
                dst = t_["y_prompt"] if t == 0 else t_["y_sample"][P * (t - 1):P * t, :]
                pool.dma_start(dst, yk[:, t, :]).then_inc(S("y_out"), 16)
            pool.wait_ge(S("y_out"), 16 * NT)

        steps = [(t, pr) for t in range(NT) for pr in range(8)]

        MOD_BEFORE = [(0, 4), (0, 5), (0, 6)]
        MOD_WITHIN = {i: slot for i, slot in zip((0, 2, 4, 6, 8, 10, 12, 14, 16, 19, 22),
                                                 [(0, j) for j in range(7, 12)] + [(1, j) for j in range(6)])}
        MOD_AFTER = [(1, j) for j in range(6, 12)]

        SUB_AT = (11, 19, 26)

        def pT_bank(l, i, m):
            return 4 + m if l == 0 else 4 + i % 2

        def blocks_of(t):
            return [0] if t == 0 else [1, 2, 3]

        def kcols(t):
            return slice(0, P) if t == 0 else slice(P, 4 * P)

        QK_BANK = (1, 3, 5, 6)

        def qk_groups(l):
            npair = 2 if l == 0 else 8
            out = []
            for b in (3, 0, 1, 2):
                for a in range(0, npair, 4):
                    out.append(("k", b, a, min(4, npair - a)))
                if b < 3:
                    for a in (0, 4):
                        out.append(("q", b, a, 4))
            return out

        @block.tensor
        def _(pe):
            def slot_ready(kind, l, j):
                s, u = place[(kind, l, j)]
                pe.wait_ge(w_ready[s], 16 * (u + 1))
                return s

            nmod = [0]

            def mod_slot(l, j):
                s = slot_ready("mod", l, j)
                if l == 0 and j == 0:
                    pe.wait_ge(S("cs_ready"), 1)
                if j or l:
                    pe.wait_ge(*at("mod_sb", l, j))
                for k in range(KC):
                    for g in range(4):
                        mm = pe.matmul(PS[32 * g:32 * g + 32, 7, 0:P], cs[:, k, :],
                                       ring[:, s, 512 * k + P * g:512 * k + P * (g + 1)], start=(k == 0), stop=(k == KC - 1))
                mm.then_inc(S("mod_ps"), 1)

            def norm_transposes(l, t):
                pe.wait_ge(*at("xn_ready", l, t + 1))
                for half in range(2):
                    g = 2 * t + half
                    for c in range(4):
                        tr = pe.transpose(PS[:, g, P * c:P * (c + 1)], xn[:, t, 4 * half + c::KC], ident)
                    tr.then_inc(S("xn_turned"), 1)

            def project(l, kind, nslots, lhs, ready, then=None):
                for j in range(nslots):
                    s = slot_ready(kind, l, j)
                    for t in range(NT):
                        n = NT * j + t
                        if j == 0:
                            ready(t)
                        else:
                            pe.wait_ge(*at(f"{kind}_copied", l, n - NT + 1))
                        for k in range(KC):
                            mm = pe.matmul(PS[:, 2 * t, :], lhs[:, k, P * t:P * (t + 1)], ring[:, s, 512 * k:512 * (k + 1)],
                                           start=(k == 0), stop=(k == KC - 1))
                        mm.then_inc(S(f"{kind}_done"), 1)
                        if then and j == nslots - 1 and t:
                            then(t - 1)

            def hT_ready(l):
                def f(t):
                    if l == 1:
                        for u in ((0, 1), (2,), ())[t]:
                            norm_transposes(1, u)
                    pe.wait_ge(*at("hT_dve", l, t + 1))
                    pe.wait_ge(*at("hT_act", l, t + 1))
                return f

            def qk_transposes(l):
                pe.wait_ge(*at("ld_cache", l, 32))
                for n, (what, b, a, cnt) in enumerate(qk_groups(l)):
                    if b == 0 and l == 1:
                        pe.wait_ge(*at("qkv_copied", 1, 12))
                    elif b < 3 and what == "q" and l == 0:
                        pe.wait_ge(S("q_ready"), b + 1)
                    elif b < 3:
                        pe.wait_ge(*at("qk_ready", l, b + 1 - l))
                    if n >= 4:
                        pe.wait_ge(*at("qkT_dve" if n % 2 == 0 else "qkT_act", l, n // 2 - 1))
                    for c in range(cnt):
                        i = a + c
                        if what == "k":
                            src = kc[:, P * i:P * (i + 1)] if b == 3 else k_[:, b, P * i:P * (i + 1)]
                        else:
                            src = q[:, b, P * i:P * (i + 1)]
                        tr = pe.transpose(PS[:, QK_BANK[n % 4], P * c:P * (c + 1)], src, ident)
                    tr.then_inc(S("qk_turned"), 1)

            def scores(l, i):
                t, pr = steps[i]
                nk = P * len(blocks_of(t))
                if i == 0:
                    g = len(qk_groups(l))
                    pe.wait_ge(*at("qkT_dve", l, (g + 1) // 2))
                    pe.wait_ge(*at("qkT_act", l, g // 2))
                    pe.wait_ge(*at("qkv_copied", l, 9 if l == 0 else 18))
                if i >= 2:
                    pe.wait_ge(*at("p_ready", l, i - 1))
                for m in range(2):
                    mm = pe.matmul(PS[:, 2 * (i % 2) + m, 0:nk], qT[64 * m:64 * m + 64, pr, P * t:P * (t + 1)],
                                   kT[64 * m:64 * m + 64, pr // 4 if l == 0 else pr, kcols(t)], start=True, stop=True)
                mm.then_inc(S("s_done"), 1)

            def turn_p(l, i):
                t, pr = steps[i]
                pe.wait_ge(*(at("p_ready", 0, i + 1) if l == 0 else (S("a_ready"), i + 1)))
                if l == 0 and i:
                    pe.wait_ge(*at("pT_act", l, i))
                    pe.wait_ge(*at("pT_dve", l, i))
                elif l:
                    pe.wait_ge(*at("pT_act", l, max(i - 1, 0)))
                for m in range(2 if l == 0 else 1):
                    for c in range(len(blocks_of(t))):
                        tr = pe.transpose(PS[:, pT_bank(l, i, m), P * c:P * (c + 1)], pr_[:, i % 2, m, P * c:P * (c + 1)], ident)
                tr.then_inc(S("p_turned"), 1)

            def times_v(l, i):
                t, pr = steps[i]
                bl = blocks_of(t)
                pe.wait_ge(*at("pT_act", l, i + 1))
                if l == 0:
                    pe.wait_ge(*at("pT_dve", l, i + 1))
                if i or l:
                    pe.wait_ge(*at("o_copied", l, i))
                for m in range(2 if l == 0 else 1):
                    for c, b in enumerate(bl):
                        if l == 0:
                            g = 2 * (pr // 4) + m
                            out, vals = PS[:, 6, 64 * m:64 * m + 64], v[:, b, 64 * g:64 * g + 64]
                        else:
                            out, vals = PS[:, 6, 0:P], v[:, b, P * pr:P * (pr + 1)]
                        mm = pe.matmul(out, ptt[:, i % 2, m, P * c:P * (c + 1)], vals, start=(c == 0), stop=(c == len(bl) - 1))
                mm.then_inc(S("o_done"), 1)

            def attention(l):
                n = len(steps)
                for i in range(n + 3):
                    if 2 <= i < n + 2:
                        turn_p(l, i - 2)
                    if i < n:
                        scores(l, i)
                    if l == 0 and i in MOD_WITHIN:
                        mod_slot(*MOD_WITHIN[i])
                    if i >= 3:
                        times_v(l, i - 3)

            def o_transposes(l):
                for g in range(6):
                    t, half = g // 2, g % 2
                    pe.wait_ge(*(at("o_copied", 0, 8 * (t + 1)) if l == 0 else (S("o_ready"), t + 1)))
                    for c in range(4):
                        tr = pe.transpose(PS[:, g, P * c:P * (c + 1)], q[:, t, 4 * half + c::KC], ident)
                    tr.then_inc(S("o_turned"), 1)

            def oT_ready(l):
                def f(t):
                    pe.wait_ge(*at("oT_dve", l, t + 1))
                    pe.wait_ge(*at("oT_act", l, t + 1))
                return f

            def logits(l, t):
                pe.wait_ge(*at("h_ready", l, t + 1))
                B = (1, 3) if t % 2 == 0 else (5, 7)
                if t == 2:
                    pe.wait_ge(*at("hr_dve", l, 1))
                    pe.wait_ge(*at("hr_act", l, 1))
                for half in range(2):
                    for c in range(4):
                        tr = pe.transpose(PS[:, B[half], P * c:P * (c + 1)],
                                          hperm[:, t, P * (4 * half + c):P * (4 * half + c + 1)], ident)
                    tr.then_inc(S("hr_turned"), 1)
                pe.wait_ge(*at("hr_dve", l, t + 1))
                pe.wait_ge(*at("hr_act", l, t + 1))
                for k in range(KC):
                    mm = pe.matmul(PS[:, 6, E * t:E * (t + 1)], hTr[:, t % 2, k // 4, P * (k % 4):P * (k % 4 + 1)], wr[:, k, :],
                                   start=(k == 0), stop=(k == KC - 1))
                mm.then_inc(S("logits"), 1)

            def ranks(l):
                pe.wait_ge(*at("oh_ready", l, 1))
                for t in range(NT):
                    for u in range(t + 1):
                        mm = pe.matmul(PS[:, 2, E * t:E * (t + 1)], upper if u == t else ones, R(0, 48)[:, E * u:E * (u + 1)],
                                       start=(u == 0), stop=(u == t))
                for u in range(NT):
                    mm = pe.matmul(PS[:, 2, 64:64 + E], ones, R(0, 48)[:, E * u:E * (u + 1)], start=(u == 0), stop=(u == NT - 1))
                mm.then_inc(S("ranks"), 1)

            def experts(l):
                base = moe_base[l]

                def tag(b):
                    return "more" if b else "main"

                def turn_x(b, nth):
                    pe.wait_ge(*at(f"xc_{tag(b)}", l, nth))
                    for c in range(4):
                        tr = pe.transpose(PS[:, 4 * b, P * c:P * (c + 1)], xc[:, b, P * c:P * (c + 1)], ident)
                    tr.then_inc(tile_sem(f"x_turned_{tag(b)}", l), 1)

                def weights(m, i, par):
                    pe.wait_ge(w_ready[3 * par + m], 16 * (base[3 * par + m] + i + 1))

                def gate_up(b, i, par, nth):
                    pe.wait_ge(*at(f"xT_{tag(b)}", l, nth))
                    weights(0, i, par)
                    weights(1, i, par)
                    s = 3 * par
                    for k in range(KC):
                        for g in range(2):
                            mm = pe.matmul(PS[64 * g:64 * g + 64, 4 * b + 1, :], xT[:, b, k % 4, 64 * (k // 4):64 * (k // 4) + 64],
                                           ring[:, s:s + 2, 512 * k + 256 * g:512 * k + 256 * (g + 1)],
                                           start=(k == 0), stop=(k == KC - 1))
                    mm.then_inc(tile_sem(f"gu_{tag(b)}", l), 1)

                def turn_h(b, nth):
                    pe.wait_ge(*at(f"h_{tag(b)}", l, nth))
                    for c in range(2):
                        tr = pe.transpose(PS[:, 4 * b + 2, P * c:P * (c + 1)], hE[:, b, P * c:P * (c + 1)], ident)
                    tr.then_inc(tile_sem(f"h_turned_{tag(b)}", l), 1)

                def down(b, i, par, nth):
                    weights(2, i, par)
                    pe.wait_ge(*at(f"hT_{tag(b)}", l, nth))
                    pe.wait_ge(*at(f"y_{tag(b)}", l, nth))
                    s = 3 * par + 2
                    for f in range(4):
                        for g in range(2):
                            mm = pe.matmul(PS[64 * g:64 * g + 64, 4 * b + 3, :], hTt[:, b, f % 2, 64 * (f // 2):64 * (f // 2) + 64],
                                           ring[:, s, 1024 * f + 512 * g:1024 * f + 512 * (g + 1)], start=(f == 0), stop=(f == 3))
                    mm.then_inc(tile_sem(f"down_{tag(b)}", l), 1)

                pe.wait_ge(*at("nx_ready", l, 1))
                more = pe.alloc_register(f"pe_more{l}")
                pe.reg_mov(more, 0)

                def expert(i, par, first=False, last=False):
                    e = 2 * i + par
                    nx = pe.value_load(nxi[0:1, bass.ds(e, 1)], min_val=0, max_val=5)
                    with pe.If(nx > 0):
                        with pe.Fori(0, nx):
                            pe.reg_add(more, more, 1)
                            nth = pe.snap(more)
                            turn_x(1, nth)
                            gate_up(1, i, par, nth)
                            turn_h(1, nth)
                            down(1, i, par, nth)
                        pe.nop()
                    with pe.Else():
                        pe.nop()
                    gate_up(0, i, par, e + 1)
                    if not last:
                        turn_x(0, e + 2)
                    if not first:
                        down(0, i if par else i - 1, 1 - par, e)
                    turn_h(0, e + 1)

                turn_x(0, 1)
                expert(0, 0, first=True)
                expert(0, 1)
                with pe.Fori(1, E // 2 - 1) as i:
                    expert(i, 0)
                    expert(i, 1)
                expert(E // 2 - 1, 0)
                expert(E // 2 - 1, 1, last=True)
                down(0, E // 2 - 1, 1, E)

            for l in range(2):
                if l == 0:
                    mod_slot(0, 0)
                    mod_slot(0, 1)
                    pe.wait_ge(S("ld_const"), 32)
                    for t in range(NT):
                        norm_transposes(0, t)
                    mod_slot(0, 2)
                    mod_slot(0, 3)
                project(l, "qkv", 3 if l == 0 else 6, hT, hT_ready(l))
                if l == 0:
                    for slot in MOD_BEFORE:
                        mod_slot(*slot)
                qk_transposes(l)
                attention(l)
                o_transposes(l)
                project(l, "wo", 2, oT, oT_ready(l), lambda t, l=l: logits(l, t))
                logits(l, 2)
                ranks(l)
                if l == 0:
                    for slot in MOD_AFTER:
                        mod_slot(*slot)
                experts(l)

        @block.vector
        def _(dve):
            chain = [0]

            def link(ins):
                chain[0] += 1
                ins.then_inc(S("dve_chain"), 1)
                dve.wait_ge(S("dve_chain"), chain[0])

            def done(ins, sem, n):
                sem = S(sem) if isinstance(sem, str) else sem
                ins.then_inc(sem, 1)
                dve.wait_ge(sem, n)

            roots = [0]

            def rstd(n, inv_n, o=0):
                roots[0] += 1
                dve.tensor_scalar(rs[:, o:o + n], ss[:, o:o + n], inv_n, EPS, ALU.mult, ALU.add).then_inc(S("var_ready"), 1)
                dve.wait_ge(S("std_ready"), roots[0])
                link(dve.reciprocal(rs[:, o:o + n], rs[:, o:o + n]))

            def norm_attn(l, t):
                dve.wait_ge(*at("sq_attn", l, t + 1))
                rstd(1, 1.0 / D, t)
                dve.tensor_scalar(xn[:, t, :], x[:, t, :], rs[:, t:t + 1], None, ALU.mult).then_inc(S("xn_ready"), 1)

            def cols(l):
                dve.wait_ge(*at("ld_cols", l, 32))
                dve.wait_ge(S("ld_par"), 16 * 11)
                for vec in range(2):
                    ins = dve.scalar_tensor_tensor(a1[:, vec, :], colp[:, vec, 1, :], 1.0, gcol[:, l, :], ALU.add, ALU.mult)
                ins.then_inc(S("a1_ready" if l == 0 else "a1_ready_b"), 1)
                dve.wait_ge(S("a1_ready" if l == 0 else "a1_ready_b"), 1)

            def hT_even(l, t):
                vec = min(t, 1)
                dve.wait_ge(*at("xn_turned", l, 2 * t + 1))
                for c in range(4):
                    ins = dve.tensor_scalar(hT[:, c, P * t:P * (t + 1)], PS[:, 2 * t, P * c:P * (c + 1)],
                                            a1[:, vec, c:c + 1], colp[:, vec, 0, c:c + 1], ALU.mult, ALU.add)
                ins.then_inc(S("hT_dve"), 1)

            def rope_tables():
                link(dve.tensor_scalar(gqk[:, 0, :], gqk[:, 0, :], 0.125, None, ALU.mult))
                for w in range(2):
                    for t in range(2):
                        cos, sin = (cf[:, o + 64 * t:o + 64 * (t + 1)] for o in (C_COS, C_SIN))
                        dve.tensor_tensor(rope_qk[:, w, 0, t, :], cos, gqk[:, w, :], ALU.mult)
                        g4 = gqk[:, w, :].rearrange("p (r f d) -> p r f d", r=2, f=2)
                        s4 = sin.rearrange("p (r f d) -> p r f d", r=2, f=2)
                        o4 = rope_qk[:, w, 1, t, :].rearrange("p (r f d) -> p r f d", r=2, f=2)
                        for f in range(2):
                            ins = dve.tensor_tensor(o4[:, :, f, :], s4[:, :, f, :], g4[:, :, 1 - f, :], ALU.mult)
                link(ins)

            def by_head(ap, nh):
                return ap.rearrange("p (h d) -> p h d", h=nh)

            def rope(dst, nh, cos, sin, end=link):
                n = nh * 64
                dve.tensor_tensor(by_head(tmp1[:, 0:n], nh), by_head(dst, nh),
                                  cos.unsqueeze(1).to_broadcast([P, nh, 64]), ALU.mult)
                s5 = dst.rearrange("p (h f d) -> p h f d", h=2 * nh, f=2)
                t5 = tmp2[:, 0:n].rearrange("p (h f d) -> p h f d", h=2 * nh, f=2)
                for rc in range(2):
                    for f in range(2):
                        sn = sin[:, 32 * rc + 16 * f:32 * rc + 16 * f + 16]
                        ins = dve.tensor_tensor(t5[:, rc::2, f, :], s5[:, rc::2, 1 - f, :],
                                                sn.unsqueeze(1).to_broadcast([P, nh, 16]), ALU.mult)
                link(ins)
                end(dve.tensor_tensor(dst, tmp1[:, 0:n], tmp2[:, 0:n], ALU.add))

            def norm_rope_a(w, src, nh, name):
                dve.wait_ge(S("q_squared" if w == 0 else "k_squared"), NT)
                link(dve.tensor_reduce(ss[:, 0:NT * nh], by_head(sqb[:, 3072 * w:3072 * w + NT * nh * 64], NT * nh), X, ALU.add))
                rstd(NT * nh, 1.0 / 64)
                for t in range(NT):
                    end = lambda ins, t=t: done(ins, name, t + 1)
                    a = src[:, t, 0:nh * 64]
                    link(dve.tensor_tensor(by_head(a, nh), by_head(a, nh),
                                           rs[:, nh * t:nh * (t + 1)].unsqueeze(2).to_broadcast([P, nh, 64]), ALU.mult))
                    if t == 0:
                        end(dve.tensor_tensor(by_head(a, nh), by_head(a, nh),
                                              gqk[:, w, :].unsqueeze(1).to_broadcast([P, nh, 64]), ALU.mult))
                    else:
                        rope(a, nh, rope_qk[:, w, 0, t - 1, :], rope_qk[:, w, 1, t - 1, :], end)

            def qk_norm_rope(l):
                if l == 0:
                    norm_rope_a(0, q, 16, "q_ready")
                    norm_rope_a(1, k_, 4, "qk_ready")
                    return
                for w, src in enumerate((q, k_)):
                    dve.wait_ge(*at("qkv_copied", 1, 6 * (w + 1)))
                    for t in (1, 2):
                        cos, sin = (cf[:, o + 64 * (t - 1):o + 64 * t] for o in (C_COS, C_SIN))
                        rope(src[:, t, :], 16, cos, sin,
                             (lambda ins, t=t: done(ins, "qk_ready", NT + t)) if w else link)

            def evac_group(l, n, what, b, a, cnt, copy):
                src = PS[:, QK_BANK[n % 4], 0:P * cnt].rearrange("p (c n) -> p c n", c=cnt)
                dst = (kT if what == "k" else qT)[:, a:a + cnt, P * b:P * (b + 1)]
                return copy(dst, src)

            def qk_even(l):
                for n, (what, b, a, cnt) in enumerate(qk_groups(l)):
                    if n % 2 == 0:
                        dve.wait_ge(*at("qk_turned", l, n + 1))
                        evac_group(l, n, what, b, a, cnt, dve.tensor_copy).then_inc(S("qkT_dve"), 1)

            def row_max(l, i):
                t, pr = steps[i]
                nk = P * len(blocks_of(t))
                dve.wait_ge(*at("s_done", l, i + 1))
                dve.tensor_reduce(nm[:, i % 2, :], PS[:, 2 * (i % 2):2 * (i % 2) + 2, 0:nk], X, ALU.max,
                                  negate=True).then_inc(S("nm_ready"), 1)

            def after_exp(l, i):
                t, pr = steps[i]
                nk = P * len(blocks_of(t))
                r = rsm[:, i % 4, :]
                dve.wait_ge(*at("p_ready", l, i + 1))
                if l == 0:
                    if i >= 4:
                        dve.wait_ge(S("o_copied"), i - 3)
                    dve.reciprocal(r, sm[:, i % 4, :]).then_inc(S("rsm_ready"), 1)
                    return
                link(dve.reciprocal(r, sm[:, i % 4, :]))
                dve.tensor_tensor(r[:, 1:2], r[:, 1:2], small[:, 4:5], ALU.mult)
                link(dve.tensor_scalar(pr_[:, i % 2, 0, 0:nk], pr_[:, i % 2, 0, 0:nk], r[:, 0:1], None, ALU.mult))
                dve.scalar_tensor_tensor(pr_[:, i % 2, 0, 0:nk], pr_[:, i % 2, 1, 0:nk], r[:, 1:2],
                                         pr_[:, i % 2, 0, 0:nk], ALU.mult, ALU.add).then_inc(S("a_ready"), 1)

            def take_pT(i):
                t, pr = steps[i]
                nk = P * len(blocks_of(t))
                dve.wait_ge(*at("p_turned", 0, i + 1))
                if i >= 2:
                    dve.wait_ge(*at("o_done", 0, i - 1))
                dve.tensor_copy(ptt[:, i % 2, 0, 0:nk], PS[:, 4, 0:nk]).then_inc(S("pT_dve"), 1)

            def take_o(l, i):
                t, pr = steps[i]
                dve.wait_ge(*at("o_done", l, i + 1))
                if l == 0:
                    dst = q[:, t, :].rearrange("p (m f d) -> p m f d", m=2, f=2)[:, pr // 4, :, 64 * (pr % 4):64 * (pr % 4) + 64]
                    src = PS[:, 6, 0:P].rearrange("p (f d) -> p f d", f=2)
                    dve.wait_ge(S("rsm_ready"), i + 1)
                    dve.tensor_tensor(dst, src, rsm[:, i % 4, :].unsqueeze(2).to_broadcast([P, 2, 64]),
                                      ALU.mult).then_inc(S("o_copied"), 1)
                else:
                    dve.tensor_copy(q[:, t, P * pr:P * (pr + 1)], PS[:, 6, 0:P]).then_inc(S("o_copied"), 1)

            def sub_norm(t):
                dve.wait_ge(S("o_squared"), 8 * (t + 1))
                rstd(8, 1.0 / P, 8 * t)
                for h in range(8):
                    ins = dve.scalar_tensor_tensor(q[:, t, P * h:P * (h + 1)], q[:, t, P * h:P * (h + 1)],
                                                   rs[:, 8 * t + h:8 * t + h + 1], gsub[:], ALU.mult, ALU.mult)
                done(ins, "o_ready", t + 1)

            def attention(l):
                n = len(steps)
                for i in range(n + 3):
                    if l == 0 and 2 <= i < n + 2:
                        take_pT(i - 2)
                    if i < n:
                        row_max(l, i)
                    if 1 <= i <= n:
                        after_exp(l, i - 1)
                    if i >= 3:
                        take_o(l, i - 3)
                    if l == 1 and i in SUB_AT:
                        sub_norm(SUB_AT.index(i))

            def oT_even(l):
                dve.wait_ge(*at("state_out", l, 32))
                for g in range(0, 6, 2):
                    dve.wait_ge(*at("o_turned", l, g + 1))
                    dve.tensor_copy(oT[:, 0:4, P * (g // 2):P * (g // 2 + 1)],
                                    PS[:, g, :].rearrange("p (c n) -> p c n", c=4)).then_inc(S("oT_dve"), 1)

            def attn_to_ffn(l):
                dve.wait_ge(*at("ld_gate_attn", l, 32))
                for j in range(2):
                    if j == 1:
                        dve.wait_ge(*at("ld_rows", l, 80))
                        for vec in range(2):
                            ins = dve.scalar_tensor_tensor(sbc[:, vec, 1, :], sbc[:, vec, 1, :], 1.0, gbc, ALU.add, ALU.mult)
                        link(ins)
                    for t in range(NT):
                        n = NT * j + t
                        dve.wait_ge(*at("wo_done", l, n + 1))
                        done(dve.tensor_tensor(tmp2[:, 0:512], PS[:, 2 * t, :], gate_bc[:, min(t, 1), 512 * j:512 * (j + 1)],
                                               ALU.mult), *at("wo_copied", l, n + 1))
                        done(dve.tensor_tensor(x[:, t, 512 * j:512 * (j + 1)], x[:, t, 512 * j:512 * (j + 1)], tmp2[:, 0:512],
                                               ALU.add), *at("x_attn", l, n + 1))
                        if j == 1:
                            norm_ffn(l, t)

            def norm_ffn(l, t):
                dve.wait_ge(*at("sq_ffn", l, t + 1))
                rstd(1, 1.0 / D, t)
                vec = min(t, 1)
                out = hperm[:, t, :].rearrange("p (k a) -> p a k", k=KC)
                link(dve.scalar_tensor_tensor(tmp1[:], x[:, t, :], rs[:, t:t + 1], sbc[:, vec, 1, :], ALU.mult, ALU.mult))
                done(dve.tensor_tensor(out, tmp1.rearrange("p (a k) -> p a k", k=KC),
                                       sbc[:, vec, 0, :].rearrange("p (a k) -> p a k", k=KC), ALU.add), *at("h_ready", l, t + 1))
                dve.wait_ge(*at("hr_turned", l, 2 * t + 1))
                if t == 2:
                    dve.wait_ge(*at("logits", l, 1))
                dve.tensor_copy(hTr[:, t % 2, 0, :], PS[:, 1 if t % 2 == 0 else 5, :]).then_inc(S("hr_dve"), 1)

            def route(l):
                dve.wait_ge(*at("logits", l, NT))
                oh = R(0, 48)
                sg_, m_ = R(48, 48), R(96, 48)
                p6 = R(144, 72).rearrange("p (g c) -> p g c", g=12)
                t3 = lambda ap, n: ap.rearrange("p (t e) -> p t e", t=n)
                oh1, oh2 = R(216, 48), R(264, 48)
                cand = R(312, 48)
                gs, gm, ing, t0 = R(360, 12), R(372, 3), R(375, 12), R(387, 12)
                vv = R(400, 6)
                cc = R(406, 6)
                sm3, rk = R(412, 3), R(416, 48)
                rr, bs, jj, tl = R(464, 6), R(470, 6), R(476, 6), R(482, 6)
                pref = R(490, 64)
                cmp_ = R(556, 80)
                dve.tensor_tensor(t3(sg_, 3), t3(PS[:, 6, 0:48], 3), br[:].unsqueeze(1).to_broadcast([P, 3, E]),
                                  ALU.add).then_inc(S("lg_ready"), 1)
                dve.wait_ge(*at("sig_ready", l, 1))
                s4 = sg_.rearrange("p (g c) -> p g c", g=12)
                dve.tensor_tensor(p6[:, :, 0:3], s4[:, :, 0:3], s4[:, :, 1:4], ALU.add)
                dve.tensor_tensor(p6[:, :, 3:5], s4[:, :, 0:2], s4[:, :, 2:4], ALU.add)
                link(dve.tensor_tensor(p6[:, :, 5:6], s4[:, :, 0:1], s4[:, :, 3:4], ALU.add))
                link(dve.tensor_reduce(gs, p6, X, ALU.max))
                link(dve.tensor_reduce(gm, t3(gs, 3), X, ALU.max))
                link(dve.tensor_tensor(t3(t0, 3), t3(gs, 3), gm.unsqueeze(2).to_broadcast([P, 3, NG]), ALU.is_equal))
                link(dve.tensor_tensor(t3(t0, 3), t3(t0, 3),
                                       cf[:, C_REVG:C_REVG + NG].unsqueeze(1).to_broadcast([P, 3, NG]), ALU.mult))
                link(dve.tensor_reduce(gm, t3(t0, 3), X, ALU.max))
                link(dve.tensor_tensor(t3(ing, 3), t3(t0, 3), gm.unsqueeze(2).to_broadcast([P, 3, NG]), ALU.is_equal))
                dve.tensor_scalar(t0, ing, 4.0, -4.0, ALU.mult, ALU.add)
                link(dve.tensor_tensor(t3(m_, 12), s4, ing.unsqueeze(2).to_broadcast([P, 12, 4]), ALU.mult))
                link(dve.tensor_tensor(t3(m_, 12), t3(m_, 12), t0.unsqueeze(2).to_broadcast([P, 12, 4]), ALU.add))
                for k, o in enumerate((oh1, oh2)):
                    vk, ck = vv[:, 3 * k:3 * k + 3], cc[:, 3 * k:3 * k + 3]
                    link(dve.tensor_reduce(vk, t3(m_, 3), X, ALU.max))
                    link(dve.tensor_tensor(t3(cand, 3), t3(m_, 3), vk.unsqueeze(2).to_broadcast([P, 3, E]), ALU.is_equal))
                    link(dve.tensor_tensor(t3(cand, 3), t3(cand, 3),
                                           cf[:, C_REVE:C_REVE + E].unsqueeze(1).to_broadcast([P, 3, E]), ALU.mult))
                    link(dve.tensor_reduce(ck, t3(cand, 3), X, ALU.max))
                    link(dve.tensor_tensor(t3(o, 3), t3(cand, 3), ck.unsqueeze(2).to_broadcast([P, 3, E]), ALU.is_equal))
                    if k == 0:
                        link(dve.scalar_tensor_tensor(m_, o, -8.0, m_, ALU.mult, ALU.add))
                dve.tensor_tensor(oh, oh1, oh2, ALU.add).then_inc(S("oh_ready"), 1)
                link(dve.tensor_tensor(sm3, vv[:, 0:3], vv[:, 3:6], ALU.add))
                link(dve.reciprocal(sm3, sm3))
                for k in range(2):
                    dve.tensor_tensor(small[:, 8 + 3 * k:11 + 3 * k], vv[:, 3 * k:3 * k + 3], sm3, ALU.mult)
                dve.memset(pref, 0.0)
                link(dve.tensor_scalar(cc, cc, -1.0, float(E), ALU.mult, ALU.add))
                dve.wait_ge(*at("ranks", l, 1))
                link(dve.tensor_copy(rk, PS[:, 2, 0:48]))
                thr = cf[:, C_THR:C_THR + 5]
                c16 = cmp_.rearrange("p (e c) -> p e c", e=E)
                link(dve.tensor_tensor(c16, PS[:, 2, 64:80].unsqueeze(2).to_broadcast([P, E, 5]),
                                       thr.unsqueeze(1).to_broadcast([P, E, 5]), ALU.is_gt))
                link(dve.tensor_reduce(pref[:, 16:32], c16, X, ALU.add))
                dve.tensor_copy(nxi[:, 0:E], pref[:, 16:32]).then_inc(S("nx_ready"), 1)
                for n, step in enumerate((1, 2, 4, 8)):
                    a, b = 32 * (n % 2), 32 * ((n + 1) % 2)
                    link(dve.tensor_tensor(pref[:, b + 16:b + 32], pref[:, a + 16:a + 32], pref[:, a + 16 - step:a + 32 - step], ALU.add))
                dve.wait_ge(*at("nx_ready", l, 1))
                link(dve.tensor_copy(nxi[:, E:E + 1], pref[:, 31:32]))
                link(dve.tensor_tensor(pref[:, 16:32], pref[:, 16:32], nxi[:, 0:E], ALU.subtract))
                for k, o in enumerate((oh1, oh2)):
                    link(dve.tensor_tensor(cand, o, rk, ALU.mult))
                    link(dve.tensor_reduce(rr[:, 3 * k:3 * k + 3], t3(cand, 3), X, ALU.add))
                    link(dve.tensor_tensor(t3(cand, 3), t3(o, 3), pref[:, 16:32].unsqueeze(1).to_broadcast([P, 3, E]), ALU.mult))
                    link(dve.tensor_reduce(bs[:, 3 * k:3 * k + 3], t3(cand, 3), X, ALU.add))
                c6 = cmp_[:, 0:30].rearrange("p (e c) -> p e c", e=6)
                link(dve.tensor_tensor(c6, rr.unsqueeze(2).to_broadcast([P, 6, 5]), thr.unsqueeze(1).to_broadcast([P, 6, 5]), ALU.is_ge))
                link(dve.tensor_reduce(jj, c6, X, ALU.add))
                link(dve.scalar_tensor_tensor(tl, jj, float(E - 1), bs, ALU.add, ALU.add))
                dve.tensor_scalar(bs, jj, 0.0, None, ALU.is_equal)
                link(dve.tensor_tensor(cc, cc, tl, ALU.subtract))
                link(dve.tensor_tensor(cc, cc, bs, ALU.mult))
                link(dve.tensor_tensor(tl, tl, cc, ALU.add))
                link(dve.scalar_tensor_tensor(rr, jj, -float(CAP), rr, ALU.mult, ALU.add))
                link(dve.scalar_tensor_tensor(tl, rr, float(TILES), tl, ALU.mult, ALU.add))
                dve.tensor_copy(rti[:], tl).then_inc(S("rows_ready"), 1)
                dve.wait_ge(*at("ld_list", l, 32))
                dve.tensor_scalar(gi[:], lst[:], 2.0, cf[:, C_HALF:C_HALF + 1], ALU.mult, ALU.add).then_inc(S("idx_ready"), 1)

            def experts(l):
                more = dve.alloc_register(f"dve_more{l}")
                dve.reg_mov(more, 0)

                def tag(b):
                    return "more" if b else "main"

                def take_x(b, col):
                    dve.tensor_copy(xc[:, b, :], xg[:, bass.ds(col, 512)]).then_inc(tile_sem(f"xc_{tag(b)}", l), 1)

                def take_xT(b, nth):
                    dve.wait_ge(*at(f"x_turned_{tag(b)}", l, nth))
                    dve.tensor_copy(xT[:, b], PS[:, 4 * b, :].rearrange("p (c n) -> p c n", c=4)).then_inc(tile_sem(f"xT_{tag(b)}", l), 1)

                def gated(b, nth):
                    dve.wait_ge(*at(f"silu_{tag(b)}", l, nth))
                    dve.tensor_tensor(hE[:, b, :], sg[:, b, :], PS[:, 4 * b + 1, 256:512], ALU.mult).then_inc(tile_sem(f"h_{tag(b)}", l), 1)

                def take_hT(b, nth):
                    dve.wait_ge(*at(f"h_turned_{tag(b)}", l, nth))
                    dve.tensor_copy(hTt[:, b], PS[:, 4 * b + 2, 0:256].rearrange("p (c n) -> p c n", c=2)).then_inc(tile_sem(f"hT_{tag(b)}", l), 1)

                def expert(e, left=2):
                    nx = dve.value_load(nxi[0:1, bass.ds(e, 1)], min_val=0, max_val=5)
                    with dve.If(nx > 0):
                        dve.wait_ge(tile_sem("xg_more", l), 1)
                        with dve.Fori(0, nx):
                            reg = dve.snap(more)
                            take_x(1, (reg + E) * 512)
                            take_xT(1, reg + 1)
                            gated(1, reg + 1)
                            take_hT(1, reg + 1)
                            dve.reg_add(more, more, 1)
                        dve.nop()
                    with dve.Else():
                        dve.nop()
                    if left >= 1:
                        take_xT(0, e + 2)
                    if left >= 2:
                        dve.wait_ge(*at("xg_main", l, e + 3))
                        take_x(0, (e + 2) * 512)
                    gated(0, e + 1)
                    take_hT(0, e + 1)

                dve.wait_ge(*at("xg_main", l, 1))
                take_x(0, 0)
                take_xT(0, 1)
                dve.wait_ge(*at("xg_main", l, 2))
                take_x(0, 512)
                with dve.Fori(0, E - 2) as e:
                    expert(e)
                expert(E - 2, 1)
                expert(E - 1, 0)

            def combine(l, t):
                dve.wait_ge(*at("y_scaled", l, t + 1))
                link(dve.scalar_tensor_tensor(yk[:, t, :], yk[:, NT + t, :], small[:, 11 + t:12 + t], yk[:, t, :], ALU.mult, ALU.add))
                link(dve.tensor_tensor(yk[:, t, :], yk[:, t, :], gate_bc[:, min(t, 1), :], ALU.mult))
                done(dve.tensor_tensor(x[:, t, :], x[:, t, :], yk[:, t, :], ALU.add), *at("x_moe", l, t + 1))

            def last_norm(t):
                dve.wait_ge(S("sq_final"), t + 1)
                rstd(1, 1.0 / D, t)
                dve.scalar_tensor_tensor(yk[:, t, :], x[:, t, :], rs[:, t:t + 1], ubuf, ALU.mult, ALU.mult).then_inc(S("y_ready"), 1)

            dve.memset(small[:], 0.0).then_inc(S("small_zero"), 1)
            dve.wait_ge(S("small_zero"), 1)
            dve.wait_ge(S("ld_x"), 32)
            for t in range(NT):
                norm_attn(0, t)
            cols(0)
            for t in range(NT):
                hT_even(0, t)
            lam0 = 0.8 - 0.6 * float(np.exp(-0.3))
            for i in range(2):
                link(dve.tensor_tensor(lamv[:, 2 * i, :], lamv[:, 2 * i, :], lamv[:, 2 * i + 1, :], ALU.mult))
                link(dve.tensor_reduce(small[:, i:i + 1], lamv[:, 2 * i, :], X, ALU.add))
            dve.tensor_scalar(gsub[:], gsub[:], 1.0 - lam0, None, ALU.mult).then_inc(S("lam_dots"), 1)
            dve.wait_ge(S("lam_exp"), 1)
            link(dve.tensor_tensor(small[:, 4:5], small[:, 3:4], small[:, 2:3], ALU.subtract))
            link(dve.tensor_scalar(small[:, 4:5], small[:, 4:5], -lam0, None, ALU.add))
            rope_tables()
            qk_norm_rope(0)
            qk_even(0)
            attention(0)
            oT_even(0)
            attn_to_ffn(0)
            route(0)
            experts(0)
            cols(1)
            dve.wait_ge(*at("ld_gate_ffn", 0, 32))
            for t in range(NT + 2):
                if t < NT:
                    combine(0, t)
                if 1 <= t <= NT:
                    norm_attn(1, t - 1)
                if t >= 2:
                    hT_even(1, t - 2)
            qk_norm_rope(1)
            qk_even(1)
            attention(1)
            oT_even(1)
            attn_to_ffn(1)
            route(1)
            experts(1)
            dve.wait_ge(*at("ld_gate_ffn", 1, 32))
            dve.wait_ge(S("ld_gf"), 16)
            for t in range(NT + 1):
                if t < NT:
                    combine(1, t)
                if t >= 1:
                    last_norm(t - 1)

        @block.scalar
        def _(act):
            def square(tag, dst, t):
                act.activation(dst, x[:, t, :], ACT.Square, accum_out=ss[:, t:t + 1]).then_inc(S(f"sq_{tag}"), 1)
                root(1, t)

            def scale_y(l, t):
                act.wait_ge(*at(f"ld_y{t}", l, 16))
                act.activation(yk[:, t, :], yk[:, t, :], ACT.Identity, scale=small[:, 8 + t:9 + t]).then_inc(S("y_scaled"), 1)

            roots = [0]

            def root(n, o=0):
                roots[0] += 1
                act.wait_ge(S("var_ready"), roots[0])
                act.activation(rs[:, o:o + n], rs[:, o:o + n], ACT.Sqrt).then_inc(S("std_ready"), 1)

            def take_mod(l, j):
                if l == 1 and j in (0, 3):
                    act.wait_ge(S("mod_stored"), 32 if j == 0 else 64)
                act.wait_ge(*at("mod_ps", l, j + 1))
                act.copy(modsb[:, j, :], PS[:, 7, 0:P]).then_inc(S("mod_sb"), 1)

            def hT_odd(l):
                act.wait_ge(S("a1_ready" if l == 0 else "a1_ready_b"), 1)
                for g in range(1, 6, 2):
                    t = g // 2
                    vec = min(t, 1)
                    act.wait_ge(*at("xn_turned", l, g + 1))
                    for c in range(4):
                        ins = act.activation(hT[:, 4 + c, P * t:P * (t + 1)], PS[:, g, P * c:P * (c + 1)], ACT.Identity,
                                             scale=a1[:, vec, 4 + c:5 + c], bias=colp[:, vec, 0, 4 + c:5 + c])
                    ins.then_inc(S("hT_act"), 1)

            def take_qkv(l, js):
                for j in js:
                    for t in range(NT):
                        act.wait_ge(*at("qkv_done", l, NT * j + t + 1))
                        src = PS[:, 2 * t, :]
                        if j < 2 and l == 0:
                            ins = act.copy(q[:, t, 512 * j:512 * (j + 1)].rearrange("p (r f d) -> p f r d", r=4, f=2),
                                           src.rearrange("p (f r d) -> p f r d", f=2, r=4))
                        elif j < 2:
                            ins = act.mul(q[:, t, 512 * j:512 * (j + 1)], src, 0.125)
                        elif l == 0:
                            act.copy(k_[:, t, 0:256], src[:, 0:256])
                            ins = act.copy(v[:, t, 0:256], src[:, 256:512])
                        elif j < 4:
                            ins = act.copy(k_[:, t, 512 * (j - 2):512 * (j - 1)], src)
                        else:
                            ins = act.copy(v[:, t, 512 * (j - 4):512 * (j - 3)], src)
                        ins.then_inc(S("qkv_copied"), 1)

            def square_heads(name, src, nh, o, copied):
                act.wait_ge(S("qkv_copied"), copied)
                for t in range(NT):
                    n = nh * 64
                    act.activation(sqb[:, o + n * t:o + n * (t + 1)], src[:, t, 0:n], ACT.Square).then_inc(S(name), 1)

            def qk_odd(l):
                for n, (what, b, a, cnt) in enumerate(qk_groups(l)):
                    if n % 2 == 1:
                        act.wait_ge(*at("qk_turned", l, n + 1))
                        src = PS[:, QK_BANK[n % 4], 0:P * cnt].rearrange("p (c n) -> p c n", c=cnt)
                        act.copy((kT if what == "k" else qT)[:, a:a + cnt, P * b:P * (b + 1)], src).then_inc(S("qkT_act"), 1)

            def exps(l, i):
                t, pr = steps[i]
                nk = P * len(blocks_of(t))
                act.wait_ge(*at("nm_ready", l, i + 1))
                if i >= 2:
                    act.wait_ge(*at("p_turned", l, i - 1))
                if i >= 4 and l == 0:
                    act.wait_ge(S("rsm_ready"), i - 3)
                for m in range(2):
                    ins = act.activation(pr_[:, i % 2, m, 0:nk], PS[:, 2 * (i % 2) + m, 0:nk], ACT.Exp,
                                         bias=nm[:, i % 2, m:m + 1], accum_out=sm[:, i % 4, m:m + 1])
                ins.then_inc(S("p_ready"), 1)

            def take_pT(l, i):
                t, pr = steps[i]
                nk = P * len(blocks_of(t))
                m = 1 if l == 0 else 0
                act.wait_ge(*at("p_turned", l, i + 1))
                if i >= 2:
                    act.wait_ge(*at("o_done", l, i - 1))
                act.copy(ptt[:, i % 2, m, 0:nk], PS[:, pT_bank(l, i, m), 0:nk]).then_inc(S("pT_act"), 1)

            def square_o(i):
                t, pr = steps[i]
                act.wait_ge(*at("o_copied", 1, i + 1))
                if i >= 2:
                    act.wait_ge(S("o_squared"), i - 1)
                act.activation(sqo[:, i % 2, :], q[:, t, P * pr:P * (pr + 1)], ACT.Square,
                               accum_out=ss[:, 8 * t + pr:8 * t + pr + 1]).then_inc(S("o_squared"), 1)

            def attention(l):
                n = len(steps)
                squared = 0
                for i in range(n + 3):
                    if 2 <= i < n + 2:
                        take_pT(l, i - 2)
                    if i < n:
                        exps(l, i)
                    if l == 0 and i in MOD_WITHIN:
                        take_mod(*MOD_WITHIN[i])
                    if l == 1 and i in SUB_AT:
                        while squared < 8 * (SUB_AT.index(i) + 1):
                            square_o(squared)
                            squared += 1
                        root(8, 8 * SUB_AT.index(i))
                    elif l == 1 and i >= 4 and squared < i - 3:
                        square_o(squared)
                        squared += 1

            def oT_odd(l):
                act.wait_ge(*at("state_out", l, 32))
                for g in range(1, 6, 2):
                    act.wait_ge(*at("o_turned", l, g + 1))
                    act.copy(oT[:, 4:8, P * (g // 2):P * (g // 2 + 1)],
                             PS[:, g, :].rearrange("p (c n) -> p c n", c=4)).then_inc(S("oT_act"), 1)

            def route(l):
                for t in range(NT):
                    act.wait_ge(*at("x_attn", l, NT + t + 1))
                    act.activation(junk[t], x[:, t, :], ACT.Square, accum_out=ss[:, t:t + 1]).then_inc(S("sq_ffn"), 1)
                    root(1, t)
                    act.wait_ge(*at("hr_turned", l, 2 * t + 2))
                    if t == 2:
                        act.wait_ge(*at("logits", l, 1))
                    act.copy(hTr[:, t % 2, 1, :], PS[:, 3 if t % 2 == 0 else 7, :]).then_inc(S("hr_act"), 1)
                act.wait_ge(*at("lg_ready", l, 1))
                act.activation(R(48, 48), R(48, 48), ACT.Sigmoid).then_inc(S("sig_ready"), 1)

            def experts(l):
                act.wait_ge(*at("nx_ready", l, 1))
                more = act.alloc_register(f"act_more{l}")
                act.reg_mov(more, 0)
                act.copy(ss[0:1, 20:21], cf[0:1, 0:1]).then_inc(S("y_main"), 1)
                act.copy(ss[0:1, 21:22], cf[0:1, 0:1]).then_inc(tile_sem("y_more", l), 1)

                def tag(b):
                    return "more" if b else "main"

                def silu(b, nth):
                    act.wait_ge(*at(f"gu_{tag(b)}", l, nth))
                    act.activation(sg[:, b, :], PS[:, 4 * b + 1, 0:256], ACT.Silu).then_inc(tile_sem(f"silu_{tag(b)}", l), 1)

                def take_y(b, col, nth):
                    act.wait_ge(*at(f"down_{tag(b)}", l, nth))
                    act.activation(xg[:, bass.ds(col, 512)], PS[:, 4 * b + 3, :], ACT.Copy).then_inc(tile_sem(f"y_{tag(b)}", l), 1)

                def expert(e, first=False):
                    nx = act.value_load(nxi[0:1, bass.ds(e, 1)], min_val=0, max_val=5)
                    with act.If(nx > 0):
                        with act.Fori(0, nx):
                            reg = act.snap(more)
                            silu(1, reg + 1)
                            take_y(1, (reg + E) * 512, reg + 1)
                            act.reg_add(more, more, 1)
                        act.nop()
                    with act.Else():
                        act.nop()
                    silu(0, e + 1)
                    if not first:
                        take_y(0, (e - 1) * 512, e)

                expert(0, first=True)
                with act.Fori(1, E) as e:
                    expert(e)
                take_y(0, (E - 1) * 512, E)
                act.copy(ss[0:1, 22:23], cf[0:1, 0:1]).then_inc(S("tiles_done"), 1)

            act.wait_ge(S("ld_c"), 32)
            act.wait_ge(S("cs_zero"), 1)
            act.activation(cs[:, :, 0:2], cvec[:].rearrange("p v k -> p k v"), ACT.Silu).then_inc(S("cs_ready"), 1)
            act.wait_ge(S("work_zero"), 1)
            act.wait_ge(S("ld_x"), 32)
            for t in range(NT):
                square("attn", k_[:, t, :], t)
            for j in range(4):
                take_mod(0, j)
            hT_odd(0)
            act.wait_ge(S("lam_dots"), 1)
            act.activation(small[:, 2:4], small[:, 0:2], ACT.Exp).then_inc(S("lam_exp"), 1)
            for l in range(2):
                if l == 0:
                    take_qkv(0, (0, 1))
                    square_heads("q_squared", q, 16, 0, 6)
                    root(48)
                    take_qkv(0, (2,))
                    square_heads("k_squared", k_, 4, 3072, 9)
                    root(12)
                    for slot in MOD_BEFORE:
                        take_mod(*slot)
                else:
                    take_qkv(1, range(6))
                qk_odd(l)
                attention(l)
                oT_odd(l)
                route(l)
                if l == 0:
                    for slot in MOD_AFTER:
                        take_mod(*slot)
                experts(l)
                for t in range(NT + 1):
                    if t < NT:
                        scale_y(l, t)
                    if t >= 1:
                        act.wait_ge(*at("x_moe", l, t))
                        square("attn" if l == 0 else "final", k_[:, t - 1, :] if l == 0 else yk[:, 2 + t, :], t - 1)
                if l == 0:
                    act.wait_ge(*at("x_moe", 0, NT))
                    hT_odd(1)


_INS = ['x_prompt', 'x_sample', 'cache_k_a', 'cache_v_a', 'cache_k_b', 'cache_v_b', 'c', 'c_ctx', 'w_mod', 'b_mod',
        'g_attn', 'g_ffn', 'w_qkv_a', 'w_o_a', 'g_q_a', 'g_k_a', 'w_qkv_b', 'w_o_b', 'lam_q1', 'lam_k1', 'lam_q2',
        'lam_k2', 'g_sub_b', 'w_router', 'b_router', 'w_gate', 'w_up', 'w_down', 'g_final']
_OUTS = [("y_prompt", (128, 1024)), ("y_sample", (256, 1024)), ("state_k0", (128, 256)), ("state_v0", (128, 256)),
         ("state_k1", (128, 1024)), ("state_v1", (128, 1024))]


def kernel(**inputs):
    import concourse.bacc as _bacc
    from concourse.bass_utils import run_bass_kernel_spmd as _run

    nc = _bacc.Bacc("TRN2", target_bir_lowering=False, num_devices=1)
    arrays, tensors = {}, {}
    cf, ci = shape_constants()
    for name, a in [(n, np.ascontiguousarray(inputs[n])) for n in _INS] + [("consts", cf), ("iconsts", ci)]:
        arrays[f"in_{name}_dram"] = a
        tensors[name] = nc.dram_tensor(f"in_{name}_dram", a.shape, mybir.dt.from_np(a.dtype), kind="ExternalInput").ap()
    for name, shape in _OUTS:
        tensors[name] = nc.dram_tensor(f"out_{name}_dram", shape, F32, kind="ExternalOutput").ap()
    hybrid_step_kernel(nc, tensors)
    r = _run(nc, [arrays], core_ids=[0])
    y_p, y_s, k_a, v_a, k_b, v_b = (r.results[0][f"out_{n}_dram"] for n, _ in _OUTS)
    return (y_p.reshape(1, 128, 1024), y_s.reshape(1, 256, 1024), k_a.reshape(1, 1, 128, 4, 64),
            v_a.reshape(1, 1, 128, 4, 64), k_b.reshape(1, 1, 128, 8, 2, 64), v_b.reshape(1, 1, 128, 8, 128))
```

```python
from contextlib import ExitStack

import numpy as np

import concourse.bass as bass
from concourse import mybir

F32 = mybir.dt.float32
I32 = mybir.dt.int32
ALU = mybir.AluOpType
ACT = mybir.ActivationFunctionType
X = mybir.AxisListType.X

P = 128
D = 1024
NT = 3
KC = D // P
E = 16
NG = 4
GRID_W = 64
CAP = 64
XT = (2 * NT * P - 1) // CAP
TILES = E + XT
EPS = 1e-6
SLOT = 4096
NSLOT = 6
DEEP = 3
N_MOD = 6

C_ID, C_UP, C_ONE = 0, 128, 256
C_COS, C_SIN = 384, 512
C_REVE, C_REVG, C_THR, C_IOTA = 640, 656, 660, 665
C_N = C_IOTA + CAP


def shape_constants():
    c = np.zeros((P, C_N), np.float32)
    c[:, C_ID:C_ID + P] = np.eye(P)
    c[:, C_UP:C_UP + P] = np.triu(np.ones((P, P)), 1)
    c[:, C_ONE:C_ONE + P] = 1.0
    inv = np.power(np.float32(10000.0), -np.arange(0, 32, 2, dtype=np.float32) / np.float32(32))
    for t in range(2):
        tok = np.arange(P) + P * t
        row = (tok // GRID_W).astype(np.float32)[:, None] * inv
        col = (tok % GRID_W).astype(np.float32)[:, None] * inv
        c[:, C_COS + 64 * t:C_COS + 64 * (t + 1)] = np.concatenate([np.cos(row)] * 2 + [np.cos(col)] * 2, 1)
        c[:, C_SIN + 64 * t:C_SIN + 64 * (t + 1)] = np.concatenate(
            [-np.sin(row), np.sin(row), -np.sin(col), np.sin(col)], 1)
    c[:, C_REVE:C_REVE + E] = E - np.arange(E)
    c[:, C_REVG:C_REVG + NG] = NG - np.arange(NG)
    c[:, C_THR:C_THR + 5] = CAP * np.arange(1, 6)
    c[:, C_IOTA:C_IOTA + CAP] = np.arange(CAP)
    return c


def hybrid_step_kernel(nc, t_):
    with ExitStack() as ctx:
        def sb(name, shape, dt=F32):
            return ctx.enter_context(nc.sbuf_tensor(name, shape, dt))

        sems = {}

        def S(name):
            if name not in sems:
                sems[name] = ctx.enter_context(nc.semaphore(name))
            return sems[name]

        FIRST = dict(mod_ps=12, mod_sb=12, mod_stored=64, ld_cols=32, ld_gate_attn=32, ld_cache=32, xn_ready=3,
                     xn_turned=6, mod_bias=32, hT_dve=3, hT_act=3, qkv_done=9, qkv_copied=9, qk_ready=3, qk_turned=10, qkT_dve=5,
                     qkT_act=5, state_out=32, s_done=24, nm_ready=24, p_ready=24, p_turned=24, pT_act=24, pT_dve=24,
                     o_done=24, o_copied=24, o_ready=3, o_turned=6, oT_dve=3, oT_act=3, wo_done=6, wo_copied=6, x_attn=6,
                     sq_attn=3, sq_ffn=3, ld_rows=80, ld_gate_ffn=32, h_ready=3, hr_turned=6, hr_dve=3,
                     hr_act=3, logits=3, lg_ready=1, sig_ready=1, oh_ready=1, ranks=1, nx_ready=1, rows_ready=1,
                     x_moe=3, y_main=E + 1, y_stored=1, y_stored0=8 * E, y_stored1=8 * E, ld_y0=32, ld_y1=32,
                     ld_y2=32, y_scaled=3)
        FIRST |= {f"{x}_main": E // 2 for x in ("rank", "one_hot", "x_picked", "xT")}
        FIRST |= {f"{x}_main": E for x in ("gu", "silu", "h", "h_turned", "hT", "down")}

        def tile_sem(name, l):
            return S(f"{name}{l}") if name.endswith("_more") else S(name)

        def at(name, l, n):
            if name.endswith("_more"):
                return tile_sem(name, l), n
            return S(name), n + (FIRST[name] if l == 1 else 0)

        mod_d = nc.dram_tensor("mod_scratch", [2, 2, N_MOD * D], F32, kind="Internal").ap()
        y_d = nc.dram_tensor("y_scratch", [TILES * CAP, D], F32, kind="Internal").ap()

        ring = sb("ring", [P, NSLOT, SLOT])
        x = sb("x", [P, NT, D])
        gate_bc = sb("gate_bc", [P, 2, D])
        cf = sb("cf", [P, C_N])
        modsb = sb("modsb", [P, 12, P])
        cs = sb("cs", [P, KC, 32])
        cvec = sb("cvec", [P, 2, KC])
        gcol = sb("gcol", [P, 2, KC])
        colp = sb("colp", [P, 2, 2, KC])
        a1 = sb("a1", [P, 2, KC])
        wr = sb("wr", [P, KC, E])
        br = sb("br", [P, E])
        gqk = sb("gqk", [P, 2, 64])
        rope_qk = sb("rope_qk", [P, 2, 2, 2, 64])
        gsub = sb("gsub", [P, P])
        small = sb("small", [P, 16])
        ss = sb("ss", [P, 64])
        rs = sb("rs", [P, 64])
        nm = sb("nm", [P, 2, 2])
        sm = sb("sm", [P, 4, 2])
        rsm = sb("rsm", [P, 4, 2])
        work = sb("work", [P, 19456])
        rti = sb("rti", [P, 6], I32)
        nxi = sb("nxi", [P, E], I32)
        rkm = sb("rkm", [P, E * NT])
        rkp = sb("rkp", [P, 2 * NT])
        rkx = sb("rkx", [P, NT])
        PS = ctx.enter_context(nc.psum_tensor("PS", [P, 8, 512], F32))

        ident = cf[:, C_ID:C_ID + P]
        upper = cf[:, C_UP:C_UP + P]
        ones = cf[:, C_ONE:C_ONE + P]

        W_R1, W_R2, W_R3, W_V, W_KT, W_P, W_SQ = 0, 3072, 6144, 9216, 13312, 17408, 18944
        r1 = work[:, W_R1:W_R1 + 3072]
        r2 = work[:, W_R2:W_R2 + 3072]
        r3 = work[:, W_R3:W_R3 + 3072]
        hT = r1.rearrange("p (k n) -> p k n", k=KC)
        qT = r1.rearrange("p (k n) -> p k n", k=KC)
        xn = r2.rearrange("p (t n) -> p t n", t=NT)
        q = xn
        k_ = r3.rearrange("p (t n) -> p t n", t=NT)
        oT = r3.rearrange("p (k n) -> p k n", k=KC)
        v = work[:, W_V:W_V + 4096].rearrange("p (t n) -> p t n", t=4)
        kc = gate_bc[:, 0, :]
        kT = work[:, W_KT:W_KT + 4096].rearrange("p (k n) -> p k n", k=KC)
        pr_ = work[:, W_P:W_P + 1536].rearrange("p (i m n) -> p i m n", i=2, m=2)
        gate_flat = gate_bc[:].rearrange("p a b -> p (a b)")
        ptt = gate_flat[:, 0:1536].rearrange("p (i m n) -> p i m n", i=2, m=2)
        zero = gate_flat[:, 1536:2048]
        lamv = gate_bc[:, 1, 0:256].rearrange("p (a b) -> p a b", a=4)
        sqo = work[:, W_SQ:W_SQ + 2 * P].rearrange("p (a b) -> p a b", a=2)
        sqb = work[:, W_KT:W_KT + 4096]
        tmp1 = work[:, W_P:W_P + 1024]
        tmp2 = work[:, W_P + 1024:W_P + 2048]
        hperm = r1.rearrange("p (t n) -> p t n", t=NT)
        gbc = work[:, W_V:W_V + 1024]
        junk = [work[:, W_R2 + 1024 * t:W_R2 + 1024 * (t + 1)] for t in range(NT)]
        hTr = work[:, W_V + 1024:W_V + 3072].rearrange("p (i b n) -> p i b n", i=2, b=2)
        sbc = work[:, W_KT:W_KT + 4096].rearrange("p (v m n) -> p v m n", v=2, m=2)
        W_E, W_S = 3072, 3072 + 3 * SLOT
        xTp = gate_flat[:, 0:1024].rearrange("p (k n) -> p k n", k=KC)
        sg = gate_flat[:, 1024:1536].rearrange("p (b n) -> p b n", b=2)
        hE = gate_flat[:, 1536:2048].rearrange("p (b n) -> p b n", b=2)
        xTx = work[:, W_S:W_S + 512].rearrange("p (k n) -> p k n", k=KC)
        hTt = work[:, W_S + 512:W_S + 1024].rearrange("p (b c n) -> p b c n", b=2, c=2)
        ys = work[:, W_S + 1024:W_S + 2560].rearrange("p (b n) -> p b n", b=3)
        hotp = work[:, W_S + 2560:W_S + 2944].rearrange("p (t n) -> p t n", t=NT)
        hotx = work[:, W_S + 2944:W_S + 3136].rearrange("p (t n) -> p t n", t=NT)
        wE = [ring[:, 0:3, :], ring[:, 3:6, :], work[:, W_E:W_S].rearrange("p (m n) -> p m n", m=3)]
        yk = work[:, 0:6144].rearrange("p (j n) -> p j n", j=6)
        gfin = modsb[:].rearrange("p a b -> p (a b)")[:, 0:D]

        rt = work[:, W_S + 3136:W_S + 4096]

        def R(a, n):
            return rt[:, a:a + n]

        def plan():
            jobs, n = [], 0

            def add(kind, l, j):
                nonlocal n
                jobs.append((kind, l, j, n % NSLOT, n // NSLOT))
                n += 1
            for j in range(4):
                add("mod", 0, j)
            for j in range(3):
                add("qkv", 0, j)
            for j in range(4, 12):
                add("mod", 0, j)
            for j in range(10):
                add("mod", 1, j)
            for j in range(2):
                add("wo", 0, j)
            for j in range(10, 12):
                add("mod", 1, j)
            return jobs, n
        jobs, _ = plan()
        uses = [0] * (3 * DEEP)
        place = {}
        for kind, l, j, s, _u in jobs:
            place[(kind, l, j)] = (s, uses[s])
            uses[s] += 1
        moe_base = [list(uses)]
        for s in range(3 * DEEP):
            uses[s] += len(range(s // 3, E, DEEP))
        jobs_b = [("qkv", 1, j) for j in range(6)] + [("wo", 1, j) for j in range(2)]
        for n, (kind, l, j) in enumerate(jobs_b):
            place[(kind, l, j)] = (n % NSLOT, uses[n % NSLOT])
            uses[n % NSLOT] += 1
        moe_base.append(list(uses))

        w_ready = [S(f"w_ready{s}") for s in range(3 * DEEP)]

        def last_use(kind, l, j):
            return at("mod_ps", l, j + 1) if kind == "mod" else at(f"{kind}_done", l, NT * (j + 1))

        wqkv = [t_["w_qkv_a"][0], t_["w_qkv_b"][0]]
        wo = [t_["w_o_a"][0], t_["w_o_b"][0]]

        def chunk_src(w, j):
            return w.rearrange("(p k) n -> p k n", k=KC)[:, :, 512 * j:512 * (j + 1)]

        block = ctx.enter_context(nc.Block())

        @block.sync
        def _(sp):
            freed = [None] * NSLOT

            def load(kind, l, j):
                s, _ = place[(kind, l, j)]
                if freed[s]:
                    sp.wait_ge(*freed[s])
                freed[s] = last_use(kind, l, j)
                src = {"mod": t_["w_mod"][l], "qkv": wqkv[l], "wo": wo[l]}[kind]
                sp.dma_start(ring[:, s, :].rearrange("p (k n) -> p k n", k=KC), chunk_src(src, j)).then_inc(w_ready[s], 16)

            def expert(l, e, par, before):
                for m, w in enumerate((t_["w_gate"], t_["w_up"], t_["w_down"])):
                    src = w[l, bass.ds(e, 1)]
                    sp.wait_ge(*before(m))
                    if m < 2:
                        sp.dma_start(wE[par][:, m, :],
                                     src.rearrange("a (p k) n -> (a p) (k n)", k=KC)).then_inc(w_ready[3 * par + m], 16)
                    else:
                        sp.dma_start(wE[par][:, m, :].rearrange("p (q n) -> p q n", q=4),
                                     src.rearrange("a (q p) n -> p (a q) n", p=P)).then_inc(w_ready[3 * par + m], 16)

            def experts(l):
                expert(l, 0, 0, lambda m: freed[m])
                expert(l, 1, 1, lambda m: freed[3 + m])
                expert(l, 2, 2, lambda m: at("logits", l, NT))

                def three_before(e):
                    return lambda m: at("gu_main" if m < 2 else "down_main", l, e + (1 - DEEP))

                with sp.Fori(1, (E - 1) // 3) as i:
                    for r in range(3):
                        expert(l, 3 * i + r, r, three_before(3 * i + r))
                for e in range(3 * ((E - 1) // 3), E):
                    expert(l, e, e % DEEP, three_before(e))
                for s in range(NSLOT):
                    last = max(range(s // 3, E, DEEP))
                    freed[s] = at("gu_main" if s % 3 < 2 else "down_main", l, last + 1)

            sp.dma_start(cvec[:, 0, :], t_["c_ctx"].rearrange("(p k) -> p k", k=KC)).then_inc(S("ld_c"), 16)
            sp.dma_start(cvec[:, 1, :], t_["c"][0].rearrange("(p k) -> p k", k=KC)).then_inc(S("ld_c"), 16)
            sp.dma_start(x[:, 0, :], t_["x_prompt"][0]).then_inc(S("ld_x"), 16)
            sp.dma_start(x[:, 1:3, :], t_["x_sample"][0].rearrange("(t p) n -> p t n", p=P)).then_inc(S("ld_x"), 16)
            sp.dma_start(cf[:], t_["consts"]).then_inc(S("ld_const"), 16)
            for n, (kind, l, j, _s, _u) in enumerate(jobs):
                if n == 4:
                    sp.wait_ge(S("mod_ps"), 1)
                if n == 5:
                    sp.wait_ge(S("ld_cols"), 32)
                load(kind, l, j)
            experts(0)
            sp.wait_ge(S("ld_y2"), 32)
            for kind, l, j in jobs_b:
                load(kind, l, j)
            experts(1)

        @block.gpsimd
        def _(pool):
            def bc(ap1d):
                return ap1d.partition_broadcast(P)

            pool.memset(cs[:], 0.0).then_inc(S("cs_zero"), 1)
            pool.memset(zero, 0.0).then_inc(S("zero_ready"), 1)
            for l in range(2):
                pool.dma_start(mod_d[l], t_["b_mod"][l].partition_broadcast(2)).then_inc(S("mod_bias"), 32)
            for l in range(2):
                pool.dma_start(gcol[:, l, :], t_["g_attn"][l].rearrange("(p k) -> p k", k=KC)).then_inc(S("ld_par"), 16)
            pool.dma_start(gqk[:, 0, :], bc(t_["g_q_a"][0])).then_inc(S("ld_par"), 16)
            pool.dma_start(gqk[:, 1, :], bc(t_["g_k_a"][0])).then_inc(S("ld_par"), 16)
            pool.dma_start(gsub[:], bc(t_["g_sub_b"][0])).then_inc(S("ld_par"), 16)
            for i, n in enumerate(("lam_q1", "lam_k1", "lam_q2", "lam_k2")):
                pool.dma_start(lamv[:, i, :], bc(t_[n][0])).then_inc(S("ld_par"), 16)
            pool.dma_start(wr[:], t_["w_router"].rearrange("(p k) e -> p k e", k=KC)).then_inc(S("ld_par"), 16)
            pool.dma_start(br[:], bc(t_["b_router"])).then_inc(S("ld_par"), 16)
            def mod_store(l, part):
                lo, hi = (0, 4) if part == 0 else (4, 12)
                pool.wait_ge(S("mod_bias"), 64)
                pool.wait_ge(*at("mod_sb", l, hi))
                for vec in range(2):
                    pool.dma_start(mod_d[l, vec].rearrange("(n g c) -> g n c", g=4, c=P)[:, lo:hi, :],
                                   modsb[vec:P:32, lo:hi, :], accum_op=ALU.add).then_inc(S("mod_stored"), 16)

            def mod_cols(l):
                pool.wait_ge(*at("mod_stored", l, 32 if l == 0 else 64))
                for vec in range(2):
                    pool.dma_start(colp[:, vec, :, :],
                                   mod_d[l, vec, 0:2 * D].rearrange("(m p k) -> p m k", m=2, k=KC)).then_inc(S("ld_cols"), 16)

            def row_bc(dst, l, vec, m, sem):
                pool.dma_start(dst, bc(mod_d[l, vec, m * D:(m + 1) * D])).then_inc(S(sem), 16)

            def cache(l):
                kk, vv = (t_["cache_k_a"], t_["cache_v_a"]) if l == 0 else (t_["cache_k_b"], t_["cache_v_b"])
                n = 256 if l == 0 else 1024
                fk = "p a b -> p (a b)" if l == 0 else "p a b c -> p (a b c)"
                pool.dma_start(kc[:, 0:n], kk[0, 0].rearrange(fk)).then_inc(S("ld_cache"), 16)
                pool.dma_start(v[:, 3, 0:n], vv[0, 0].rearrange("p a b -> p (a b)")).then_inc(S("ld_cache"), 16)

            def states(l):
                n = 256 if l == 0 else 1024
                pool.wait_ge(*at("qkv_copied", l, 9 if l == 0 else 18))
                pool.dma_start(t_[f"state_v{l}"], v[:, 0, 0:n]).then_inc(S("state_out"), 16)
                if l == 0:
                    pool.wait_ge(*at("qk_ready", 0, 1))
                pool.dma_start(t_[f"state_k{l}"], k_[:, 0, 0:n]).then_inc(S("state_out"), 16)

            def ffn_rows(l):
                pool.wait_ge(*at("o_done", l, 24))
                for vec in range(2):
                    row_bc(gate_bc[:, vec, :], l, vec, 2, "ld_gate_attn")
                pool.dma_start(gbc, bc(t_["g_ffn"][l])).then_inc(S("ld_rows"), 16)
                for vec in range(2):
                    row_bc(sbc[:, vec, 0, :], l, vec, 3, "ld_rows")
                    row_bc(sbc[:, vec, 1, :], l, vec, 4, "ld_rows")

            def moe_dmas(l):
                if l == 0:
                    mod_store(1, 1)
                    pool.wait_ge(*at("hT_act", 0, 3))
                    pool.wait_ge(*at("hT_dve", 0, 3))
                    mod_cols(1)
                    pool.wait_ge(S("mod_stored"), 128)
                    pool.dma_start(gfin, bc(t_["g_final"])).then_inc(S("ld_gf"), 16)
                pool.wait_ge(*at("hT_main", l, E))
                for vec in range(2):
                    row_bc(gate_bc[:, vec, :], l, vec, 5, "ld_gate_ffn")
                pool.wait_ge(*at("rows_ready", l, 1))
                pool.wait_ge(*at("y_stored", l, 1))
                for t in range(NT):
                    for k in range(2):
                        pool.indirect_dma_start(yk[:, NT * k + t, :], None, y_d,
                                                bass.IndirectOffsetOnAxis(ap=rti[:, NT * k + t:NT * k + t + 1], axis=0)
                                                ).then_inc(S(f"ld_y{t}"), 16)

            mod_store(0, 0)
            mod_cols(0)
            cache(0)
            mod_store(0, 1)
            states(0)
            pool.wait_ge(S("zero_ready"), 1)
            pool.dma_start(y_d[E * CAP:].rearrange("r n -> (r n)").rearrange("(p c n) -> p c n", p=P, n=512),
                           zero.unsqueeze(1).to_broadcast([P, XT, 512])).then_inc(S("y_cleared"), 16)
            mod_store(1, 0)
            pool.wait_ge(*at("mod_stored", 0, 64))
            pool.wait_ge(S("y_cleared"), 16)
            ffn_rows(0)
            moe_dmas(0)
            pool.wait_ge(*at("x_moe", 0, 3))
            cache(1)
            states(1)
            ffn_rows(1)
            moe_dmas(1)
            for t in range(NT):
                pool.wait_ge(S("y_ready"), t + 1)
                dst = t_["y_prompt"] if t == 0 else t_["y_sample"][P * (t - 1):P * t, :]
                pool.dma_start(dst, yk[:, t, :]).then_inc(S("y_out"), 16)
            pool.wait_ge(S("y_out"), 16 * NT)

        steps = [(t, pr) for t in range(NT) for pr in range(8)]

        MOD_BEFORE = [(0, 4), (0, 5), (0, 6)]
        MOD_WITHIN = {i: slot for i, slot in zip(range(0, 26, 2), [(0, j) for j in range(7, 12)] + [(1, j) for j in range(8)])}
        MOD_BY_WO, MOD_BY_LOGITS, MOD_BY_RANKS = [(1, 8), (1, 9)], [(1, 10)], [(1, 11)]

        SUB_AT = (11, 19, 26)

        def pT_bank(l, i, m):
            return 4 + m if l == 0 else 4 + i % 2

        def blocks_of(t):
            return [0] if t == 0 else [1, 2, 3]

        def kcols(t):
            return slice(0, P) if t == 0 else slice(P, 4 * P)

        QK_BANK = (1, 3, 5, 6)

        def qk_groups(l):
            npair = 2 if l == 0 else 8
            out = []
            for b in (3, 0, 1, 2):
                for a in range(0, npair, 4):
                    out.append(("k", b, a, min(4, npair - a)))
                if b < 3:
                    for a in (0, 4):
                        out.append(("q", b, a, 4))
            return out

        @block.tensor
        def _(pe):
            def slot_ready(kind, l, j):
                s, u = place[(kind, l, j)]
                pe.wait_ge(w_ready[s], 16 * (u + 1))
                return s

            def mod_slot(l, j):
                s = slot_ready("mod", l, j)
                if l == 0 and j == 0:
                    pe.wait_ge(S("cs_ready"), 1)
                if j or l:
                    pe.wait_ge(*at("mod_sb", l, j))
                for k in range(KC):
                    for g in range(4):
                        mm = pe.matmul(PS[32 * g:32 * g + 32, 7, 0:P], cs[:, k, :],
                                       ring[:, s, 512 * k + P * g:512 * k + P * (g + 1)], start=(k == 0), stop=(k == KC - 1))
                mm.then_inc(S("mod_ps"), 1)

            def norm_transposes(l, t):
                pe.wait_ge(*at("xn_ready", l, t + 1))
                for half in range(2):
                    g = 2 * t + half
                    for c in range(4):
                        tr = pe.transpose(PS[:, g, P * c:P * (c + 1)], xn[:, t, 4 * half + c::KC], ident)
                    tr.then_inc(S("xn_turned"), 1)

            def project(l, kind, nslots, lhs, ready, then=None):
                for j in range(nslots):
                    s = slot_ready(kind, l, j)
                    for t in range(NT):
                        n = NT * j + t
                        if j == 0:
                            ready(t)
                        else:
                            pe.wait_ge(*at(f"{kind}_copied", l, n - NT + 1))
                        for k in range(KC):
                            mm = pe.matmul(PS[:, 2 * t, :], lhs[:, k, P * t:P * (t + 1)], ring[:, s, 512 * k:512 * (k + 1)],
                                           start=(k == 0), stop=(k == KC - 1))
                        mm.then_inc(S(f"{kind}_done"), 1)
                        if then and j == nslots - 1 and t:
                            then(t - 1)

            def hT_ready(l):
                def f(t):
                    if l == 1:
                        for u in ((0, 1), (2,), ())[t]:
                            norm_transposes(1, u)
                    pe.wait_ge(*at("hT_dve", l, t + 1))
                    pe.wait_ge(*at("hT_act", l, t + 1))
                return f

            def qk_transposes(l):
                pe.wait_ge(*at("ld_cache", l, 32))
                for n, (what, b, a, cnt) in enumerate(qk_groups(l)):
                    if b == 0 and l == 1:
                        pe.wait_ge(*at("qkv_copied", 1, 12))
                    elif b < 3 and what == "q" and l == 0:
                        pe.wait_ge(S("q_ready"), b + 1)
                    elif b < 3:
                        pe.wait_ge(*at("qk_ready", l, b + 1 - l))
                    if n >= 4:
                        pe.wait_ge(*at("qkT_dve" if n % 2 == 0 else "qkT_act", l, n // 2 - 1))
                    for c in range(cnt):
                        i = a + c
                        if what == "k":
                            src = kc[:, P * i:P * (i + 1)] if b == 3 else k_[:, b, P * i:P * (i + 1)]
                        else:
                            src = q[:, b, P * i:P * (i + 1)]
                        tr = pe.transpose(PS[:, QK_BANK[n % 4], P * c:P * (c + 1)], src, ident)
                    tr.then_inc(S("qk_turned"), 1)

            def scores(l, i):
                t, pr = steps[i]
                nk = P * len(blocks_of(t))
                if i == 0:
                    g = len(qk_groups(l))
                    pe.wait_ge(*at("qkT_dve", l, (g + 1) // 2))
                    pe.wait_ge(*at("qkT_act", l, g // 2))
                    pe.wait_ge(*at("qkv_copied", l, 9 if l == 0 else 18))
                if i >= 2:
                    pe.wait_ge(*at("p_ready", l, i - 1))
                for m in range(2):
                    mm = pe.matmul(PS[:, 2 * (i % 2) + m, 0:nk], qT[64 * m:64 * m + 64, pr, P * t:P * (t + 1)],
                                   kT[64 * m:64 * m + 64, pr // 4 if l == 0 else pr, kcols(t)], start=True, stop=True)
                mm.then_inc(S("s_done"), 1)

            def turn_p(l, i):
                t, pr = steps[i]
                pe.wait_ge(*(at("p_ready", 0, i + 1) if l == 0 else (S("a_ready"), i + 1)))
                if l == 0 and i:
                    pe.wait_ge(*at("pT_act", l, i))
                    pe.wait_ge(*at("pT_dve", l, i))
                elif l:
                    pe.wait_ge(*at("pT_act", l, max(i - 1, 0)))
                for m in range(2 if l == 0 else 1):
                    for c in range(len(blocks_of(t))):
                        tr = pe.transpose(PS[:, pT_bank(l, i, m), P * c:P * (c + 1)], pr_[:, i % 2, m, P * c:P * (c + 1)], ident)
                tr.then_inc(S("p_turned"), 1)

            def times_v(l, i):
                t, pr = steps[i]
                bl = blocks_of(t)
                pe.wait_ge(*at("pT_act", l, i + 1))
                if l == 0:
                    pe.wait_ge(*at("pT_dve", l, i + 1))
                if i or l:
                    pe.wait_ge(*at("o_copied", l, i))
                for m in range(2 if l == 0 else 1):
                    for c, b in enumerate(bl):
                        if l == 0:
                            g = 2 * (pr // 4) + m
                            out, vals = PS[:, 6, 64 * m:64 * m + 64], v[:, b, 64 * g:64 * g + 64]
                        else:
                            out, vals = PS[:, 6, 0:P], v[:, b, P * pr:P * (pr + 1)]
                        mm = pe.matmul(out, ptt[:, i % 2, m, P * c:P * (c + 1)], vals, start=(c == 0), stop=(c == len(bl) - 1))
                mm.then_inc(S("o_done"), 1)

            def attention(l):
                n = len(steps)
                for i in range(n + 3):
                    if i < n:
                        scores(l, i)
                    if 2 <= i < n + 2:
                        turn_p(l, i - 2)
                    if l == 0 and i in MOD_WITHIN:
                        mod_slot(*MOD_WITHIN[i])
                    if i >= 3:
                        times_v(l, i - 3)

            def o_transposes(l):
                for g in range(6):
                    t, half = g // 2, g % 2
                    pe.wait_ge(*(at("o_copied", 0, 8 * (t + 1)) if l == 0 else (S("o_ready"), t + 1)))
                    for c in range(4):
                        tr = pe.transpose(PS[:, g, P * c:P * (c + 1)], q[:, t, 4 * half + c::KC], ident)
                    tr.then_inc(S("o_turned"), 1)

            def oT_ready(l):
                def f(t):
                    pe.wait_ge(*at("oT_dve", l, t + 1))
                    pe.wait_ge(*at("oT_act", l, t + 1))
                return f

            def logits(l, t):
                pe.wait_ge(*at("h_ready", l, t + 1))
                B = (1, 3) if t % 2 == 0 else (5, 7)
                if t == 2:
                    pe.wait_ge(*at("hr_dve", l, 1))
                    pe.wait_ge(*at("hr_act", l, 1))
                for half in range(2):
                    for c in range(4):
                        tr = pe.transpose(PS[:, B[half], P * c:P * (c + 1)],
                                          hperm[:, t, P * (4 * half + c):P * (4 * half + c + 1)], ident)
                    tr.then_inc(S("hr_turned"), 1)
                pe.wait_ge(*at("hr_dve", l, t + 1))
                pe.wait_ge(*at("hr_act", l, t + 1))
                for k in range(KC):
                    mm = pe.matmul(PS[:, 6, E * t:E * (t + 1)], hTr[:, t % 2, k // 4, P * (k % 4):P * (k % 4 + 1)], wr[:, k, :],
                                   start=(k == 0), stop=(k == KC - 1))
                mm.then_inc(S("logits"), 1)

            def ranks(l):
                pe.wait_ge(*at("oh_ready", l, 1))
                pe.matmul(PS[:, 2, 0:48], upper, R(0, 48), start=True, stop=True)
                pe.matmul(PS[:, 2, 64:112], ones, R(0, 48), start=True, stop=True).then_inc(S("ranks"), 1)

            def experts(l):
                base = moe_base[l]

                def tag(b):
                    return "more" if b else "main"

                def pick_pair(nth):
                    pe.wait_ge(*at("one_hot_main", l, nth))
                    for k in range(KC):
                        for t in range(NT):
                            mm = pe.matmul(PS[:, 0 if k < 4 else 6, P * (k % 4):P * (k % 4 + 1)], hperm[:, t, P * k:P * (k + 1)],
                                           hotp[:, t, :], start=(t == 0), stop=(t == NT - 1))
                    mm.then_inc(S("x_picked_main"), 1)

                def pick_further(nth):
                    pe.wait_ge(*at("one_hot_more", l, nth))
                    for k in range(KC):
                        for t in range(NT):
                            mm = pe.matmul(PS[:, 4, CAP * k:CAP * (k + 1)], hperm[:, t, P * k:P * (k + 1)], hotx[:, t, :],
                                           start=(t == 0), stop=(t == NT - 1))
                    mm.then_inc(tile_sem("x_picked_more", l), 1)

                def weights(m, i, r):
                    s = 3 * (r % DEEP) + m
                    pe.wait_ge(w_ready[s], 16 * (base[s] + 2 * i + r // DEEP + 1))

                def gate_up(b, i, r, nth):
                    pe.wait_ge(*(at("xT_more", l, nth) if b else at("xT_main", l, 3 * i + r // 2 + 1)))
                    weights(0, i, r)
                    weights(1, i, r)
                    w = wE[r % DEEP]
                    for k in range(KC):
                        for g in range(2):
                            mm = pe.matmul(PS[64 * g:64 * g + 64, 4 * b + 1, :],
                                           xTx[:, k, :] if b else xTp[:, k, CAP * (r % 2):CAP * (r % 2 + 1)],
                                           w[:, 0:2, 512 * k + 256 * g:512 * k + 256 * (g + 1)],
                                           start=(k == 0), stop=(k == KC - 1))
                    mm.then_inc(tile_sem(f"gu_{tag(b)}", l), 1)

                def turn_h(b, nth):
                    pe.wait_ge(*at(f"h_{tag(b)}", l, nth))
                    for c in range(2):
                        tr = pe.transpose(PS[:, 4 if b else 2, P * c:P * (c + 1)], hE[:, b, P * c:P * (c + 1)], ident)
                    tr.then_inc(tile_sem(f"h_turned_{tag(b)}", l), 1)

                def down(b, i, r, nth):
                    weights(2, i, r)
                    pe.wait_ge(*at(f"hT_{tag(b)}", l, nth))
                    pe.wait_ge(*at(f"y_{tag(b)}", l, nth))
                    w = wE[r % DEEP][:, 2, :]
                    for f in range(4):
                        for g in range(2):
                            mm = pe.matmul(PS[64 * g:64 * g + 64, 4 * b + 3, :],
                                           hTt[:, b, f % 2, 64 * (f // 2):64 * (f // 2) + 64],
                                           w[:, 1024 * f + 512 * g:1024 * f + 512 * (g + 1)], start=(f == 0), stop=(f == 3))
                    mm.then_inc(tile_sem(f"down_{tag(b)}", l), 1)

                pick_pair(1)
                pe.wait_ge(*at("nx_ready", l, 1))
                more = pe.alloc_register(f"pe_more{l}")
                pe.reg_mov(more, 0)

                def expert(i, r):
                    e = 6 * i + r
                    nx = pe.value_load(nxi[0:1, bass.ds(e, 1)], min_val=0, max_val=5)
                    with pe.If(nx > 0):
                        with pe.Fori(0, nx):
                            pe.reg_add(more, more, 1)
                            nth = pe.snap(more)
                            pick_further(nth)
                            gate_up(1, i, r, nth)
                            turn_h(1, nth)
                            down(1, i, r, nth)
                        pe.nop()
                    with pe.Else():
                        pe.nop()
                    gate_up(0, i, r, e + 1)
                    if r % 2 and not (isinstance(e, int) and e == E - 1):
                        pick_pair(3 * i + (r + 3) // 2)
                    if not (isinstance(e, int) and e == 0):
                        down(0, i, r - 1, e)
                    turn_h(0, e + 1)

                expert(0, 0)
                with pe.Fori(0, (E - 1) // 6) as i:
                    for r in range(1, 7):
                        expert(i, r)
                for r in range(1 + 6 * ((E - 1) // 6), E):
                    expert(0, r)
                down(0, 0, E - 1, E)

            for l in range(2):
                if l == 0:
                    mod_slot(0, 0)
                    mod_slot(0, 1)
                    pe.wait_ge(S("ld_const"), 16)
                    for t in range(NT):
                        norm_transposes(0, t)
                    mod_slot(0, 2)
                    mod_slot(0, 3)
                project(l, "qkv", 3 if l == 0 else 6, hT, hT_ready(l))
                if l == 0:
                    for slot in MOD_BEFORE:
                        mod_slot(*slot)
                qk_transposes(l)
                attention(l)
                o_transposes(l)
                if l == 0:
                    for slot in MOD_BY_WO:
                        mod_slot(*slot)
                project(l, "wo", 2, oT, oT_ready(l), lambda t, l=l: logits(l, t))
                if l == 0:
                    pe.wait_ge(*at("hr_act", 0, 2))
                    for slot in MOD_BY_LOGITS:
                        mod_slot(*slot)
                logits(l, 2)
                if l == 0:
                    for slot in MOD_BY_RANKS:
                        mod_slot(*slot)
                ranks(l)
                experts(l)

        @block.vector
        def _(dve):
            chain = [0]

            def link(ins):
                chain[0] += 1
                ins.then_inc(S("dve_chain"), 1)
                dve.wait_ge(S("dve_chain"), chain[0])

            def done(ins, sem, n):
                sem = S(sem) if isinstance(sem, str) else sem
                ins.then_inc(sem, 1)
                dve.wait_ge(sem, n)

            roots = [0]

            def rstd(n, inv_n, o=0):
                roots[0] += 1
                dve.tensor_scalar(rs[:, o:o + n], ss[:, o:o + n], inv_n, EPS, ALU.mult, ALU.add).then_inc(S("var_ready"), 1)
                dve.wait_ge(S("std_ready"), roots[0])
                link(dve.reciprocal(rs[:, o:o + n], rs[:, o:o + n]))

            def norm_attn(l, t):
                dve.wait_ge(*at("sq_attn", l, t + 1))
                rstd(1, 1.0 / D, t)
                dve.tensor_scalar(xn[:, t, :], x[:, t, :], rs[:, t:t + 1], None, ALU.mult).then_inc(S("xn_ready"), 1)

            def cols(l):
                dve.wait_ge(*at("ld_cols", l, 32))
                dve.wait_ge(S("ld_par"), 16 * 11)
                for vec in range(2):
                    ins = dve.scalar_tensor_tensor(a1[:, vec, :], colp[:, vec, 1, :], 1.0, gcol[:, l, :], ALU.add, ALU.mult)
                ins.then_inc(S("a1_ready" if l == 0 else "a1_ready_b"), 1)
                dve.wait_ge(S("a1_ready" if l == 0 else "a1_ready_b"), 1)

            def hT_even(l, t):
                vec = min(t, 1)
                dve.wait_ge(*at("xn_turned", l, 2 * t + 1))
                for c in range(4):
                    ins = dve.tensor_scalar(hT[:, c, P * t:P * (t + 1)], PS[:, 2 * t, P * c:P * (c + 1)],
                                            a1[:, vec, c:c + 1], colp[:, vec, 0, c:c + 1], ALU.mult, ALU.add)
                ins.then_inc(S("hT_dve"), 1)

            def rope_tables():
                link(dve.tensor_scalar(gqk[:, 0, :], gqk[:, 0, :], 0.125, None, ALU.mult))
                for w in range(2):
                    for t in range(2):
                        cos, sin = (cf[:, o + 64 * t:o + 64 * (t + 1)] for o in (C_COS, C_SIN))
                        dve.tensor_tensor(rope_qk[:, w, 0, t, :], cos, gqk[:, w, :], ALU.mult)
                        g4 = gqk[:, w, :].rearrange("p (r f d) -> p r f d", r=2, f=2)
                        s4 = sin.rearrange("p (r f d) -> p r f d", r=2, f=2)
                        o4 = rope_qk[:, w, 1, t, :].rearrange("p (r f d) -> p r f d", r=2, f=2)
                        for f in range(2):
                            ins = dve.tensor_tensor(o4[:, :, f, :], s4[:, :, f, :], g4[:, :, 1 - f, :], ALU.mult)
                link(ins)

            def by_head(ap, nh):
                return ap.rearrange("p (h d) -> p h d", h=nh)

            def rope(dst, nh, cos, sin, end=link):
                n = nh * 64
                dve.tensor_tensor(by_head(tmp1[:, 0:n], nh), by_head(dst, nh),
                                  cos.unsqueeze(1).to_broadcast([P, nh, 64]), ALU.mult)
                s5 = dst.rearrange("p (h f d) -> p h f d", h=2 * nh, f=2)
                t5 = tmp2[:, 0:n].rearrange("p (h f d) -> p h f d", h=2 * nh, f=2)
                for rc in range(2):
                    for f in range(2):
                        sn = sin[:, 32 * rc + 16 * f:32 * rc + 16 * f + 16]
                        ins = dve.tensor_tensor(t5[:, rc::2, f, :], s5[:, rc::2, 1 - f, :],
                                                sn.unsqueeze(1).to_broadcast([P, nh, 16]), ALU.mult)
                link(ins)
                end(dve.tensor_tensor(dst, tmp1[:, 0:n], tmp2[:, 0:n], ALU.add))

            def norm_rope_a(w, src, nh, name):
                dve.wait_ge(S("q_squared" if w == 0 else "k_squared"), NT)
                link(dve.tensor_reduce(ss[:, 0:NT * nh], by_head(sqb[:, 3072 * w:3072 * w + NT * nh * 64], NT * nh), X, ALU.add))
                rstd(NT * nh, 1.0 / 64)
                for t in range(NT):
                    end = lambda ins, t=t: done(ins, name, t + 1)
                    a = src[:, t, 0:nh * 64]
                    link(dve.tensor_tensor(by_head(a, nh), by_head(a, nh),
                                           rs[:, nh * t:nh * (t + 1)].unsqueeze(2).to_broadcast([P, nh, 64]), ALU.mult))
                    if t == 0:
                        end(dve.tensor_tensor(by_head(a, nh), by_head(a, nh),
                                              gqk[:, w, :].unsqueeze(1).to_broadcast([P, nh, 64]), ALU.mult))
                    else:
                        rope(a, nh, rope_qk[:, w, 0, t - 1, :], rope_qk[:, w, 1, t - 1, :], end)

            def qk_norm_rope(l):
                if l == 0:
                    norm_rope_a(0, q, 16, "q_ready")
                    norm_rope_a(1, k_, 4, "qk_ready")
                    return
                for w, src in enumerate((q, k_)):
                    dve.wait_ge(*at("qkv_copied", 1, 6 * (w + 1)))
                    for t in (1, 2):
                        cos, sin = (cf[:, o + 64 * (t - 1):o + 64 * t] for o in (C_COS, C_SIN))
                        rope(src[:, t, :], 16, cos, sin,
                             (lambda ins, t=t: done(ins, "qk_ready", NT + t)) if w else link)

            def evac_group(l, n, what, b, a, cnt, copy):
                src = PS[:, QK_BANK[n % 4], 0:P * cnt].rearrange("p (c n) -> p c n", c=cnt)
                dst = (kT if what == "k" else qT)[:, a:a + cnt, P * b:P * (b + 1)]
                return copy(dst, src)

            def qk_even(l):
                for n, (what, b, a, cnt) in enumerate(qk_groups(l)):
                    if n % 2 == 0:
                        dve.wait_ge(*at("qk_turned", l, n + 1))
                        evac_group(l, n, what, b, a, cnt, dve.tensor_copy).then_inc(S("qkT_dve"), 1)

            def row_max(l, i):
                t, pr = steps[i]
                nk = P * len(blocks_of(t))
                dve.wait_ge(*at("s_done", l, i + 1))
                dve.tensor_reduce(nm[:, i % 2, :], PS[:, 2 * (i % 2):2 * (i % 2) + 2, 0:nk], X, ALU.max,
                                  negate=True).then_inc(S("nm_ready"), 1)

            def after_exp(l, i):
                t, pr = steps[i]
                nk = P * len(blocks_of(t))
                r = rsm[:, i % 4, :]
                dve.wait_ge(*at("p_ready", l, i + 1))
                if l == 0:
                    if i >= 4:
                        dve.wait_ge(S("o_copied"), i - 3)
                    dve.reciprocal(r, sm[:, i % 4, :]).then_inc(S("rsm_ready"), 1)
                    return
                link(dve.reciprocal(r, sm[:, i % 4, :]))
                dve.tensor_tensor(r[:, 1:2], r[:, 1:2], small[:, 4:5], ALU.mult)
                link(dve.tensor_scalar(pr_[:, i % 2, 0, 0:nk], pr_[:, i % 2, 0, 0:nk], r[:, 0:1], None, ALU.mult))
                dve.scalar_tensor_tensor(pr_[:, i % 2, 0, 0:nk], pr_[:, i % 2, 1, 0:nk], r[:, 1:2],
                                         pr_[:, i % 2, 0, 0:nk], ALU.mult, ALU.add).then_inc(S("a_ready"), 1)

            def take_pT(i):
                t, pr = steps[i]
                nk = P * len(blocks_of(t))
                dve.wait_ge(*at("p_turned", 0, i + 1))
                if i >= 2:
                    dve.wait_ge(*at("o_done", 0, i - 1))
                dve.tensor_copy(ptt[:, i % 2, 0, 0:nk], PS[:, 4, 0:nk]).then_inc(S("pT_dve"), 1)

            def take_o(l, i):
                t, pr = steps[i]
                dve.wait_ge(*at("o_done", l, i + 1))
                if l == 0:
                    dst = q[:, t, :].rearrange("p (m f d) -> p m f d", m=2, f=2)[:, pr // 4, :, 64 * (pr % 4):64 * (pr % 4) + 64]
                    src = PS[:, 6, 0:P].rearrange("p (f d) -> p f d", f=2)
                    dve.wait_ge(S("rsm_ready"), i + 1)
                    dve.tensor_tensor(dst, src, rsm[:, i % 4, :].unsqueeze(2).to_broadcast([P, 2, 64]),
                                      ALU.mult).then_inc(S("o_copied"), 1)
                else:
                    dve.tensor_copy(q[:, t, P * pr:P * (pr + 1)], PS[:, 6, 0:P]).then_inc(S("o_copied"), 1)

            def sub_norm(t):
                dve.wait_ge(S("o_squared"), 8 * (t + 1))
                rstd(8, 1.0 / P, 8 * t)
                for h in range(8):
                    ins = dve.scalar_tensor_tensor(q[:, t, P * h:P * (h + 1)], q[:, t, P * h:P * (h + 1)],
                                                   rs[:, 8 * t + h:8 * t + h + 1], gsub[:], ALU.mult, ALU.mult)
                done(ins, "o_ready", t + 1)

            def attention(l):
                n = len(steps)
                for i in range(n + 3):
                    if i < n:
                        row_max(l, i)
                    if l == 0 and 2 <= i < n + 2:
                        take_pT(i - 2)
                    if 1 <= i <= n:
                        after_exp(l, i - 1)
                    if i >= 3:
                        take_o(l, i - 3)
                    if l == 1 and i in SUB_AT:
                        sub_norm(SUB_AT.index(i))

            def oT_even(l):
                dve.wait_ge(*at("state_out", l, 32))
                for g in range(0, 6, 2):
                    dve.wait_ge(*at("o_turned", l, g + 1))
                    dve.tensor_copy(oT[:, 0:4, P * (g // 2):P * (g // 2 + 1)],
                                    PS[:, g, :].rearrange("p (c n) -> p c n", c=4)).then_inc(S("oT_dve"), 1)

            def attn_to_ffn(l):
                dve.wait_ge(*at("ld_gate_attn", l, 32))
                for j in range(2):
                    if j == 1:
                        dve.wait_ge(*at("ld_rows", l, 80))
                        for vec in range(2):
                            ins = dve.scalar_tensor_tensor(sbc[:, vec, 1, :], sbc[:, vec, 1, :], 1.0, gbc, ALU.add, ALU.mult)
                        link(ins)
                    for t in range(NT):
                        n = NT * j + t
                        dve.wait_ge(*at("wo_done", l, n + 1))
                        done(dve.tensor_tensor(tmp2[:, 0:512], PS[:, 2 * t, :], gate_bc[:, min(t, 1), 512 * j:512 * (j + 1)],
                                               ALU.mult), *at("wo_copied", l, n + 1))
                        done(dve.tensor_tensor(x[:, t, 512 * j:512 * (j + 1)], x[:, t, 512 * j:512 * (j + 1)], tmp2[:, 0:512],
                                               ALU.add), *at("x_attn", l, n + 1))
                        if j == 1:
                            norm_ffn(l, t)

            def norm_ffn(l, t):
                dve.wait_ge(*at("sq_ffn", l, t + 1))
                rstd(1, 1.0 / D, t)
                vec = min(t, 1)
                out = hperm[:, t, :].rearrange("p (k a) -> p a k", k=KC)
                link(dve.scalar_tensor_tensor(tmp1[:], x[:, t, :], rs[:, t:t + 1], sbc[:, vec, 1, :], ALU.mult, ALU.mult))
                done(dve.tensor_tensor(out, tmp1.rearrange("p (a k) -> p a k", k=KC),
                                       sbc[:, vec, 0, :].rearrange("p (a k) -> p a k", k=KC), ALU.add), *at("h_ready", l, t + 1))
                dve.wait_ge(*at("hr_turned", l, 2 * t + 1))
                if t == 2:
                    dve.wait_ge(*at("logits", l, 1))
                dve.tensor_copy(hTr[:, t % 2, 0, :], PS[:, 1 if t % 2 == 0 else 5, :]).then_inc(S("hr_dve"), 1)

            def one_hot(out, ranks):
                return dve.tensor_tensor(out, cf[:, C_IOTA:C_IOTA + CAP].unsqueeze(1).unsqueeze(1).to_broadcast(out.shape),
                                         ranks.unsqueeze(3).to_broadcast(out.shape), ALU.is_equal)

            def hot_pair(l, i):
                dve.tensor_copy(rkp[:], rkm[:, bass.ds(2 * NT * i, 2 * NT)]).then_inc(S("rank_main"), 1)
                dve.wait_ge(*at("rank_main", l, i + 1))
                one_hot(hotp.rearrange("p t (e n) -> p e t n", e=2),
                        rkp[:].rearrange("p (e t) -> p e t", e=2)).then_inc(S("one_hot_main"), 1)

            def route(l):
                dve.wait_ge(*at("logits", l, NT))
                oh = R(0, 48)
                sg_, m_ = R(48, 48), R(96, 48)
                p6 = R(144, 72).rearrange("p (g c) -> p g c", g=12)
                t3 = lambda ap, n: ap.rearrange("p (t e) -> p t e", t=n)
                oh1, oh2 = R(216, 48), R(264, 48)
                cand = R(312, 48)
                tot = R(640, 48)
                cnt, c1 = R(688, 16), R(704, 16)
                gs, gm, ing, t0 = R(360, 12), R(372, 3), R(375, 12), R(387, 12)
                vv = R(400, 6)
                cc = R(406, 6)
                sm3, rk = R(412, 3), R(416, 48)
                rr, bs, jj, tl = R(464, 6), R(470, 6), R(476, 6), R(482, 6)
                pref = R(490, 64)
                cmp_ = R(556, 80)
                dve.tensor_tensor(t3(sg_, 3), t3(PS[:, 6, 0:48], 3), br[:].unsqueeze(1).to_broadcast([P, 3, E]),
                                  ALU.add).then_inc(S("lg_ready"), 1)
                dve.wait_ge(*at("sig_ready", l, 1))
                s4 = sg_.rearrange("p (g c) -> p g c", g=12)
                dve.tensor_tensor(p6[:, :, 0:3], s4[:, :, 0:3], s4[:, :, 1:4], ALU.add)
                dve.tensor_tensor(p6[:, :, 3:5], s4[:, :, 0:2], s4[:, :, 2:4], ALU.add)
                link(dve.tensor_tensor(p6[:, :, 5:6], s4[:, :, 0:1], s4[:, :, 3:4], ALU.add))
                link(dve.tensor_reduce(gs, p6, X, ALU.max))
                link(dve.tensor_reduce(gm, t3(gs, 3), X, ALU.max))
                link(dve.tensor_tensor(t3(t0, 3), t3(gs, 3), gm.unsqueeze(2).to_broadcast([P, 3, NG]), ALU.is_equal))
                link(dve.tensor_tensor(t3(t0, 3), t3(t0, 3),
                                       cf[:, C_REVG:C_REVG + NG].unsqueeze(1).to_broadcast([P, 3, NG]), ALU.mult))
                link(dve.tensor_reduce(gm, t3(t0, 3), X, ALU.max))
                link(dve.tensor_tensor(t3(ing, 3), t3(t0, 3), gm.unsqueeze(2).to_broadcast([P, 3, NG]), ALU.is_equal))
                dve.tensor_scalar(t0, ing, 4.0, -4.0, ALU.mult, ALU.add)
                link(dve.tensor_tensor(t3(m_, 12), s4, ing.unsqueeze(2).to_broadcast([P, 12, 4]), ALU.mult))
                link(dve.tensor_tensor(t3(m_, 12), t3(m_, 12), t0.unsqueeze(2).to_broadcast([P, 12, 4]), ALU.add))
                for k, o in enumerate((oh1, oh2)):
                    vk, ck = vv[:, 3 * k:3 * k + 3], cc[:, 3 * k:3 * k + 3]
                    link(dve.tensor_reduce(vk, t3(m_, 3), X, ALU.max))
                    link(dve.tensor_tensor(t3(cand, 3), t3(m_, 3), vk.unsqueeze(2).to_broadcast([P, 3, E]), ALU.is_equal))
                    link(dve.tensor_tensor(t3(cand, 3), t3(cand, 3),
                                           cf[:, C_REVE:C_REVE + E].unsqueeze(1).to_broadcast([P, 3, E]), ALU.mult))
                    link(dve.tensor_reduce(ck, t3(cand, 3), X, ALU.max))
                    link(dve.tensor_tensor(t3(o, 3), t3(cand, 3), ck.unsqueeze(2).to_broadcast([P, 3, E]), ALU.is_equal))
                    if k == 0:
                        link(dve.scalar_tensor_tensor(m_, o, -8.0, m_, ALU.mult, ALU.add))
                dve.tensor_tensor(oh, oh1, oh2, ALU.add).then_inc(S("oh_ready"), 1)
                dve.wait_ge(*at("ranks", l, 1))
                dve.tensor_copy(rk, PS[:, 2, 0:48])
                link(dve.tensor_copy(tot, PS[:, 2, 64:112]))
                dve.tensor_tensor(rk[:, 16:32], rk[:, 16:32], tot[:, 0:16], ALU.add)
                link(dve.tensor_tensor(c1, tot[:, 0:16], tot[:, 16:32], ALU.add))
                dve.tensor_tensor(rk[:, 32:48], rk[:, 32:48], c1, ALU.add)
                link(dve.tensor_tensor(cnt, c1, tot[:, 32:48], ALU.add))
                link(dve.scalar_tensor_tensor(tot, rk, 1.0, oh, ALU.add, ALU.mult))
                link(dve.tensor_scalar(rkm[:].rearrange("p (e t) -> p t e", t=NT), t3(tot, 3), -1.0, None, ALU.add))
                hot_pair(l, 0)
                dve.memset(pref, 0.0)
                thr = cf[:, C_THR:C_THR + 5]
                c16 = cmp_.rearrange("p (e c) -> p e c", e=E)
                link(dve.tensor_tensor(c16, cnt.unsqueeze(2).to_broadcast([P, E, 5]),
                                       thr.unsqueeze(1).to_broadcast([P, E, 5]), ALU.is_gt))
                link(dve.tensor_reduce(pref[:, 16:32], c16, X, ALU.add))
                dve.tensor_copy(nxi[:], pref[:, 16:32]).then_inc(S("nx_ready"), 1)

            def rows(l):
                oh = R(0, 48)
                t3 = lambda ap, n: ap.rearrange("p (t e) -> p t e", t=n)
                oh1, oh2 = R(216, 48), R(264, 48)
                cand = R(312, 48)
                vv, cc = R(400, 6), R(406, 6)
                sm3, rk = R(412, 3), R(416, 48)
                rr, bs, jj, tl = R(464, 6), R(470, 6), R(476, 6), R(482, 6)
                pref, cmp_ = R(490, 64), R(556, 80)
                thr = cf[:, C_THR:C_THR + 5]
                link(dve.tensor_tensor(sm3, vv[:, 0:3], vv[:, 3:6], ALU.add))
                link(dve.reciprocal(sm3, sm3))
                for k in range(2):
                    dve.tensor_tensor(small[:, 8 + 3 * k:11 + 3 * k], vv[:, 3 * k:3 * k + 3], sm3, ALU.mult)
                link(dve.tensor_scalar(cc, cc, -1.0, float(E), ALU.mult, ALU.add))
                for n, step in enumerate((1, 2, 4, 8)):
                    a, b = 32 * (n % 2), 32 * ((n + 1) % 2)
                    link(dve.tensor_tensor(pref[:, b + 16:b + 32], pref[:, a + 16:a + 32],
                                           pref[:, a + 16 - step:a + 32 - step], ALU.add))
                dve.wait_ge(*at("nx_ready", l, 1))
                link(dve.tensor_tensor(pref[:, 16:32], pref[:, 16:32], nxi[:], ALU.subtract))
                for k, o in enumerate((oh1, oh2)):
                    link(dve.tensor_tensor(cand, o, rk, ALU.mult))
                    link(dve.tensor_reduce(rr[:, 3 * k:3 * k + 3], t3(cand, 3), X, ALU.add))
                    link(dve.tensor_tensor(t3(cand, 3), t3(o, 3), pref[:, 16:32].unsqueeze(1).to_broadcast([P, 3, E]), ALU.mult))
                    link(dve.tensor_reduce(bs[:, 3 * k:3 * k + 3], t3(cand, 3), X, ALU.add))
                c6 = cmp_[:, 0:30].rearrange("p (e c) -> p e c", e=6)
                link(dve.tensor_tensor(c6, rr.unsqueeze(2).to_broadcast([P, 6, 5]),
                                       thr.unsqueeze(1).to_broadcast([P, 6, 5]), ALU.is_ge))
                link(dve.tensor_reduce(jj, c6, X, ALU.add))
                link(dve.scalar_tensor_tensor(tl, jj, float(E - 1), bs, ALU.add, ALU.add))
                dve.tensor_scalar(bs, jj, 0.0, None, ALU.is_equal)
                link(dve.tensor_tensor(cc, cc, tl, ALU.subtract))
                link(dve.tensor_tensor(cc, cc, bs, ALU.mult))
                link(dve.tensor_tensor(tl, tl, cc, ALU.add))
                link(dve.scalar_tensor_tensor(rr, jj, -float(CAP), rr, ALU.mult, ALU.add))
                link(dve.scalar_tensor_tensor(tl, tl, float(CAP), rr, ALU.mult, ALU.add))
                dve.tensor_copy(rti[:], tl).then_inc(S("rows_ready"), 1)

            def experts(l):
                more = dve.alloc_register(f"dve_more{l}")
                dve.reg_mov(more, 0)
                seen = dve.alloc_register(f"dve_seen{l}")
                dve.reg_mov(seen, 0)

                def tag(b):
                    return "more" if b else "main"

                def take_pair(nth):
                    dve.wait_ge(*at("x_picked_main", l, nth))
                    dve.tensor_copy(xTp[:, 0:4, :], PS[:, 0, :].rearrange("p (k n) -> p k n", k=4))
                    dve.tensor_copy(xTp[:, 4:8, :], PS[:, 6, :].rearrange("p (k n) -> p k n", k=4)).then_inc(S("xT_main"), 1)

                def take_further(nth):
                    dve.wait_ge(*at("x_picked_more", l, nth))
                    dve.tensor_copy(xTx, PS[:, 4, :].rearrange("p (k n) -> p k n", k=KC)).then_inc(tile_sem("xT_more", l), 1)

                def gated(b, nth):
                    dve.wait_ge(*at(f"silu_{tag(b)}", l, nth))
                    dve.tensor_tensor(hE[:, b, :], sg[:, b, :], PS[:, 4 * b + 1, 256:512],
                                      ALU.mult).then_inc(tile_sem(f"h_{tag(b)}", l), 1)

                def take_hT(b, nth):
                    dve.wait_ge(*at(f"h_turned_{tag(b)}", l, nth))
                    dve.tensor_copy(hTt[:, b],
                                    PS[:, 4 if b else 2, 0:256].rearrange("p (c n) -> p c n", c=2)).then_inc(tile_sem(f"hT_{tag(b)}", l), 1)

                def expert(i, par, left=2):
                    e = 2 * i + par
                    nx = dve.value_load(nxi[0:1, bass.ds(e, 1)], min_val=0, max_val=5)
                    with dve.If(nx > 0):
                        dve.tensor_copy(rkx[:], rkm[:, bass.ds(NT * e, NT)]).then_inc(tile_sem("rank_more", l), 1)
                        dve.reg_add(seen, seen, 1)
                        with dve.Fori(0, nx):
                            reg = dve.snap(more)
                            dve.wait_ge(tile_sem("rank_more", l), dve.snap(seen))
                            dve.tensor_scalar(rkx[:], rkx[:], -float(CAP), None, ALU.add).then_inc(tile_sem("rank_more", l), 1)
                            dve.reg_add(seen, seen, 1)
                            dve.wait_ge(tile_sem("rank_more", l), dve.snap(seen))
                            one_hot(hotx.unsqueeze(1), rkx[:].unsqueeze(1)).then_inc(tile_sem("one_hot_more", l), 1)
                            take_further(reg + 1)
                            gated(1, reg + 1)
                            take_hT(1, reg + 1)
                            dve.reg_add(more, more, 1)
                        dve.nop()
                    with dve.Else():
                        dve.nop()
                    gated(0, e + 1)
                    if par and left >= 1:
                        take_pair(i + 2)
                    if par and left >= 2:
                        hot_pair(l, i + 2)
                    take_hT(0, e + 1)

                take_pair(1)
                hot_pair(l, 1)
                expert(0, 0)
                rows(l)
                expert(0, 1)
                with dve.Fori(1, E // 2 - 2) as i:
                    expert(i, 0)
                    expert(i, 1)
                for i in (E // 2 - 2, E // 2 - 1):
                    expert(i, 0, E // 2 - 1 - i)
                    expert(i, 1, E // 2 - 1 - i)

            def combine(l, t):
                dve.wait_ge(*at("y_scaled", l, t + 1))
                link(dve.scalar_tensor_tensor(yk[:, t, :], yk[:, NT + t, :], small[:, 11 + t:12 + t],
                                              yk[:, t, :], ALU.mult, ALU.add))
                link(dve.tensor_tensor(yk[:, t, :], yk[:, t, :], gate_bc[:, min(t, 1), :], ALU.mult))
                done(dve.tensor_tensor(x[:, t, :], x[:, t, :], yk[:, t, :], ALU.add), *at("x_moe", l, t + 1))

            def last_norm(t):
                dve.wait_ge(S("sq_final"), t + 1)
                rstd(1, 1.0 / D, t)
                dve.scalar_tensor_tensor(yk[:, t, :], x[:, t, :], rs[:, t:t + 1], gfin,
                                         ALU.mult, ALU.mult).then_inc(S("y_ready"), 1)

            dve.memset(small[:], 0.0).then_inc(S("small_zero"), 1)
            dve.wait_ge(S("small_zero"), 1)
            dve.wait_ge(S("ld_x"), 32)
            for t in range(NT):
                norm_attn(0, t)
            cols(0)
            for t in range(NT):
                hT_even(0, t)
            lam0 = 0.8 - 0.6 * float(np.exp(-0.3))
            for i in range(2):
                link(dve.tensor_tensor(lamv[:, 2 * i, :], lamv[:, 2 * i, :], lamv[:, 2 * i + 1, :], ALU.mult))
                link(dve.tensor_reduce(small[:, i:i + 1], lamv[:, 2 * i, :], X, ALU.add))
            dve.tensor_scalar(gsub[:], gsub[:], 1.0 - lam0, None, ALU.mult).then_inc(S("lam_dots"), 1)
            dve.wait_ge(S("lam_exp"), 1)
            link(dve.tensor_tensor(small[:, 4:5], small[:, 3:4], small[:, 2:3], ALU.subtract))
            link(dve.tensor_scalar(small[:, 4:5], small[:, 4:5], -lam0, None, ALU.add))
            rope_tables()
            qk_norm_rope(0)
            qk_even(0)
            attention(0)
            oT_even(0)
            attn_to_ffn(0)
            route(0)
            experts(0)
            cols(1)
            dve.wait_ge(*at("ld_gate_ffn", 0, 32))
            for t in range(NT + 2):
                if t < NT:
                    combine(0, t)
                if 1 <= t <= NT:
                    norm_attn(1, t - 1)
                if t >= 2:
                    hT_even(1, t - 2)
            qk_norm_rope(1)
            qk_even(1)
            attention(1)
            oT_even(1)
            attn_to_ffn(1)
            route(1)
            experts(1)
            dve.wait_ge(*at("ld_gate_ffn", 1, 32))
            dve.wait_ge(S("ld_gf"), 16)
            for t in range(NT + 1):
                if t < NT:
                    combine(1, t)
                if t >= 1:
                    last_norm(t - 1)

        @block.scalar
        def _(act):
            def square(tag, dst, t):
                act.activation(dst, x[:, t, :], ACT.Square, accum_out=ss[:, t:t + 1]).then_inc(S(f"sq_{tag}"), 1)
                root(1, t)

            def scale_y(l, t):
                act.wait_ge(*at(f"ld_y{t}", l, 32))
                act.activation(yk[:, t, :], yk[:, t, :], ACT.Identity, scale=small[:, 8 + t:9 + t]).then_inc(S("y_scaled"), 1)

            roots = [0]

            def root(n, o=0):
                roots[0] += 1
                act.wait_ge(S("var_ready"), roots[0])
                act.activation(rs[:, o:o + n], rs[:, o:o + n], ACT.Sqrt).then_inc(S("std_ready"), 1)

            def take_mod(l, j):
                if l == 1 and j in (0, 3):
                    act.wait_ge(S("mod_stored"), 32 if j == 0 else 64)
                act.wait_ge(*at("mod_ps", l, j + 1))
                act.copy(modsb[:, j, :], PS[:, 7, 0:P]).then_inc(S("mod_sb"), 1)

            def hT_odd(l):
                act.wait_ge(S("a1_ready" if l == 0 else "a1_ready_b"), 1)
                for g in range(1, 6, 2):
                    t = g // 2
                    vec = min(t, 1)
                    act.wait_ge(*at("xn_turned", l, g + 1))
                    for c in range(4):
                        ins = act.activation(hT[:, 4 + c, P * t:P * (t + 1)], PS[:, g, P * c:P * (c + 1)], ACT.Identity,
                                             scale=a1[:, vec, 4 + c:5 + c], bias=colp[:, vec, 0, 4 + c:5 + c])
                    ins.then_inc(S("hT_act"), 1)

            def take_qkv(l, js):
                for j in js:
                    for t in range(NT):
                        act.wait_ge(*at("qkv_done", l, NT * j + t + 1))
                        src = PS[:, 2 * t, :]
                        if j < 2 and l == 0:
                            ins = act.copy(q[:, t, 512 * j:512 * (j + 1)].rearrange("p (r f d) -> p f r d", r=4, f=2),
                                           src.rearrange("p (f r d) -> p f r d", f=2, r=4))
                        elif j < 2:
                            ins = act.mul(q[:, t, 512 * j:512 * (j + 1)], src, 0.125)
                        elif l == 0:
                            act.copy(k_[:, t, 0:256], src[:, 0:256])
                            ins = act.copy(v[:, t, 0:256], src[:, 256:512])
                        elif j < 4:
                            ins = act.copy(k_[:, t, 512 * (j - 2):512 * (j - 1)], src)
                        else:
                            ins = act.copy(v[:, t, 512 * (j - 4):512 * (j - 3)], src)
                        ins.then_inc(S("qkv_copied"), 1)

            def square_heads(name, src, nh, o, copied):
                act.wait_ge(S("qkv_copied"), copied)
                for t in range(NT):
                    n = nh * 64
                    act.activation(sqb[:, o + n * t:o + n * (t + 1)], src[:, t, 0:n], ACT.Square).then_inc(S(name), 1)

            def qk_odd(l):
                for n, (what, b, a, cnt) in enumerate(qk_groups(l)):
                    if n % 2 == 1:
                        act.wait_ge(*at("qk_turned", l, n + 1))
                        src = PS[:, QK_BANK[n % 4], 0:P * cnt].rearrange("p (c n) -> p c n", c=cnt)
                        act.copy((kT if what == "k" else qT)[:, a:a + cnt, P * b:P * (b + 1)], src).then_inc(S("qkT_act"), 1)

            def exps(l, i):
                t, pr = steps[i]
                nk = P * len(blocks_of(t))
                act.wait_ge(*at("nm_ready", l, i + 1))
                if i >= 2:
                    act.wait_ge(*at("p_turned", l, i - 1))
                if i >= 4 and l == 0:
                    act.wait_ge(S("rsm_ready"), i - 3)
                for m in range(2):
                    ins = act.activation(pr_[:, i % 2, m, 0:nk], PS[:, 2 * (i % 2) + m, 0:nk], ACT.Exp,
                                         bias=nm[:, i % 2, m:m + 1], accum_out=sm[:, i % 4, m:m + 1])
                ins.then_inc(S("p_ready"), 1)

            def take_pT(l, i):
                t, pr = steps[i]
                nk = P * len(blocks_of(t))
                m = 1 if l == 0 else 0
                act.wait_ge(*at("p_turned", l, i + 1))
                if i >= 2:
                    act.wait_ge(*at("o_done", l, i - 1))
                act.copy(ptt[:, i % 2, m, 0:nk], PS[:, pT_bank(l, i, m), 0:nk]).then_inc(S("pT_act"), 1)

            def square_o(i):
                t, pr = steps[i]
                act.wait_ge(*at("o_copied", 1, i + 1))
                if i >= 2:
                    act.wait_ge(S("o_squared"), i - 1)
                act.activation(sqo[:, i % 2, :], q[:, t, P * pr:P * (pr + 1)], ACT.Square,
                               accum_out=ss[:, 8 * t + pr:8 * t + pr + 1]).then_inc(S("o_squared"), 1)

            def attention(l):
                n = len(steps)
                squared = 0
                for i in range(n + 3):
                    if 2 <= i < n + 2:
                        take_pT(l, i - 2)
                    if i < n:
                        exps(l, i)
                    if l == 0 and i in MOD_WITHIN:
                        take_mod(*MOD_WITHIN[i])
                    if l == 1 and i in SUB_AT:
                        while squared < 8 * (SUB_AT.index(i) + 1):
                            square_o(squared)
                            squared += 1
                        root(8, 8 * SUB_AT.index(i))
                    elif l == 1 and i >= 4 and squared < i - 3:
                        square_o(squared)
                        squared += 1

            def oT_odd(l):
                act.wait_ge(*at("state_out", l, 32))
                for g in range(1, 6, 2):
                    act.wait_ge(*at("o_turned", l, g + 1))
                    act.copy(oT[:, 4:8, P * (g // 2):P * (g // 2 + 1)],
                             PS[:, g, :].rearrange("p (c n) -> p c n", c=4)).then_inc(S("oT_act"), 1)

            def route(l):
                for t in range(NT):
                    act.wait_ge(*at("x_attn", l, NT + t + 1))
                    act.activation(junk[t], x[:, t, :], ACT.Square, accum_out=ss[:, t:t + 1]).then_inc(S("sq_ffn"), 1)
                    root(1, t)
                    if t == 2 and l == 0:
                        for slot in MOD_BY_LOGITS:
                            take_mod(*slot)
                    act.wait_ge(*at("hr_turned", l, 2 * t + 2))
                    if t == 2:
                        act.wait_ge(*at("logits", l, 1))
                    act.copy(hTr[:, t % 2, 1, :], PS[:, 3 if t % 2 == 0 else 7, :]).then_inc(S("hr_act"), 1)
                act.wait_ge(*at("lg_ready", l, 1))
                act.activation(R(48, 48), R(48, 48), ACT.Sigmoid).then_inc(S("sig_ready"), 1)

            def experts(l):
                act.wait_ge(*at("nx_ready", l, 1))
                more = act.alloc_register(f"act_more{l}")
                act.reg_mov(more, 0)
                act.wait_ge(S("y_cleared"), 16)
                act.copy(ss[0:1, 20:21], cf[0:1, 0:1]).then_inc(S("y_main"), 1)
                act.copy(ss[0:1, 21:22], cf[0:1, 0:1]).then_inc(tile_sem("y_more", l), 1)
                act.copy(ss[0:1, 22:23], cf[0:1, 0:1]).then_inc(tile_sem("y_stored_more", l), 16)

                def tag(b):
                    return "more" if b else "main"

                def silu(b, nth):
                    act.wait_ge(*at(f"gu_{tag(b)}", l, nth))
                    act.activation(sg[:, b, :], PS[:, 4 * b + 1, 0:256], ACT.Silu).then_inc(tile_sem(f"silu_{tag(b)}", l), 1)

                y_rows = y_d.rearrange("(c s) (g n) -> c g s n", s=CAP, g=2)

                def take_y(b, buf, nth, c, sem):
                    act.wait_ge(*at(f"down_{tag(b)}", l, nth))
                    act.activation(ys[:, buf, :], PS[:, 4 * b + 3, :], ACT.Copy).then_inc(tile_sem(f"y_{tag(b)}", l), 1)
                    act.wait_ge(*at(f"y_{tag(b)}", l, nth + 1))
                    act.dma_start(y_rows[bass.ds(c, 1)].rearrange("a g s n -> (a g) s n"), ys[:, buf, :]).then_inc(sem, 16)

                def further(e):
                    nx = act.value_load(nxi[0:1, bass.ds(e, 1)], min_val=0, max_val=5)
                    with act.If(nx > 0):
                        with act.Fori(0, nx):
                            reg = act.snap(more)
                            silu(1, reg + 1)
                            act.wait_ge(tile_sem("y_stored_more", l), reg * 16 + 16)
                            take_y(1, 2, reg + 1, reg + E, tile_sem("y_stored_more", l))
                            act.reg_add(more, more, 1)
                        act.nop()
                    with act.Else():
                        act.nop()

                def expert(e, par, before=None):
                    further(e)
                    silu(0, e + 1)
                    if before is not None:
                        act.wait_ge(*at(f"y_stored{1 - par}", l, 16 * before))
                    take_y(0, 1 - par, e, e - 1, S(f"y_stored{1 - par}"))

                further(0)
                silu(0, 1)
                expert(1, 1)
                expert(2, 0)
                expert(3, 1, 1)
                with act.Fori(2, E // 2) as i:
                    expert(2 * i, 0, i - 1)
                    expert(2 * i + 1, 1, i)
                act.wait_ge(*at("y_stored1", l, 16 * (E // 2 - 1)))
                take_y(0, 1, E, E - 1, S("y_stored1"))
                for par in range(2):
                    act.wait_ge(*at(f"y_stored{par}", l, 8 * E))
                act.wait_ge(tile_sem("y_stored_more", l), act.snap(more) * 16 + 16)
                act.copy(ss[0:1, 23:24], cf[0:1, 0:1]).then_inc(S("y_stored"), 1)

            act.wait_ge(S("ld_c"), 32)
            act.wait_ge(S("cs_zero"), 1)
            act.activation(cs[:, :, 0:2], cvec[:].rearrange("p v k -> p k v"), ACT.Silu).then_inc(S("cs_ready"), 1)
            act.wait_ge(S("ld_x"), 32)
            for t in range(NT):
                square("attn", junk[t], t)
            for j in range(4):
                take_mod(0, j)
            hT_odd(0)
            act.wait_ge(S("lam_dots"), 1)
            act.activation(small[:, 2:4], small[:, 0:2], ACT.Exp).then_inc(S("lam_exp"), 1)
            for l in range(2):
                if l == 0:
                    take_qkv(0, (0, 1))
                    square_heads("q_squared", q, 16, 0, 6)
                    root(48)
                    take_qkv(0, (2,))
                    square_heads("k_squared", k_, 4, 3072, 9)
                    root(12)
                    for slot in MOD_BEFORE:
                        take_mod(*slot)
                else:
                    take_qkv(1, range(6))
                qk_odd(l)
                attention(l)
                oT_odd(l)
                if l == 0:
                    for slot in MOD_BY_WO:
                        take_mod(*slot)
                route(l)
                if l == 0:
                    for slot in MOD_BY_RANKS:
                        take_mod(*slot)
                experts(l)
                for t in range(NT):
                    scale_y(l, t)
                for t in range(NT):
                    act.wait_ge(*at("x_moe", l, t + 1))
                    square("attn" if l == 0 else "final", k_[:, t, :] if l == 0 else yk[:, 3 + t, :], t)
                if l == 0:
                    act.wait_ge(*at("x_moe", 0, NT))
                    hT_odd(1)


_INS = ['x_prompt', 'x_sample', 'cache_k_a', 'cache_v_a', 'cache_k_b', 'cache_v_b', 'c', 'c_ctx', 'w_mod', 'b_mod',
        'g_attn', 'g_ffn', 'w_qkv_a', 'w_o_a', 'g_q_a', 'g_k_a', 'w_qkv_b', 'w_o_b', 'lam_q1', 'lam_k1', 'lam_q2',
        'lam_k2', 'g_sub_b', 'w_router', 'b_router', 'w_gate', 'w_up', 'w_down', 'g_final']
_OUTS = [("y_prompt", (128, 1024)), ("y_sample", (256, 1024)), ("state_k0", (128, 256)), ("state_v0", (128, 256)),
         ("state_k1", (128, 1024)), ("state_v1", (128, 1024))]


def kernel(**inputs):
    import concourse.bacc as _bacc
    from concourse.bass_utils import run_bass_kernel_spmd as _run

    nc = _bacc.Bacc("TRN2", target_bir_lowering=False, num_devices=1)
    arrays, tensors = {}, {}
    for name, a in [(n, np.ascontiguousarray(inputs[n])) for n in _INS] + [("consts", shape_constants())]:
        arrays[f"in_{name}_dram"] = a
        tensors[name] = nc.dram_tensor(f"in_{name}_dram", a.shape, mybir.dt.from_np(a.dtype), kind="ExternalInput").ap()
    for name, shape in _OUTS:
        tensors[name] = nc.dram_tensor(f"out_{name}_dram", shape, F32, kind="ExternalOutput").ap()
    hybrid_step_kernel(nc, tensors)
    r = _run(nc, [arrays], core_ids=[0])
    y_p, y_s, k_a, v_a, k_b, v_b = (r.results[0][f"out_{n}_dram"] for n, _ in _OUTS)
    return (y_p.reshape(1, 128, 1024), y_s.reshape(1, 256, 1024), k_a.reshape(1, 1, 128, 4, 64),
            v_a.reshape(1, 1, 128, 4, 64), k_b.reshape(1, 1, 128, 8, 2, 64), v_b.reshape(1, 1, 128, 8, 128))
```
